# Optimizing a Trainium2 kernel written in Bass

```python
import jax, jax.numpy as jnp
from jax import lax
import numpy as np

D_MODEL = 1024
BATCH = 1
SEQ = 256
DEPTH = 2
DEC_BATCH = 8
DEC_SEQ = 1
PAST_LEN = 2048
PAGE_SIZE = 128

N_MIXERS = 2
N_RET_LAYERS = (DEPTH + 1) // 2
N_GLA_LAYERS = DEPTH // 2

RET_HEADS = 4
RET_DK = D_MODEL // RET_HEADS
RET_DV = 2 * RET_DK
RET_CHUNK = 64
ROPE_BASE = 10000.0

GLA_HEADS = 4
GLA_DK = D_MODEL // (2 * GLA_HEADS)
GLA_DV = D_MODEL // GLA_HEADS
GLA_RANK = 16
GLA_TAU = 16.0
GLA_CHUNK = 16

N_EXPERTS = 64
TOP_K = 8
N_GROUPS = 8
TOPK_GROUPS = 4
D_EXPERT = D_MODEL // 4
D_SHARED = D_EXPERT
ROUTED_SCALE = 2.5
MOE_BLOCK = 128

EPS = 1e-6

kernel_name = "hybrid_retnet_gla_moe_adaln_step"

def rmsnorm(x, g):
    xf = x.astype(jnp.float32)
    y = xf * lax.rsqrt(jnp.mean(xf * xf, axis=-1, keepdims=True) + EPS)
    return (y * g.astype(jnp.float32)).astype(x.dtype)

def modulate(x, g, shift, scale):
    return rmsnorm(x, g) * (1 + scale[:, None, :]) + shift[:, None, :]

def rotary(x, pos):
    half = x.shape[-1] // 2
    inv = ROPE_BASE ** (-jnp.arange(half, dtype=jnp.float32) / half)
    ang = pos.astype(jnp.float32)[:, None] * inv[None, :]
    cos = jnp.cos(ang)[None, :, None, :]
    sin = jnp.sin(ang)[None, :, None, :]
    xf = x.astype(jnp.float32)
    x1, x2 = xf[..., :half], xf[..., half:]
    return jnp.concatenate([x1 * cos - x2 * sin, x1 * sin + x2 * cos], axis=-1)

def pad_time(x, tp):
    return jnp.pad(x, [(0, 0), (0, tp - x.shape[1])] + [(0, 0)] * (x.ndim - 2))

def to_chunks(x, L):
    B, Tp, H, d = x.shape
    return x.reshape(B, Tp // L, L, H, d).transpose(1, 0, 3, 2, 4)

def from_chunks(o, T):
    nC, B, H, L, d = o.shape
    return o.transpose(1, 0, 3, 2, 4).reshape(B, nC * L, H, d)[:, :T]

def retention_chunked(q, k, v, log_gamma, S0):
    T = q.shape[1]
    L = min(RET_CHUNK, T)
    tp = -(-T // L) * L
    valid = jnp.arange(tp) < T
    log_a = jnp.where(valid[:, None], log_gamma[None, :], 0.0)
    cum = jnp.cumsum(log_a.reshape(tp // L, L, -1).transpose(0, 2, 1), axis=-1)
    qc, kc, vc = (to_chunks(pad_time(a, tp), L) for a in (q, k, v))
    causal = jnp.tril(jnp.ones((L, L), dtype=bool))

    def step(S, inp):
        qb, kb, vb, cb = inp
        dec = jnp.exp(jnp.where(causal, cb[:, :, None] - cb[:, None, :], -jnp.inf))
        att = jnp.einsum('bhid,bhjd->bhij', qb, kb) * dec[None]
        o = (jnp.einsum('bhij,bhjv->bhiv', att, vb)
             + jnp.einsum('bhid,bhdv->bhiv', qb * jnp.exp(cb)[..., None], S))
        tot = cb[:, -1]
        kd = kb * jnp.exp(tot[:, None] - cb)[..., None]
        S = jnp.exp(tot)[:, None, None] * S + jnp.einsum('bhjd,bhjv->bhdv', kd, vb)
        return S, o

    S, oc = lax.scan(step, S0.astype(jnp.float32), (qc, kc, vc, cum))
    return from_chunks(oc, T), S

def gla_chunked(q, k, v, log_a, S0):
    T = q.shape[1]
    L = min(GLA_CHUNK, T)
    tp = -(-T // L) * L
    qc, kc, vc, ac = (to_chunks(pad_time(a, tp), L) for a in (q, k, v, log_a))
    cum = jnp.cumsum(ac, axis=3)
    causal = jnp.tril(jnp.ones((L, L), dtype=bool))

    def step(S, inp):
        qb, kb, vb, cb = inp
        qe = qb * jnp.exp(cb)
        ke = kb * jnp.exp(-cb)
        att = jnp.where(causal, jnp.einsum('bhid,bhjd->bhij', qe, ke), 0.0)
        o = jnp.einsum('bhij,bhjv->bhiv', att, vb) + jnp.einsum('bhid,bhdv->bhiv', qe, S)
        tot = cb[:, :, -1:, :]
        kd = kb * jnp.exp(tot - cb)
        S = jnp.exp(tot)[:, :, 0, :, None] * S + jnp.einsum('bhjd,bhjv->bhdv', kd, vb)
        return S, o

    S, oc = lax.scan(step, S0.astype(jnp.float32), (qc, kc, vc, cum))
    return from_chunks(oc, T), S

def retention_mixer(h, pos, S0, w_in, norm_g, w_out):
    B, T, _ = h.shape
    nqk, nv = RET_HEADS * RET_DK, RET_HEADS * RET_DV
    proj = h @ w_in
    q, k, v, g = jnp.split(proj, [nqk, 2 * nqk, 2 * nqk + nv], axis=-1)
    q = rotary(q.reshape(B, T, RET_HEADS, RET_DK), pos)
    k = rotary(k.reshape(B, T, RET_HEADS, RET_DK), pos) * (RET_DK ** -0.5)
    v = v.reshape(B, T, RET_HEADS, RET_DV).astype(jnp.float32)
    log_gamma = jnp.log1p(-jnp.power(2.0, -5.0 - jnp.arange(RET_HEADS, dtype=jnp.float32)))
    o, S = retention_chunked(q, k, v, log_gamma, S0)
    mu = jnp.mean(o, axis=-1, keepdims=True)
    var = jnp.mean(jnp.square(o - mu), axis=-1, keepdims=True)
    o = (o - mu) * lax.rsqrt(var + EPS) * norm_g.reshape(RET_HEADS, RET_DV).astype(jnp.float32)
    o = o.reshape(B, T, nv).astype(h.dtype) * jax.nn.silu(g)
    return o @ w_out, S.astype(S0.dtype)

def gla_mixer(h, S0, w_in, w_a1, w_a2, b_a, norm_g, w_out):
    B, T, _ = h.shape
    nqk, nv = GLA_HEADS * GLA_DK, GLA_HEADS * GLA_DV
    proj = h @ w_in
    q, k, v, r = jnp.split(proj, [nqk, 2 * nqk, 2 * nqk + nv], axis=-1)
    q = q.reshape(B, T, GLA_HEADS, GLA_DK).astype(jnp.float32) * (GLA_DK ** -0.5)
    k = k.reshape(B, T, GLA_HEADS, GLA_DK).astype(jnp.float32)
    v = v.reshape(B, T, GLA_HEADS, GLA_DV).astype(jnp.float32)
    z = ((h @ w_a1) @ w_a2 + b_a).astype(jnp.float32)
    log_a = (jax.nn.log_sigmoid(z) / GLA_TAU).reshape(B, T, GLA_HEADS, GLA_DK)
    o, S = gla_chunked(q, k, v, log_a, S0)
    o = o * lax.rsqrt(jnp.mean(o * o, axis=-1, keepdims=True) + EPS)
    o = o * norm_g.reshape(GLA_HEADS, GLA_DV).astype(jnp.float32)
    o = o.reshape(B, T, nv).astype(h.dtype) * jax.nn.silu(r)
    return o @ w_out, S.astype(S0.dtype)

def swiglu(x, wg, wu, wd):
    return (jax.nn.silu(x @ wg) * (x @ wu)) @ wd

def moe_ffn(h, w_router, router_bias, w_gate, w_up, w_down, ws_gate, ws_up, ws_down):
    Bsz, T, D = h.shape
    x = h.reshape(-1, D)
    N = x.shape[0]
    scores = jax.nn.sigmoid((x @ w_router).astype(jnp.float32))
    biased = scores + router_bias.astype(jnp.float32)
    grp_score = lax.top_k(biased.reshape(N, N_GROUPS, -1), 2)[0].sum(-1)
    _, top_g = lax.top_k(grp_score, TOPK_GROUPS)
    gmask = jnp.any(top_g[..., None] == jnp.arange(N_GROUPS)[None, None, :], axis=1)
    emask = jnp.repeat(gmask, N_EXPERTS // N_GROUPS, axis=1)
    _, idx = lax.top_k(jnp.where(emask, biased, -jnp.inf), TOP_K)
    wsel = jnp.take_along_axis(scores, idx, axis=1)
    wsel = wsel / jnp.sum(wsel, axis=-1, keepdims=True) * ROUTED_SCALE
    NK = N * TOP_K
    e_flat = idx.reshape(-1)
    tok_flat = jnp.repeat(jnp.arange(N), TOP_K)
    w_flat = wsel.reshape(-1)
    order = jnp.argsort(e_flat)
    e_s, tok_s, w_s = e_flat[order], tok_flat[order], w_flat[order]
    counts = jnp.bincount(e_flat, length=N_EXPERTS)
    padded = (counts + MOE_BLOCK - 1) // MOE_BLOCK * MOE_BLOCK
    start = jnp.cumsum(counts) - counts
    pend = jnp.cumsum(padded)
    pstart = pend - padded
    dest = pstart[e_s] + jnp.arange(NK) - start[e_s]
    cap = -(-(NK + N_EXPERTS * (MOE_BLOCK - 1)) // MOE_BLOCK) * MOE_BLOCK
    nb = cap // MOE_BLOCK
    xbuf = jnp.zeros((cap, D), x.dtype).at[dest].set(x[tok_s])
    block_expert = jnp.minimum(
        jnp.searchsorted(pend, jnp.arange(nb) * MOE_BLOCK, side='right'), N_EXPERTS - 1)

    def expert_block(args):
        xb, e = args
        return swiglu(xb, w_gate[e], w_up[e], w_down[e])

    ybuf = lax.map(expert_block, (xbuf.reshape(nb, MOE_BLOCK, D), block_expert)).reshape(cap, D)
    routed = jnp.zeros_like(x).at[tok_s].add(ybuf[dest] * w_s[:, None].astype(x.dtype))
    shared = swiglu(x, ws_gate, ws_up, ws_down)
    return (routed + shared).reshape(Bsz, T, D)

def trunk(x, c, pos0, s_ret, s_gla,
          ret_w_in, ret_norm_g, ret_w_out,
          gla_w_in, gla_w_a1, gla_w_a2, gla_b_a, gla_norm_g, gla_w_out,
          ada_w, ada_b, norm_mix_g, norm_ffn_g,
          moe_w_router, moe_router_bias, moe_w_gate, moe_w_up, moe_w_down,
          sh_w_gate, sh_w_up, sh_w_down, final_norm_g):
    T = x.shape[1]
    pos = pos0 + jnp.arange(T, dtype=jnp.int32)
    new_ret, new_gla = [], []
    for i in range(DEPTH):
        mod = jax.nn.silu(c) @ ada_w[i] + ada_b[i]
        sh1, sc1, g1, sh2, sc2, g2 = jnp.split(mod, 6, axis=-1)
        h = modulate(x, norm_mix_g[i], sh1, sc1)
        j = i // N_MIXERS
        if i % N_MIXERS == 0:
            m, S = retention_mixer(h, pos, s_ret[j], ret_w_in[j], ret_norm_g[j], ret_w_out[j])
            new_ret.append(S)
        else:
            m, S = gla_mixer(h, s_gla[j], gla_w_in[j], gla_w_a1[j], gla_w_a2[j],
                             gla_b_a[j], gla_norm_g[j], gla_w_out[j])
            new_gla.append(S)
        x = x + g1[:, None, :] * m
        h = modulate(x, norm_ffn_g[i], sh2, sc2)
        f = moe_ffn(h, moe_w_router[i], moe_router_bias[i], moe_w_gate[i], moe_w_up[i],
                    moe_w_down[i], sh_w_gate[i], sh_w_up[i], sh_w_down[i])
        x = x + g2[:, None, :] * f
    return rmsnorm(x, final_norm_g), jnp.stack(new_ret), jnp.stack(new_gla)

def setup_inputs(seed: int = 0) -> dict:
    key = jax.random.key(seed)
    ks = iter(jax.random.split(key, 40))

    def nrm(shape, scale):
        return jax.random.normal(next(ks), shape, jnp.float32) * scale

    def gain(shape):
        return 1.0 + nrm(shape, 0.02)

    D = D_MODEL
    ret_w = 2 * RET_HEADS * RET_DK + 2 * RET_HEADS * RET_DV
    gla_w = 2 * GLA_HEADS * GLA_DK + 2 * GLA_HEADS * GLA_DV
    return {
        "x_prompt": nrm((BATCH, SEQ, D), 1.0),
        "x_sample": nrm((DEC_BATCH, DEC_SEQ, D), 1.0),
        "state_ret": nrm((N_RET_LAYERS, DEC_BATCH, RET_HEADS, RET_DK, RET_DV), 0.1),
        "state_gla": nrm((N_GLA_LAYERS, DEC_BATCH, GLA_HEADS, GLA_DK, GLA_DV), 0.1),
        "c_prompt": nrm((BATCH, D), 1.0),
        "c_sample": nrm((DEC_BATCH, D), 1.0),
        "ret_w_in": nrm((N_RET_LAYERS, D, ret_w), D ** -0.5),
        "ret_norm_g": gain((N_RET_LAYERS, RET_HEADS * RET_DV)),
        "ret_w_out": nrm((N_RET_LAYERS, RET_HEADS * RET_DV, D), (RET_HEADS * RET_DV) ** -0.5),
        "gla_w_in": nrm((N_GLA_LAYERS, D, gla_w), D ** -0.5),
        "gla_w_a1": nrm((N_GLA_LAYERS, D, GLA_RANK), D ** -0.5),
        "gla_w_a2": nrm((N_GLA_LAYERS, GLA_RANK, GLA_HEADS * GLA_DK), GLA_RANK ** -0.5),
        "gla_b_a": nrm((N_GLA_LAYERS, GLA_HEADS * GLA_DK), 0.1),
        "gla_norm_g": gain((N_GLA_LAYERS, GLA_HEADS * GLA_DV)),
        "gla_w_out": nrm((N_GLA_LAYERS, GLA_HEADS * GLA_DV, D), (GLA_HEADS * GLA_DV) ** -0.5),
        "ada_w": nrm((DEPTH, D, 6 * D), 0.5 * D ** -0.5),
        "ada_b": nrm((DEPTH, 6 * D), 0.02),
        "norm_mix_g": gain((DEPTH, D)),
        "norm_ffn_g": gain((DEPTH, D)),
        "moe_w_router": nrm((DEPTH, D, N_EXPERTS), D ** -0.5),
        "moe_router_bias": nrm((DEPTH, N_EXPERTS), 0.01),
        "moe_w_gate": nrm((DEPTH, N_EXPERTS, D, D_EXPERT), D ** -0.5),
        "moe_w_up": nrm((DEPTH, N_EXPERTS, D, D_EXPERT), D ** -0.5),
        "moe_w_down": nrm((DEPTH, N_EXPERTS, D_EXPERT, D), D_EXPERT ** -0.5),
        "sh_w_gate": nrm((DEPTH, D, D_SHARED), D ** -0.5),
        "sh_w_up": nrm((DEPTH, D, D_SHARED), D ** -0.5),
        "sh_w_down": nrm((DEPTH, D_SHARED, D), D_SHARED ** -0.5),
        "final_norm_g": gain((D,)),
    }

def reference(x_prompt, x_sample, state_ret, state_gla, c_prompt, c_sample,
              ret_w_in, ret_norm_g, ret_w_out,
              gla_w_in, gla_w_a1, gla_w_a2, gla_b_a, gla_norm_g, gla_w_out,
              ada_w, ada_b, norm_mix_g, norm_ffn_g,
              moe_w_router, moe_router_bias, moe_w_gate, moe_w_up, moe_w_down,
              sh_w_gate, sh_w_up, sh_w_down, final_norm_g):
    weights = (ret_w_in, ret_norm_g, ret_w_out,
               gla_w_in, gla_w_a1, gla_w_a2, gla_b_a, gla_norm_g, gla_w_out,
               ada_w, ada_b, norm_mix_g, norm_ffn_g,
               moe_w_router, moe_router_bias, moe_w_gate, moe_w_up, moe_w_down,
               sh_w_gate, sh_w_up, sh_w_down, final_norm_g)
    b = x_prompt.shape[0]
    s_ret0 = jnp.zeros((N_RET_LAYERS, b, RET_HEADS, RET_DK, RET_DV), state_ret.dtype)
    s_gla0 = jnp.zeros((N_GLA_LAYERS, b, GLA_HEADS, GLA_DK, GLA_DV), state_gla.dtype)
    y_prompt, ret_prompt, gla_prompt = trunk(x_prompt, c_prompt, 0, s_ret0, s_gla0, *weights)
    y_sample, ret_sample, gla_sample = trunk(x_sample, c_sample, PAST_LEN, state_ret, state_gla,
                                             *weights)
    return (y_prompt, y_sample, ret_prompt, gla_prompt, ret_sample, gla_sample)


_drawn_inputs = setup_inputs


def setup_inputs(seed=0):
    import zlib

    import numpy as np

    out = dict(_drawn_inputs(seed))
    spreads = {}
    factors = {'ret_norm_g': 2.702, 'gla_norm_g': 5.946, 'final_norm_g': 3.088}
    for name, (base, spread) in spreads.items():
        noise = np.random.default_rng([zlib.crc32(name.encode()), seed]).standard_normal(out[name].shape)
        drawn = base * np.exp(spread * noise) if base else spread * noise
        out[name] = __import__('jax').numpy.asarray(drawn.astype(out[name].dtype))
    for name, factor in factors.items():
        out[name] = (out[name] * factor).astype(out[name].dtype)
    return out
```

```python
import concourse.bass as bass
import numpy as np
from concourse import mybir
from contextlib import ExitStack

F32 = mybir.dt.float32
BF16 = mybir.dt.bfloat16
I32 = mybir.dt.int32
ALU = mybir.AluOpType
ACT = mybir.ActivationFunctionType
AX = mybir.AxisListType

P = 128
D = 1024
DC = D // P
TP = 256
NS = 8
T = TP + NS
NCOND = 1 + NS
DEPTH = 2
PAST = 2048
EPS = 1e-6

RH, RDK, RDV = 4, 256, 512
GH, GDK, GDV = 4, 128, 256
RANK = 16
TAU = 16.0

NE, TOPK, NG, TOPG = 64, 8, 8, 4
DE = D // 4
FC = DE // P
SCALE = 2.5
CAP = 64
XB = (T * TOPK) // (CAP + 1)
XBP = XB + 2
TT = 3
TOKENS = [(0, P), (P, P), (TP, NS)]

RING = 12
SLOT = 2048
EPI = 4
ROUNDS = NE // EPI

TAB = {}
_at = 0
for _name, _w in (("cos", T), ("sin", T), ("decay", RH * TP), ("kdec", 2 * RH), ("causal", P), ("ident", P),
                  ("before", P), ("ones", P), ("gtri", NG * NG), ("iota", NE), ("valid", TT), ("zero", 1),
                  ("one", 1)):
    TAB[_name] = (_at, _at + _w)
    _at += _w
TABW = _at


def tables():
    t = np.zeros((P, TABW), np.float32)

    def put(name, a):
        a0, a1 = TAB[name]
        t[:, a0:a1] = np.asarray(a, np.float32).reshape(P, a1 - a0)

    half = RDK // 2
    inv = (np.float32(10000.0) ** (-np.arange(half, dtype=np.float32) / np.float32(half))).astype(np.float32)
    pos = np.concatenate([np.arange(TP), np.full(NS, PAST)]).astype(np.float32)
    ang = inv[:, None] * pos[None, :]
    put("cos", np.cos(ang.astype(np.float64)))
    put("sin", np.sin(ang.astype(np.float64)))
    lg = np.log1p(-np.power(2.0, -5.0 - np.arange(RH)))
    i, j = np.arange(TP)[None, :], np.arange(P)[:, None]
    put("decay", np.stack([np.where(i >= j, np.exp(lg[h] * (i - j)), 0.0) for h in range(RH)], 1))
    jj = np.arange(TP).reshape(2, P).T
    put("kdec", np.stack([np.exp(lg[h] * (TP - 1 - jj)) for h in range(RH)], 2))
    q, r = np.arange(P)[:, None], np.arange(P)[None, :]
    put("causal", q <= r)
    put("ident", q == r)
    put("before", q < r)
    put("ones", np.ones((P, P)))
    g = np.arange(NG)
    put("gtri", np.tile((g[None, :] < g[:, None]).reshape(1, -1), (P, 1)))
    put("iota", np.tile(np.arange(NE)[None], (P, 1)))
    put("valid", np.stack([np.arange(P) < n for _, n in TOKENS], 1))
    put("one", np.ones((P, 1)))
    return t


GAMMA = [float(1.0 - 2.0 ** (-5.0 - h)) for h in range(RH)]


class Chain:

    def __init__(self, sem):
        self.sem, self.n = sem, 0

    def link(self, eng, ins):
        self.n += 1
        ins.then_inc(self.sem, 1)
        eng.wait_ge(self.sem, self.n)


class Core:
    pass


def build(nc, inp, out, dbg=None):
    ctx = ExitStack()
    with ctx:
        k = Core()
        k.nc, k.inp, k.out = nc, inp, out

        def sb(name, cols, dt=F32, parts=P):
            return ctx.enter_context(nc.sbuf_tensor(name, [parts, cols], dt))

        k.persistent = [nc.alloc_semaphore(name=n) for n in
                        [f"ring_full{s}" for s in range(RING)] + [f"ring_free{s}" for s in range(RING)]
                        + ["vector_step"]]
        k.stored = {n: nc.alloc_semaphore(name=n) for n in
                    ["ret_state_stored"] + [f"ret_sample_state_stored{b}" for b in range(4)]
                    + ["gla_state_stored"] + [f"gla_sample_state_stored{b}" for b in range(2)]}
        k.row_fetched = [nc.alloc_semaphore(name=f"row_fetched{b}") for b in range(3)]
        k.mine = []
        k.sem = lambda name: k.mine.append(nc.alloc_semaphore(name=name)) or k.mine[-1]
        k.ring = sb("ring", RING * SLOT)
        k.tab = sb("tab", TABW)
        k.x = sb("xT", DC * T)[:, :].rearrange("p (c t) -> p c t", c=DC)
        k.h = sb("hT", DC * T)[:, :].rearrange("p (c t) -> p c t", c=DC)
        k.mod = sb("mod", DEPTH * 48 * NCOND)[:, :].rearrange("p (l g c s) -> p l g c s", l=DEPTH, g=6, c=DC)
        k.gain = sb("gain", DEPTH * 2 * DC * NCOND)[:, :].rearrange("p (l n c s) -> p l n c s", l=DEPTH, n=2, c=DC)
        k.vec = sb("vec", 164)
        k.rstd = sb("rstd", RH * T)
        k.size = 19800
        k.scratch = sb("scratch", k.size)
        k.ps = ctx.enter_context(nc.psum_tensor("ps", [P, 8, 512], F32))
        k.y = nc.dram_tensor("expert_rows", (NE * CAP + XBP * CAP, D), F32, kind="Internal").ap()

        k.const = lambda name: k.tab[:, TAB[name][0]:TAB[name][1]]
        k.ident = k.const("ident")
        k.ones = k.const("ones")
        k.ada_b = k.vec[:, 0:96].rearrange("p (l g c) -> p l g c", l=DEPTH, g=6)
        k.norm_g = k.vec[:, 96:128].rearrange("p (n l c) -> p l n c", n=2, l=DEPTH)
        k.ret_g = k.vec[:, 128:144]
        k.gla_g = k.vec[:, 144:152]
        k.fin_g = k.vec[:, 152:160]
        k.b_a = k.vec[:, 160:164]

        k.ring_full, k.ring_free = k.persistent[0:RING], k.persistent[RING:2 * RING]
        k.plan, k.issued = plan_loads(inp), 0
        k.stage = {}
        for n, (what, _) in enumerate(k.plan):
            k.stage.setdefault(what, n)
        k.dve = Chain(k.persistent[2 * RING])

        setup(k)
        if dbg != "setup":
            conditioning(k)
        if dbg not in ("setup", "ada"):
            norm(k, 0, 0, "retention_in")
            retention(k)
            if dbg != "ret":
                norm(k, 0, 1, "moe0")
                experts(k, 0)
                reuse_semaphores(k)
                if dbg != "moe0":
                    norm(k, 1, 0, "gla_in")
                    gla(k)
                    if dbg != "gla":
                        norm(k, 1, 1, "moe1")
                        experts(k, 1)
                        final(k)
        if dbg:
            dump(k)


def reuse_semaphores(k):
    nc = k.nc
    with nc.Block() as block:
        @block.gpsimd
        def _(pool):
            for s in k.mine:
                pool.sem_clear(s)
    for s in k.mine:
        nc.release_semaphore(s)
    k.mine.clear()


def dump(k):
    nc, s = k.nc, k.sem("dumped")
    with nc.Block() as block:
        @block.sync
        def _(sp):
            sp.dma_start(k.out["dbg_x"], k.x.rearrange("p c t -> p (c t)")).then_inc(s, 16)
            sp.dma_start(k.out["dbg_h"], k.h.rearrange("p c t -> p (c t)")).then_inc(s, 16)
            sp.dma_start(k.out["dbg_mod"], k.mod.rearrange("p l g c s -> p (l g c s)")).then_inc(s, 16)
            sp.wait_ge(s, 48)



def plan_loads(inp):
    plan = []

    def columns(what, w, width):
        kc, n = w.shape[0] // P, w.shape[1] // width
        for j in range(n):
            plan.append((what, w[:, j * width:(j + 1) * width].rearrange("(k p) n -> p k n", k=kc)))

    def moe(layer):
        what = f"shared{layer}"
        for name in ("sh_w_gate", "sh_w_up", "sh_w_down"):
            w = inp[name][layer]
            plan.append((what, w.rearrange("(k p) n -> p k n", p=P)))
        for r in range(ROUNDS):
            for name, e in ROUND:
                plan.append((f"moe{layer}", inp[name][layer][r * EPI + e].rearrange("(k p) n -> p k n", p=P)))

    for layer in range(DEPTH):
        columns("ada", inp["ada_w"][layer], 256)
    columns("ret_in", inp["ret_w_in"][0], 256)
    columns("ret_out", inp["ret_w_out"][0], 128)
    moe(0)
    columns("gla_in", inp["gla_w_in"][0], 256)
    columns("gla_out", inp["gla_w_out"][0], 256)
    moe(1)
    return plan


ROUND = [(n, e) for e in range(EPI) for n in ("moe_w_gate", "moe_w_up")] + [("moe_w_down", e) for e in range(EPI)]
PLACE = {ne: i for i, ne in enumerate(ROUND)}


def slot(k, n, inner):
    s = n % RING
    return k.ring[:, s * SLOT:(s + 1) * SLOT].rearrange("p (k n) -> p k n", n=inner)


def load_until(k, sp, last):
    while k.issued < min(last, len(k.plan)):
        n = k.issued
        src = k.plan[n][1]
        if n >= RING:
            sp.wait_ge(k.ring_free[n % RING], n // RING)
        sp.dma_start(slot(k, n, src.shape[2]), src).then_inc(k.ring_full[n % RING], 16)
        k.issued += 1


def wait_slot(k, pe, n):
    pe.wait_ge(k.ring_full[n % RING], 16 * (n // RING + 1))


def wait_used(k, eng, n):
    eng.wait_ge(k.ring_free[n % RING], n // RING + 1)



def setup(k):
    nc, inp = k.nc, k.inp
    s_tab, s_in, s_cond = k.sem("tables_loaded"), k.sem("inputs_loaded"), k.sem("cond_loaded")
    s_silu, s_tr, s_cp = k.sem("cond_silu"), k.sem("inputs_transposed"), k.sem("transposed_copied")
    sc = k.scratch
    xn = sc[:, 0:TT * D].rearrange("p (t d) -> p t d", t=TT)
    vn = sc[:, 3072:3072 + 2 * P].rearrange("p (t d) -> p t d", t=2)
    cn = sc[0:NCOND, 3400:3400 + D]
    k.condT = sc[:, 5000:5000 + DC * NCOND].rearrange("p (c s) -> p c s", c=DC)
    with nc.Block() as block:
        @block.sync
        def _(sp):
            sp.dma_start(k.tab[:, :], inp["tables"]).then_inc(s_tab, 16)
            sp.dma_start(cn[0:1, :], inp["c_prompt"]).then_inc(s_cond, 16)
            sp.dma_start(cn[1:NCOND, :], inp["c_sample"]).then_inc(s_cond, 16)
            for t, (t0, n) in enumerate(TOKENS):
                src = inp["x_prompt"][0, t0:t0 + n] if t < 2 else inp["x_sample"].rearrange("b o d -> (b o) d")
                sp.dma_start(xn[0:n, t, :], src).then_inc(s_in, 16)
            at = 0
            for name, rows in (("ada_b", 96), ("norm_mix_g", 16), ("norm_ffn_g", 16), ("ret_norm_g", 16),
                               ("gla_norm_g", 8), ("final_norm_g", 8), ("gla_b_a", 4)):
                src = inp[name]
                src = (src.rearrange("(r p) -> r p", p=P) if len(src.shape) == 1
                       else src.rearrange("l (r p) -> (l r) p", p=P))
                sp.dma_start(vn[at % P:at % P + rows, at // P, :], src).then_inc(s_in, 16)
                at += rows
            load_until(k, sp, RING)

        @block.scalar
        def _(act):
            act.wait_ge(s_cond, 32)
            nc.scalar.activation(cn, cn, ACT.Silu).then_inc(s_silu, 1)

        @block.tensor
        def _(pe):
            pe.wait_ge(s_tab, 16)
            pe.wait_ge(s_silu, 1)
            for c in range(DC):
                mm = nc.tensor.transpose(k.ps[:, 0, c * NCOND:(c + 1) * NCOND], cn[:, c * P:(c + 1) * P],
                                         k.ident[0:NCOND, 0:NCOND])
            mm.then_inc(s_tr, 1)
            pe.wait_ge(s_in, 16 * 10)
            for t, rows in ((0, 128), (1, 36)):
                mm = nc.tensor.transpose(k.ps[:, 1, t * P:t * P + rows], vn[0:rows, t, :], k.ident[0:rows, 0:rows])
            mm.then_inc(s_tr, 1)
            for c in range(DC):
                if c >= 2:
                    pe.wait_ge(s_cp, c - 2 + 1 + 2)
                for t, (t0, n) in enumerate(TOKENS):
                    mm = nc.tensor.transpose(k.ps[:, 2 + c % 2, t0:t0 + n], xn[0:n, t, c * P:(c + 1) * P],
                                             k.ident[0:n, 0:n])
                mm.then_inc(s_tr, 1)

        @block.vector
        def _(v):
            v.wait_ge(s_tr, 1)
            nc.vector.tensor_copy(k.condT.rearrange("p c s -> p (c s)"), k.ps[:, 0, 0:DC * NCOND]).then_inc(s_cp, 1)
            v.wait_ge(s_tr, 2)
            nc.vector.tensor_copy(k.vec[:, :], k.ps[:, 1, 0:164]).then_inc(s_cp, 1)
            for c in range(DC):
                v.wait_ge(s_tr, 3 + c)
                nc.vector.tensor_copy(k.x[:, c, :], k.ps[:, 2 + c % 2, 0:T]).then_inc(s_cp, 1)



def conditioning(k):
    nc = k.nc
    n0, rounds = k.stage["ada"], 4
    with nc.Block() as block:
        @block.sync
        def _(sp):
            load_until(k, sp, n0 + 12 * rounds + RING)

        @block.tensor
        def _(pe):
            out = k.ps[:, 0:2, :].rearrange("p b (h n) -> p (b h) n", h=2)
            with pe.Fori(0, rounds) as r:
                for s in range(RING):
                    pe.wait_ge(k.ring_full[s], r * 16 + 16)
                    w = slot(k, s, 256)
                    for m in range(2):
                        j = (2 * s + m) * NCOND
                        for c in range(DC):
                            mm = nc.tensor.matmul(out[:, bass.ds(r, 1), j:j + NCOND], w[:, c, m * P:(m + 1) * P],
                                                  k.condT[:, c, :], start=(c == 0), stop=(c == DC - 1))
                    mm.then_inc(k.ring_free[s], 1)

        @block.vector
        def _(v):
            wait_used(k, v, n0 + RING * rounds - 1)
            for r in range(rounds):
                mod = k.mod.rearrange("p l g c s -> p (l g c) s")[:, r * 24:(r + 1) * 24, :]
                b = k.vec[:, r * 24:(r + 1) * 24].unsqueeze(2).to_broadcast([P, 24, NCOND])
                src = k.ps[:, r // 2, (r % 2) * 256:(r % 2) * 256 + 24 * NCOND].rearrange("p (c s) -> p c s", c=24)
                ins = nc.vector.tensor_tensor(mod, src, b, ALU.add)
                k.dve.link(v, ins)
            for layer in range(DEPTH):
                for n in range(2):
                    g = k.norm_g[:, layer, n, :].unsqueeze(2).to_broadcast([P, DC, NCOND])
                    ins = nc.vector.scalar_tensor_tensor(k.gain[:, layer, n], k.mod[:, layer, 3 * n + 1], 1.0, g,
                                                         ALU.add, ALU.mult)
            k.dve.link(v, ins)



def norm(k, layer, which, then):
    nc = k.nc
    tag = f"{layer}{which}"
    s_sq, s_sum, s_ms, s_rt = (k.sem(f"norm{tag}_{n}") for n in ("squared", "summed", "meansq", "root"))
    s_prod = k.sem(f"norm{tag}_scaled")
    sq = k.scratch[:, 0:DC * T].rearrange("p (c t) -> p c t", c=DC)
    tmp = k.scratch[:, DC * T:DC * T + T]
    root = k.scratch[:, DC * T + T:DC * T + 2 * T]
    rstd = k.rstd[:, 0:T]
    final_norm = layer == DEPTH

    with nc.Block() as block:
        @block.scalar
        def _(act):
            for c in range(DC):
                nc.scalar.activation(sq[:, c, :], k.x[:, c, :], ACT.Square).then_inc(s_sq, 1)
            act.wait_ge(s_ms, 1)
            nc.scalar.activation(root, tmp, ACT.Sqrt).then_inc(s_rt, 1)
            if not final_norm:
                for c in range(DC):
                    act.wait_ge(s_prod, c + 1)
                    nc.scalar.activation(k.h[:, c, 0:TP], k.h[:, c, 0:TP], ACT.Identity,
                                         bias=k.mod[:, layer, 3 * which, c, 0:1])

        @block.tensor
        def _(pe):
            for c in range(DC):
                pe.wait_ge(s_sq, c + 1)
                mm = nc.tensor.matmul(k.ps[:, 0, 0:T], k.ones, sq[:, c, :], start=(c == 0), stop=(c == DC - 1))
            mm.then_inc(s_sum, 1)

        @block.vector
        def _(v):
            v.wait_ge(s_sum, 1)
            nc.vector.tensor_scalar(tmp, k.ps[:, 0, 0:T], 1.0 / D, EPS, ALU.mult, ALU.add).then_inc(s_ms, 1)
            v.wait_ge(s_rt, 1)
            k.dve.link(v, nc.vector.reciprocal(rstd, root))
            if final_norm:
                for c in range(DC):
                    nc.vector.scalar_tensor_tensor(k.h[:, c, :], k.x[:, c, :], k.fin_g[:, c:c + 1], rstd,
                                                   ALU.mult, ALU.mult)
                return
            for c in range(DC):
                nc.vector.scalar_tensor_tensor(k.h[:, c, 0:TP], k.x[:, c, 0:TP], k.gain[:, layer, which, c, 0:1],
                                               rstd[:, 0:TP], ALU.mult, ALU.mult).then_inc(s_prod, 1)
            hs = k.h[:, :, TP:T]
            rs = rstd[:, TP:T].unsqueeze(1).to_broadcast([P, DC, NS])
            k.dve.link(v, nc.vector.tensor_tensor(hs, k.x[:, :, TP:T], rs, ALU.mult))
            k.dve.link(v, nc.vector.tensor_tensor(hs, hs, k.gain[:, layer, which, :, 1:NCOND], ALU.mult))
            nc.vector.tensor_tensor(hs, hs, k.mod[:, layer, 3 * which, :, 1:NCOND], ALU.add)


def add_gated(k, v, chunk, psum, gate, tmp):
    nc = k.nc
    nc.vector.scalar_tensor_tensor(k.x[:, chunk, 0:TP], psum[:, 0:TP], gate[:, chunk, 0:1], k.x[:, chunk, 0:TP],
                                   ALU.mult, ALU.add)
    k.dve.link(v, nc.vector.tensor_tensor(tmp, psum[:, TP:T], gate[:, chunk, 1:NCOND], ALU.mult))
    return nc.vector.tensor_tensor(k.x[:, chunk, TP:T], tmp, k.x[:, chunk, TP:T], ALU.add)



def retention(k):
    nc, inp, out = k.nc, k.inp, k.out
    sc = k.scratch
    at = [0]

    def area(cols):
        at[0] += cols
        assert at[0] <= k.size
        return sc[:, at[0] - cols:at[0]]

    q = area(DC * T).rearrange("p (c t) -> p c t", c=DC)
    kk = area(DC * T).rearrange("p (c t) -> p c t", c=DC)
    vo = area(16 * T).rearrange("p (c t) -> p c t", c=16)
    vs = area(2048)[0:NS, :]
    vn = area(2 * 1024).rearrange("p (b j n) -> p b j n", b=2, j=2)
    kn = area(2 * 512).rearrange("p (b j n) -> p b j n", b=2, j=2)
    att = area(384)
    st = area(4 * 1024).rearrange("p (b c n) -> p b c n", b=4, c=2)
    tmp = area(4 * T).rearrange("p (b t) -> p b t", b=4)
    outer = vn[:, 0]
    n_in, n_out = k.stage["ret_in"], k.stage["ret_out"]
    cos, sin = k.const("cos"), k.const("sin")

    s_rot, s_vc = k.sem("ret_rotated"), k.sem("ret_values_copied")
    with nc.Block() as block:
        @block.sync
        def _(sp):
            load_until(k, sp, n_in + 16 + RING)

        @block.tensor
        def _(pe):
            for t in range(16):
                wait_slot(k, pe, n_in + t)
                if 2 <= t < 10:
                    pe.wait_ge(s_rot, t - 1)
                elif t >= 10:
                    pe.wait_ge(s_vc, t - 9)
                w = slot(k, n_in + t, 256)
                for m in range(2):
                    for c in range(DC):
                        mm = nc.tensor.matmul(k.ps[:, 2 * (t % 2) + m, 0:T], w[:, c, m * P:(m + 1) * P], k.h[:, c, :],
                                              start=(c == 0), stop=(c == DC - 1))
                mm.then_inc(k.ring_free[(n_in + t) % RING], 1)

        @block.vector
        def _(v):
            for t in range(8):
                wait_used(k, v, n_in + t)
                dst, scale = (q, 1.0) if t < 4 else (kk, RDK ** -0.5)
                h = t % 4
                x1, x2 = k.ps[:, 2 * (t % 2), 0:T], k.ps[:, 2 * (t % 2) + 1, 0:T]
                for j, (a, b) in enumerate(((x1, cos), (x2, sin), (x1, sin), (x2, cos))):
                    ins = nc.vector.scalar_tensor_tensor(tmp[:, j], a, scale, b, ALU.mult, ALU.mult)
                ins.then_inc(s_rot, 1)
                v.wait_ge(s_rot, t + 1)
                nc.vector.tensor_tensor(dst[:, 2 * h], tmp[:, 0], tmp[:, 1], ALU.subtract)
                k.dve.link(v, nc.vector.tensor_tensor(dst[:, 2 * h + 1], tmp[:, 2], tmp[:, 3], ALU.add))

        @block.scalar
        def _(act):
            for t in range(8, 16):
                wait_used(k, act, n_in + t)
                for m in range(2):
                    ins = nc.scalar.copy(vo[:, 2 * (t - 8) + m], k.ps[:, 2 * (t % 2) + m, 0:T])
                ins.then_inc(s_vc, 1)

    tr, trs, s_at, s_o, s_st = (k.sem(f"ret_{n}") for n in ("tokens_first", "keys_first", "scores", "heads", "state"))
    c_v, c_k, c_at, c_o, c_st = (k.sem(f"ret_{n}") for n in (
        "values_out", "keys_out", "scores_out", "heads_out", "state_out"))
    c_out = k.stored["ret_state_stored"]
    with nc.Block() as block:
        @block.tensor
        def _(pe):
            for h in range(RH):
                b = h % 2
                if h:
                    pe.wait_ge(c_v, h)
                for j in range(2):
                    for c in range(4):
                        mm = nc.tensor.transpose(k.ps[:, j, c * P:(c + 1) * P], vo[:, 4 * h + c, j * P:(j + 1) * P],
                                                 k.ident)
                for c in range(4):
                    mm = nc.tensor.transpose(k.ps[0:NS, 3, c * P:(c + 1) * P], vo[:, 4 * h + c, TP:T], k.ident)
                mm.then_inc(tr, 1)
                if h:
                    pe.wait_ge(c_k, h)
                for j in range(2):
                    for c in range(2):
                        mm = nc.tensor.transpose(k.ps[:, 2, (2 * j + c) * P:(2 * j + c + 1) * P],
                                                 kk[:, 2 * h + c, j * P:(j + 1) * P], k.ident)
                mm.then_inc(trs, 1)
                if h:
                    pe.wait_ge(c_at, h)
                for j in range(2):
                    for c in range(2):
                        mm = nc.tensor.matmul(k.ps[:, 4, j * TP:j * TP + TP - j * P],
                                              kk[:, 2 * h + c, j * P:(j + 1) * P], q[:, 2 * h + c, j * P:TP],
                                              start=(c == 0), stop=(c == 1))
                mm.then_inc(s_at, 1)
                pe.wait_ge(c_v, h + 1)
                pe.wait_ge(c_k, h + 1)
                if h:
                    pe.wait_ge(c_st, 2 * h - 1)
                for c in range(2):
                    if c:
                        pe.wait_ge(c_st, 2 * h + 1)
                    for j in range(2):
                        mm = nc.tensor.matmul(k.ps[:, 7, :], kn[:, b, j, c * P:(c + 1) * P], vn[:, b, j, :],
                                              start=(j == 0), stop=(j == 1))
                    mm.then_inc(s_st, 1)
                    if c == 0:
                        pe.wait_ge(c_at, h + 1)
                        if h:
                            pe.wait_ge(c_o, h)
                        for cc in range(4):
                            o = k.ps[:, 5 + cc // 2, (cc % 2) * TP:(cc % 2 + 1) * TP]
                            nc.tensor.matmul(o, vn[:, b, 0, cc * P:(cc + 1) * P], att[:, 0:TP], start=True, stop=False)
                            mm = nc.tensor.matmul(o[:, P:TP], vn[:, b, 1, cc * P:(cc + 1) * P], att[:, TP:TP + P],
                                                  start=False, stop=True)
                        mm.then_inc(s_o, 1)

        @block.scalar
        def _(act):
            for h in range(RH):
                act.wait_ge(tr, h + 1)
                if h >= 2:
                    act.wait_ge(s_st, 2 * h - 2)
                for j in range(2):
                    nc.scalar.copy(vn[:, h % 2, j, :], k.ps[:, j, :])
                nc.scalar.copy(vs[:, h * RDV:(h + 1) * RDV], k.ps[0:NS, 3, :]).then_inc(c_v, 1)
                act.wait_ge(s_o, h + 1)
                for c in range(2):
                    ins = nc.scalar.copy(vo[:, 4 * h + 2 * c:4 * h + 2 * c + 2, 0:TP],
                                         k.ps[:, 5 + c, :].rearrange("p (c t) -> p c t", c=2))
                ins.then_inc(c_o, 1)

        @block.vector
        def _(v):
            for h in range(RH):
                v.wait_ge(trs, h + 1)
                if h >= 2:
                    v.wait_ge(s_st, 2 * h - 2)
                for j in range(2):
                    ins = nc.vector.tensor_scalar(kn[:, h % 2, j, :], k.ps[:, 2, j * TP:(j + 1) * TP],
                                                  k.const("kdec")[:, j * RH + h:j * RH + h + 1], None, ALU.mult)
                ins.then_inc(c_k, 1)
                v.wait_ge(s_at, h + 1)
                if h:
                    v.wait_ge(s_o, h)
                dec = k.const("decay")[:, h * TP:(h + 1) * TP]
                nc.vector.tensor_tensor(att[:, 0:TP], k.ps[:, 4, 0:TP], dec, ALU.mult)
                nc.vector.tensor_tensor(att[:, TP:TP + P], k.ps[:, 4, TP:TP + P], dec[:, 0:P],
                                        ALU.mult).then_inc(c_at, 1)
                for c in range(2):
                    v.wait_ge(s_st, 2 * h + c + 1)
                    if h >= 2 and c == 0:
                        v.wait_ge(c_out, 16 * (h - 1))
                    nc.vector.tensor_copy(st[:, h % 2, c, :], k.ps[:, 7, :]).then_inc(c_st, 1)

        @block.gpsimd
        def _(pool):
            for h in range(RH):
                pool.wait_ge(c_st, 2 * h + 2)
                pool.dma_start(out["ret_prompt"][0, 0, h].rearrange("(c p) n -> p c n", p=P),
                               st[:, h % 2]).then_inc(c_out, 16)
                pool.wait_ge(c_out, 16 * (h + 1))

    s_bc, s_out, s_new, s_q = (k.sem(f"ret_sample_{n}") for n in ("values_spread", "outer", "state_new", "read"))
    s_ldb = [k.sem(f"ret_sample_state_loaded{b}") for b in range(4)]
    s_stb = [k.stored[f"ret_sample_state_stored{b}"] for b in range(4)]
    units = [(b, h) for b in range(NS) for h in range(RH)]
    with nc.Block() as block:
        @block.sync
        def _(sp):
            for u, (b, h) in enumerate(units):
                if u >= 4:
                    sp.wait_ge(s_stb[u % 4], 16 * (u // 4))
                sp.dma_start(st[:, u % 4], inp["state_ret"][0, b, h].rearrange("(c p) n -> p c n", p=P))\
                    .then_inc(s_ldb[u % 4], 16)

        @block.gpsimd
        def _(pool):
            for u, (b, h) in enumerate(units):
                pool.wait_ge(s_new, 2 * u + 2)
                pool.wait_ge(s_q, u + 1)
                pool.dma_start(out["ret_sample"][0, b, h].rearrange("(c p) n -> p c n", p=P), st[:, u % 4])\
                    .then_inc(s_stb[u % 4], 16)
            for b in range(4):
                pool.wait_ge(s_stb[b], 16 * len(units) // 4)

        @block.tensor
        def _(pe):
            for u in range(len(units) + 1):
                if u < len(units):
                    b, h = units[u]
                    if u >= 2:
                        pe.wait_ge(s_out, 2 * (u - 1))
                    nc.tensor.matmul(k.ps[:, u % 2, :], k.ident[0:NS, b:b + 1].to_broadcast([NS, P]),
                                     vs[:, h * RDV:(h + 1) * RDV], start=True, stop=True).then_inc(s_bc, 1)
                if u >= 1:
                    b, h = units[u - 1]
                    pe.wait_ge(s_new, 2 * u)
                    for cc in range(4):
                        col = (4 * h + cc) * NS + b
                        for c in range(2):
                            mm = nc.tensor.matmul(k.ps[:, 2, col:col + 1], st[:, (u - 1) % 4, c, cc * P:(cc + 1) * P],
                                                  q[:, 2 * h + c, TP + b:TP + b + 1], start=(c == 0), stop=(c == 1))
                    mm.then_inc(s_q, 1)

        @block.scalar
        def _(act):
            for u, (b, h) in enumerate(units):
                act.wait_ge(s_bc, u + 1)
                for c in range(2):
                    if u >= 1:
                        act.wait_ge(s_new, 2 * (u - 1) + c + 1)
                    nc.scalar.activation(outer[:, c, :], k.ps[:, u % 2, :], ACT.Copy,
                                         scale=kk[:, 2 * h + c, TP + b:TP + b + 1]).then_inc(s_out, 1)

        @block.vector
        def _(v):
            for u, (b, h) in enumerate(units):
                v.wait_ge(s_ldb[u % 4], 16 * (u // 4 + 1))
                for c in range(2):
                    v.wait_ge(s_out, 2 * u + c + 1)
                    nc.vector.scalar_tensor_tensor(st[:, u % 4, c, :], st[:, u % 4, c, :], GAMMA[h], outer[:, c, :],
                                                   ALU.mult, ALU.add).then_inc(s_new, 1)
            v.wait_ge(s_q, len(units))
            nc.vector.tensor_copy(vo[:, :, TP:T], k.ps[:, 2, 0:16 * NS].rearrange("p (c t) -> p c t", c=16))

    head_norm(k, "ret", vo, 4, RH, k.ret_g, center=True)

    gate_and_out(k, "ret", vo, n_in + 16, 8, n_out, 128, 16, 0, tmp)


def head_norm(k, tag, o, per, heads, gain, center):
    nc = k.nc
    width = per * P
    s_mu, s_cen, s_sq, s_ss, s_ms, s_rt, s_sqf = (k.sem(f"{tag}_norm_{n}") for n in (
        "sums", "centered", "squared", "square_sums", "meansq", "root", "squares_used"))
    root = k.scratch[:, k.size - 2 * heads * T:k.size].rearrange("p (b h t) -> p b h t", b=2, h=heads)
    squares = k.scratch[:, k.size - 2 * heads * T - 2 * T:k.size - 2 * heads * T].rearrange("p (b t) -> p b t", b=2)
    rstd = k.rstd[:, 0:heads * T].rearrange("p (h t) -> p h t", h=heads)
    with nc.Block() as block:
        @block.tensor
        def _(pe):
            if center:
                for h in range(heads):
                    for c in range(per):
                        mm = nc.tensor.matmul(k.ps[:, h, 0:T], k.ones, o[:, per * h + c, :], start=(c == 0),
                                              stop=(c == per - 1))
                    mm.then_inc(s_mu, 1)
            for n in range(heads * per):
                h, c = divmod(n, per)
                pe.wait_ge(s_sq, n + 1)
                mm = nc.tensor.matmul(k.ps[:, 4 + h, 0:T], k.ones, squares[:, n % 2], start=(c == 0),
                                      stop=(c == per - 1))
                mm.then_inc(s_ss, 1)

        @block.scalar
        def _(act):
            for n in range(heads * per):
                if center:
                    act.wait_ge(s_cen, n + 1)
                if n >= 2:
                    act.wait_ge(s_ss, n - 1)
                nc.scalar.activation(squares[:, n % 2], o[:, n, :], ACT.Square).then_inc(s_sq, 1)
            act.wait_ge(s_ms, heads)
            nc.scalar.activation(root[:, 1].rearrange("p h t -> p (h t)"), root[:, 0].rearrange("p h t -> p (h t)"),
                                 ACT.Sqrt).then_inc(s_rt, 1)

        @block.vector
        def _(v):
            if center:
                for n in range(heads * per):
                    v.wait_ge(s_mu, n // per + 1)
                    nc.vector.scalar_tensor_tensor(o[:, n, :], k.ps[:, n // per, 0:T], -1.0 / width, o[:, n, :],
                                                   ALU.mult, ALU.add).then_inc(s_cen, 1)
                v.wait_ge(s_cen, heads * per)
            for h in range(heads):
                v.wait_ge(s_ss, per * (h + 1))
                nc.vector.tensor_scalar(root[:, 0, h, :], k.ps[:, 4 + h, 0:T], 1.0 / width, EPS, ALU.mult,
                                        ALU.add).then_inc(s_ms, 1)
            v.wait_ge(s_rt, 1)
            k.dve.link(v, nc.vector.reciprocal(rstd.rearrange("p h t -> p (h t)"),
                                               root[:, 1].rearrange("p h t -> p (h t)")))
            for n in range(heads * per):
                nc.vector.scalar_tensor_tensor(o[:, n, :], o[:, n, :], gain[:, n:n + 1], rstd[:, n // per, :],
                                               ALU.mult, ALU.mult)


def gate_and_out(k, tag, o, n_gate, gates, n_out, width, kc, layer, tmp):
    nc = k.nc
    s_sil, s_mul, s_add = (k.sem(f"{tag}_{n}") for n in ("gate_silu", "gated", "residual_added"))
    per = width // P
    outs = D // width
    small = k.scratch[:, k.size - NS:k.size]
    with nc.Block() as block:
        @block.sync
        def _(sp):
            load_until(k, sp, n_out + outs + RING)

        @block.tensor
        def _(pe):
            for t in range(gates):
                wait_slot(k, pe, n_gate + t)
                w = slot(k, n_gate + t, 256)
                for m in range(2):
                    n = 2 * t + m
                    if n >= 4:
                        pe.wait_ge(s_sil, n - 3)
                    for c in range(DC):
                        mm = nc.tensor.matmul(k.ps[:, n % 4, 0:T], w[:, c, m * P:(m + 1) * P], k.h[:, c, :],
                                              start=(c == 0), stop=(c == DC - 1))
                mm.then_inc(k.ring_free[(n_gate + t) % RING], 1)
            for t in range(outs):
                wait_slot(k, pe, n_out + t)
                w = slot(k, n_out + t, width)
                for m in range(per):
                    n = per * t + m
                    if n >= 4:
                        pe.wait_ge(s_add, n - 3)
                    for c in range(kc):
                        if n == 0:
                            pe.wait_ge(s_mul, c + 1)
                        mm = nc.tensor.matmul(k.ps[:, 4 + n % 4, 0:T], w[:, c, m * P:(m + 1) * P], o[:, c, :],
                                              start=(c == 0), stop=(c == kc - 1))
                mm.then_inc(k.ring_free[(n_out + t) % RING], 1)

        @block.scalar
        def _(act):
            for n in range(2 * gates):
                wait_used(k, act, n_gate + n // 2)
                if n >= 4:
                    act.wait_ge(s_mul, n - 3)
                nc.scalar.activation(tmp[:, n % 4], k.ps[:, n % 4, 0:T], ACT.Silu).then_inc(s_sil, 1)

        @block.vector
        def _(v):
            for n in range(2 * gates):
                v.wait_ge(s_sil, n + 1)
                nc.vector.tensor_tensor(o[:, n, :], o[:, n, :], tmp[:, n % 4], ALU.mult).then_inc(s_mul, 1)
            for n in range(DC):
                wait_used(k, v, n_out + n // per)
                add_gated(k, v, n, k.ps[:, 4 + n % 4, :], k.mod[:, layer, 2], small).then_inc(s_add, 1)
                if n < DC - 1:
                    v.wait_ge(s_add, n + 1)



def gla(k):
    nc, inp, out = k.nc, k.inp, k.out
    sc = k.scratch
    at = [0]

    def area(cols):
        at[0] += cols
        assert at[0] <= k.size
        return sc[:, at[0] - cols:at[0]]

    q = area(GH * T).rearrange("p (c t) -> p c t", c=GH)
    kk = area(GH * T).rearrange("p (c t) -> p c t", c=GH)
    vo = area(8 * T).rearrange("p (c t) -> p c t", c=8)
    z = area(GH * T).rearrange("p (c t) -> p c t", c=GH)
    ez = area(GH * T).rearrange("p (c t) -> p c t", c=GH)
    az = area(GH * T).rearrange("p (c t) -> p c t", c=GH)
    alpha = area(GH * NS).rearrange("p (c t) -> p c t", c=GH)
    edge = area(GH * 2 * 3).rearrange("p (h j n) -> p h j n", h=GH, j=2)
    last_ = area(GH)
    qe = area(TP)
    ke = area(TP)
    q0 = area(P)
    kd = area(TP)
    fac = area(4 * TP).rearrange("p (b t) -> p b t", b=4)
    knat = area(TP).rearrange("p (j n) -> p j n", j=2)
    vn = area(2 * GDV).rearrange("p (j n) -> p j n", j=2)
    att = area(TP).rearrange("p (j n) -> p j n", j=2)
    s1 = area(GDV)
    s2 = area(2 * GDV).rearrange("p (b n) -> p b n", b=2)
    vs = area(GH * GDV)[0:NS, :]
    st = area(2 * GH * GDV).rearrange("p (b h n) -> p b h n", b=2, h=GH)
    outer = area(GH * GDV).rearrange("p (h n) -> p h n", h=GH)
    tmp = area(4 * T).rearrange("p (b t) -> p b t", b=4)
    a1 = area(DC * RANK).rearrange("p (c r) -> p c r", c=DC)
    a2 = area(GH * GDK)[0:RANK, :]
    low = area(T)[0:RANK, :]
    n_in, n_out = k.stage["gla_in"], k.stage["gla_out"]

    s_w, s_low, s_lowc, s_z, s_zc, s_qk, s_abs, s_exp, s_ln, s_cum, s_edge, s_al = (k.sem(f"gla_{n}") for n in (
        "gate_weights", "low_rank", "low_rank_out", "logits", "logits_out", "copied", "absolute", "exp", "log",
        "cumulated", "edges", "alphas"))
    with nc.Block() as block:
        @block.sync
        def _(sp):
            sp.dma_start(a1, inp["gla_w_a1"][0].rearrange("(c p) r -> p c r", p=P)).then_inc(s_w, 16)
            sp.dma_start(a2, inp["gla_w_a2"][0]).then_inc(s_w, 16)
            load_until(k, sp, n_in + 8 + RING)

        @block.tensor
        def _(pe):
            pe.wait_ge(s_w, 32)
            for c in range(DC):
                mm = nc.tensor.matmul(k.ps[0:RANK, 4, 0:T], a1[:, c, :], k.h[:, c, :], start=(c == 0),
                                      stop=(c == DC - 1))
            mm.then_inc(s_low, 1)
            for t in range(8):
                wait_slot(k, pe, n_in + t)
                if t >= 2:
                    pe.wait_ge(s_qk, 2 * (t - 1))
                w = slot(k, n_in + t, 256)
                for m in range(2):
                    for c in range(DC):
                        mm = nc.tensor.matmul(k.ps[:, 2 * (t % 2) + m, 0:T], w[:, c, m * P:(m + 1) * P], k.h[:, c, :],
                                              start=(c == 0), stop=(c == DC - 1))
                mm.then_inc(k.ring_free[(n_in + t) % RING], 1)
                if t == 0:
                    pe.wait_ge(s_lowc, 1)
                    for h in range(GH):
                        if h >= 3:
                            pe.wait_ge(s_zc, h - 2)
                        nc.tensor.matmul(k.ps[:, 5 + h % 3, 0:T], a2[:, h * P:(h + 1) * P], low, start=True,
                                         stop=True).then_inc(s_z, 1)

        @block.scalar
        def _(act):
            act.wait_ge(s_low, 1)
            nc.scalar.copy(low, k.ps[0:RANK, 4, 0:T]).then_inc(s_lowc, 1)
            for h in range(GH):
                act.wait_ge(s_z, h + 1)
                nc.scalar.activation(z[:, h], k.ps[:, 5 + h % 3, 0:T], ACT.Identity,
                                     bias=k.b_a[:, h:h + 1]).then_inc(s_zc, 1)
            for t in range(8):
                wait_used(k, act, n_in + t)
                for m in range(2):
                    n = 2 * t + m
                    src = k.ps[:, 2 * (t % 2) + m, 0:T]
                    if t < 2:
                        ins = nc.scalar.activation(q[:, n], src, ACT.Copy, scale=GDK ** -0.5)
                    elif t < 4:
                        ins = nc.scalar.copy(kk[:, n - 4], src)
                    else:
                        ins = nc.scalar.copy(vo[:, n - 8], src)
                    ins.then_inc(s_qk, 1)
                if t == 1:
                    act.wait_ge(s_abs, 1)
                    flat = lambda a: a.rearrange("p c t -> p (c t)")
                    nc.scalar.activation(flat(ez), flat(az), ACT.Exp, scale=-1.0).then_inc(s_exp, 1)
                    act.wait_ge(s_exp, 1)
                    nc.scalar.activation(flat(az), flat(ez), ACT.Ln, bias=1.0).then_inc(s_ln, 1)
            act.wait_ge(s_cum, 1)
            nc.scalar.activation(alpha, z[:, :, TP:T], ACT.Exp, scale=1.0 / TAU)
            act.wait_ge(s_edge, 1)
            nc.scalar.activation(last_, edge[:, :, 1, 2], ACT.Exp)

        @block.vector
        def _(v):
            link = lambda ins: k.dve.link(v, ins)
            v.wait_ge(s_zc, GH)
            flat = lambda a: a.rearrange("p c t -> p (c t)")
            nc.vector.scalar_tensor_tensor(flat(az), flat(z), -1.0, flat(z), ALU.mult, ALU.max).then_inc(s_abs, 1)
            v.wait_ge(s_ln, 1)
            link(nc.vector.scalar_tensor_tensor(flat(ez), flat(z), 0.0, flat(az), ALU.min, ALU.subtract))
            for h in range(GH):
                for j in range(2):
                    nc.vector.tensor_tensor_scan(z[:, h, j * P:(j + 1) * P], k.ones, ez[:, h, j * P:(j + 1) * P], 0.0,
                                                 ALU.mult, ALU.add)
            nc.vector.tensor_copy(z[:, :, TP:T], ez[:, :, TP:T]).then_inc(s_cum, 1)
            v.wait_ge(s_cum, 1)
            zj = z[:, :, 0:TP].rearrange("p h (j t) -> p h j t", j=2)
            nc.vector.tensor_scalar(edge[:, :, :, 0], zj[:, :, :, P // 2 - 1], -1.0 / TAU, None, ALU.mult)
            nc.vector.tensor_scalar(edge[:, :, :, 1], zj[:, :, :, P // 2 - 1], 1.0 / TAU, None, ALU.mult)
            nc.vector.tensor_scalar(edge[:, :, :, 2], zj[:, :, :, P - 1], 1.0 / TAU, None, ALU.mult).then_inc(s_edge, 1)

    tv, s_f, s_e, s_kt, s_a, s_s1, s_o, s_s2 = (k.sem(f"gla_{n}") for n in (
        "tokens_first", "factors", "decayed", "keys_first", "scores", "state_mid", "heads", "state_last"))
    c_v, c_k, c_a, c_s1, c_o, c_s2 = (k.sem(f"gla_{n}") for n in (
        "values_out", "keys_out", "scores_out", "state_mid_out", "heads_out", "state_out"))
    c_out = k.stored["gla_state_stored"]
    with nc.Block() as block:
        @block.tensor
        def _(pe):
            for h in range(GH):
                if h:
                    pe.wait_ge(c_v, h)
                for j in range(2):
                    for c in range(2):
                        nc.tensor.transpose(k.ps[:, 0, (2 * j + c) * P:(2 * j + c + 1) * P],
                                            vo[:, 2 * h + c, j * P:(j + 1) * P], k.ident)
                for c in range(2):
                    mm = nc.tensor.transpose(k.ps[0:NS, 1, c * P:(c + 1) * P], vo[:, 2 * h + c, TP:T], k.ident)
                mm.then_inc(tv, 1)
                pe.wait_ge(s_e, h + 1)
                if h:
                    pe.wait_ge(c_k, h)
                    pe.wait_ge(c_a, h)
                for j in range(2):
                    mm = nc.tensor.transpose(k.ps[:, 2, j * P:(j + 1) * P], kd[:, j * P:(j + 1) * P], k.ident)
                mm.then_inc(s_kt, 1)
                for j in range(2):
                    mm = nc.tensor.matmul(k.ps[:, 3, j * P:(j + 1) * P], ke[:, j * P:(j + 1) * P],
                                          qe[:, j * P:(j + 1) * P], start=True, stop=True)
                mm.then_inc(s_a, 1)
                pe.wait_ge(c_v, h + 1)
                pe.wait_ge(c_k, h + 1)
                if h:
                    pe.wait_ge(c_s1, h)
                    pe.wait_ge(c_s2, h)
                nc.tensor.matmul(k.ps[:, 4, 0:GDV], knat[:, 0, :], vn[:, 0, :], start=True, stop=True).then_inc(s_s1, 1)
                nc.tensor.matmul(k.ps[:, 5, 0:GDV], knat[:, 1, :], vn[:, 1, :], start=True, stop=True).then_inc(s_s2, 1)
                pe.wait_ge(c_a, h + 1)
                pe.wait_ge(c_s1, h + 1)
                if h:
                    pe.wait_ge(c_o, h)
                for c in range(2):
                    o = k.ps[:, 6, c * TP:(c + 1) * TP]
                    nc.tensor.matmul(o[:, 0:P], vn[:, 0, c * P:(c + 1) * P], att[:, 0, :], start=True, stop=True)
                    nc.tensor.matmul(o[:, P:TP], vn[:, 1, c * P:(c + 1) * P], att[:, 1, :], start=True, stop=False)
                    mm = nc.tensor.matmul(o[:, P:TP], s1[:, c * P:(c + 1) * P], q0, start=False, stop=True)
                mm.then_inc(s_o, 1)

        @block.scalar
        def _(act):
            for h in range(GH):
                if h:
                    act.wait_ge(s_e, h)
                for j in range(2):
                    cols = slice(j * P, (j + 1) * P)
                    nc.scalar.activation(fac[:, 0, cols], z[:, h, cols], ACT.Exp, scale=1.0 / TAU,
                                         bias=edge[:, h, j, 0:1])
                    nc.scalar.activation(fac[:, 1, cols], z[:, h, cols], ACT.Exp, scale=-1.0 / TAU,
                                         bias=edge[:, h, j, 1:2])
                    nc.scalar.activation(fac[:, 2, cols], z[:, h, cols], ACT.Exp, scale=-1.0 / TAU,
                                         bias=edge[:, h, j, 2:3])
                nc.scalar.activation(fac[:, 3, 0:P], z[:, h, P:TP], ACT.Exp, scale=1.0 / TAU).then_inc(s_f, 1)
                act.wait_ge(tv, h + 1)
                if h:
                    act.wait_ge(s_o, h)
                nc.scalar.copy(vn.rearrange("p j n -> p (j n)"), k.ps[:, 0, :])
                nc.scalar.copy(vs[:, h * GDV:(h + 1) * GDV], k.ps[0:NS, 1, 0:GDV]).then_inc(c_v, 1)
                act.wait_ge(s_o, h + 1)
                nc.scalar.copy(vo[:, 2 * h:2 * h + 2, 0:TP], k.ps[:, 6, :].rearrange("p (c t) -> p c t", c=2))\
                    .then_inc(c_o, 1)

        @block.vector
        def _(v):
            for h in range(GH):
                v.wait_ge(s_f, h + 1)
                if h:
                    v.wait_ge(s_o, h)
                nc.vector.tensor_tensor(qe, q[:, h, 0:TP], fac[:, 0], ALU.mult)
                nc.vector.tensor_tensor(ke, kk[:, h, 0:TP], fac[:, 1], ALU.mult)
                nc.vector.tensor_tensor(kd, kk[:, h, 0:TP], fac[:, 2], ALU.mult)
                nc.vector.tensor_tensor(q0, q[:, h, P:TP], fac[:, 3, 0:P], ALU.mult).then_inc(s_e, 1)
                v.wait_ge(s_kt, h + 1)
                nc.vector.tensor_copy(knat.rearrange("p j n -> p (j n)"), k.ps[:, 2, 0:TP]).then_inc(c_k, 1)
                v.wait_ge(s_a, h + 1)
                nc.vector.tensor_tensor(att, k.ps[:, 3, 0:TP].rearrange("p (j n) -> p j n", j=2),
                                        k.const("causal").unsqueeze(1).to_broadcast([P, 2, P]),
                                        ALU.mult).then_inc(c_a, 1)
                v.wait_ge(s_s1, h + 1)
                nc.vector.tensor_copy(s1, k.ps[:, 4, 0:GDV]).then_inc(c_s1, 1)
                v.wait_ge(c_s1, h + 1)
                v.wait_ge(s_s2, h + 1)
                if h >= 2:
                    v.wait_ge(c_out, 16 * (h - 1))
                nc.vector.scalar_tensor_tensor(s2[:, h % 2], s1, last_[:, h:h + 1], k.ps[:, 5, 0:GDV], ALU.mult,
                                               ALU.add).then_inc(c_s2, 1)

        @block.gpsimd
        def _(pool):
            for h in range(GH):
                pool.wait_ge(c_s2, h + 1)
                pool.dma_start(out["gla_prompt"][0, 0, h], s2[:, h % 2]).then_inc(c_out, 16)
                pool.wait_ge(c_out, 16 * (h + 1))

    s_bc, s_out, s_new, s_q = (k.sem(f"gla_sample_{n}") for n in ("values_spread", "outer", "state_new", "read"))
    s_ldb = [k.sem(f"gla_sample_state_loaded{b}") for b in range(2)]
    s_stb = [k.stored[f"gla_sample_state_stored{b}"] for b in range(2)]
    with nc.Block() as block:
        @block.sync
        def _(sp):
            for b in range(NS):
                if b >= 2:
                    sp.wait_ge(s_stb[b % 2], 16 * (b // 2))
                sp.dma_start(st[:, b % 2], inp["state_gla"][0, b].rearrange("h p n -> p h n")).then_inc(s_ldb[b % 2], 16)

        @block.gpsimd
        def _(pool):
            for b in range(NS):
                pool.wait_ge(s_new, GH * (b + 1))
                pool.wait_ge(s_q, b + 1)
                pool.dma_start(out["gla_sample"][0, b].rearrange("h p n -> p h n"), st[:, b % 2])\
                    .then_inc(s_stb[b % 2], 16)
            for b in range(2):
                pool.wait_ge(s_stb[b], 16 * NS // 2)

        @block.tensor
        def _(pe):
            for b in range(NS + 1):
                if b < NS:
                    for i in range(2):
                        if b >= 1:
                            pe.wait_ge(s_out, GH * (b - 1) + 2 * i + 2)
                        nc.tensor.matmul(k.ps[:, i, :], k.ident[0:NS, b:b + 1].to_broadcast([NS, P]),
                                         vs[:, i * 512:(i + 1) * 512], start=True, stop=True).then_inc(s_bc, 1)
                if b >= 1:
                    pe.wait_ge(s_new, GH * b)
                    for h in range(GH):
                        for c in range(2):
                            col = (2 * h + c) * NS + b - 1
                            mm = nc.tensor.matmul(k.ps[:, 2, col:col + 1], st[:, (b - 1) % 2, h, c * P:(c + 1) * P],
                                                  q[:, h, TP + b - 1:TP + b], start=True, stop=True)
                    mm.then_inc(s_q, 1)

        @block.scalar
        def _(act):
            for b in range(NS):
                for h in range(GH):
                    act.wait_ge(s_bc, 2 * b + h // 2 + 1)
                    if b:
                        act.wait_ge(s_new, GH * (b - 1) + h + 1)
                    nc.scalar.activation(outer[:, h, :], k.ps[:, h // 2, (h % 2) * GDV:(h % 2 + 1) * GDV], ACT.Copy,
                                         scale=kk[:, h, TP + b:TP + b + 1]).then_inc(s_out, 1)

        @block.vector
        def _(v):
            for b in range(NS):
                v.wait_ge(s_ldb[b % 2], 16 * (b // 2 + 1))
                for h in range(GH):
                    v.wait_ge(s_out, GH * b + h + 1)
                    nc.vector.scalar_tensor_tensor(st[:, b % 2, h, :], st[:, b % 2, h, :], alpha[:, h, b:b + 1],
                                                   outer[:, h, :], ALU.mult, ALU.add).then_inc(s_new, 1)
            v.wait_ge(s_q, NS)
            nc.vector.tensor_copy(vo[:, :, TP:T], k.ps[:, 2, 0:8 * NS].rearrange("p (c t) -> p c t", c=8))

    head_norm(k, "gla", vo, 2, GH, k.gla_g, center=False)
    gate_and_out(k, "gla", vo, n_in + 8, 4, n_out, 256, 8, 1, tmp)



def final(k):
    nc, out = k.nc, k.out
    norm(k, DEPTH, 0, "")
    s_tr, s_cp, s_st = k.sem("y_token_major"), k.sem("y_copied"), k.sem("y_stored")
    y = k.scratch[:, 0:TT * D].rearrange("p (t d) -> p t d", t=TT)
    with nc.Block() as block:
        @block.tensor
        def _(pe):
            for t, (t0, n) in enumerate(TOKENS):
                for c in range(DC):
                    mm = nc.tensor.transpose(k.ps[0:n, 2 * t + c // 4, (c % 4) * P:(c % 4 + 1) * P],
                                             k.h[:, c, t0:t0 + n], k.ident)
                mm.then_inc(s_tr, 1)

        @block.vector
        def _(v):
            for t, (_, n) in enumerate(TOKENS):
                v.wait_ge(s_tr, t + 1)
                nc.vector.tensor_copy(y[0:n, t, :], k.ps[0:n, 2 * t:2 * t + 2, :].rearrange("p b d -> p (b d)"))\
                    .then_inc(s_cp, 1)

        @block.sync
        def _(sp):
            for t, (t0, n) in enumerate(TOKENS):
                sp.wait_ge(s_cp, t + 1)
                dst = out["y_prompt"][0, t0:t0 + n] if t < 2 else out["y_sample"].rearrange("b o d -> (b o) d")
                sp.dma_start(dst, y[0:n, t, :]).then_inc(s_st, 16)
            sp.wait_ge(s_st, 16 * TT)



def experts(k, layer):
    nc, inp = k.nc, k.inp
    sc = k.scratch
    at = [0]

    def area(cols):
        at[0] += cols
        assert at[0] <= k.size, at[0]
        return sc[:, at[0] - cols:at[0]]

    tag = f"moe{layer}"
    parts_area = area(TT * 3 * D // 2)
    parts = parts_area.bitcast(BF16).rearrange("p (t s d) -> p t s d", t=TT, s=3)
    acc = parts_area[:, 0:TT * D].rearrange("p (t d) -> p t d", t=TT)
    xg_area = area(2 * SLOT)
    xg = xg_area[:, 0:DC * EPI * CAP].rearrange("p (c n) -> p c n", c=DC)
    hot = area(TT * EPI * CAP // 2).bitcast(BF16).rearrange("p (t e s) -> p t e s", t=TT, e=EPI)
    gath = area(3 * D).rearrange("p (b d) -> p b d", b=3)
    x_extra = area(DC * CAP).rearrange("p (c n) -> p c n", c=DC)
    silu = area(EPI * FC * CAP).rearrange("p (e n) -> p e n", e=EPI)
    hid = area(EPI * FC * CAP).rearrange("p (e n) -> p e n", e=EPI)
    rows = area(D)
    sh_silu = area(FC * T).rearrange("p (m t) -> p m t", m=FC)
    sh_hid = area(FC * T).rearrange("p (m t) -> p m t", m=FC)
    wr = area(DC * NE).rearrange("p (c e) -> p c e", c=DC)
    bias = area(NE)

    def grid():
        return area(TT * NE).rearrange("p (t e) -> p t e", t=TT)

    score, biased, left, chosen, weight, rank, key = (grid() for _ in range(7))
    best = area(TT * NG * 8).rearrange("p (t g n) -> p t g n", t=TT, g=NG)
    beats = area(TT * NG * NG).rearrange("p (t g n) -> p t g n", t=TT, g=NG)
    ties = area(TT * NG * NG).rearrange("p (t g n) -> p t g n", t=TT, g=NG)
    gscore = area(TT * NG).rearrange("p (t g) -> p t g", t=TT)
    gmask = area(TT * NG).rearrange("p (t g) -> p t g", t=TT)
    top = area(TT * 8).rearrange("p (t n) -> p t n", t=TT)
    total = area(2 * TT)
    count, blocks, ends, shift = (area(NE) for _ in range(4))
    at_rows = area(TT * 8).rearrange("p (t n) -> p t n", t=TT)
    row_index = area(TT * 8).bitcast(I32).rearrange("p (t n) -> p t n", t=TT)
    row_weight = area(TT * 8).rearrange("p (t n) -> p t n", t=TT)
    lookup = area(XBP)
    extra = area(1 + XBP).bitcast(I32)
    low, high = area(1), area(1)
    found = area(2 * TT)
    w_extra = [xg_area[:, 0:SLOT], xg_area[:, SLOT:2 * SLOT], gath.rearrange("p b d -> p (b d)")[:, 0:SLOT]]
    compare = xg_area[0:1, 0:XBP * NE].rearrange("p (b e) -> p b e", b=XBP)
    rest = gath[:, 0, :]
    keep_small = area(NS)

    n_sh, n_moe = k.stage[f"shared{layer}"], k.stage[f"moe{layer}"]
    ident, ones, before, iota = k.ident, k.ones, k.const("before"), k.const("iota")

    s_w, s_log, s_sc, s_rk, s_ch, s_nat, s_natc, s_hi = (k.sem(f"{tag}_{n}") for n in (
        "router_loaded", "logits", "scores", "ranks", "chosen", "token_major", "parts", "high_part"))
    s_zero, s_clear = k.sem(f"{tag}_zeros"), k.sem(f"{tag}_rows_cleared")
    s_shs, s_shh, s_shd, s_shx, s_fill = (k.sem(f"{tag}_{n}") for n in (
        "shared_silu", "shared_hidden", "shared_down", "shared_added", "scores_filled"))
    with nc.Block() as block:
        @block.sync
        def _(sp):
            sp.dma_start(wr, inp["moe_w_router"][layer].rearrange("(c p) e -> p c e", p=P)).then_inc(s_w, 16)
            sp.dma_start(bias, inp["moe_router_bias"][layer:layer + 1, :].to_broadcast([P, NE])).then_inc(s_w, 16)
            load_until(k, sp, n_sh + 3 + RING)
            if layer == 0:
                sp.wait_ge(s_zero, 1)
                sp.dma_start(k.y[NE * CAP:, :].rearrange("(b p) d -> p b d", p=P),
                             rows.unsqueeze(1).to_broadcast([P, XBP * CAP // P, D])).then_inc(s_clear, 16)
                sp.wait_ge(s_clear, 16)

        @block.tensor
        def _(pe):
            pe.wait_ge(s_w, 32)
            for t, (t0, n) in enumerate(TOKENS):
                for c in range(DC):
                    mm = nc.tensor.matmul(k.ps[0:n, 0, t * NE:(t + 1) * NE], k.h[:, c, t0:t0 + n], wr[:, c, :],
                                          start=(c == 0), stop=(c == DC - 1))
                mm.then_inc(s_log, 1)
            for j in range(2):
                wait_slot(k, pe, n_sh + j)
                w = slot(k, n_sh + j, DE)
                for m in range(FC):
                    for c in range(DC):
                        mm = nc.tensor.matmul(k.ps[:, 2 + 2 * j + m, 0:T], w[:, c, m * P:(m + 1) * P], k.h[:, c, :],
                                              start=(c == 0), stop=(c == DC - 1))
                mm.then_inc(k.ring_free[(n_sh + j) % RING], 1)
            for t, (t0, n) in enumerate(TOKENS):
                if t:
                    pe.wait_ge(s_natc, t)
                for c in range(DC):
                    mm = nc.tensor.transpose(k.ps[0:n, 6 + c // 4, (c % 4) * P:(c % 4 + 1) * P], k.h[:, c, t0:t0 + n],
                                             ident)
                mm.then_inc(s_nat, 1)
                if t == 0:
                    pe.wait_ge(s_ch, 1)
                    for u in range(TT + 1):
                        for s in range(min(u + 1, TT)):
                            mm = nc.tensor.matmul(k.ps[:, 1, u * NE:(u + 1) * NE], before if s == u else ones,
                                                  chosen[:, s, :], start=(s == 0), stop=(s == min(u, TT - 1)))
                    mm.then_inc(s_rk, 1)
            wait_slot(k, pe, n_sh + 2)
            pe.wait_ge(s_shh, FC)
            w = slot(k, n_sh + 2, D)
            for c in range(DC):
                if c >= 4:
                    pe.wait_ge(s_shx, c - 3)
                for m in range(FC):
                    mm = nc.tensor.matmul(k.ps[:, 2 + c % 4, 0:T], w[:, m, c * P:(c + 1) * P], sh_hid[:, m],
                                          start=(m == 0), stop=(m == FC - 1))
                mm.then_inc(s_shd if c < DC - 1 else k.ring_free[(n_sh + 2) % RING], 1)

        @block.scalar
        def _(act):
            act.wait_ge(s_fill, 1)
            for t, (_, n) in enumerate(TOKENS):
                act.wait_ge(s_log, 3)
                ins = nc.scalar.activation(score[0:n, t, :], k.ps[0:n, 0, t * NE:(t + 1) * NE], ACT.Sigmoid)
            ins.then_inc(s_sc, 1)
            for m in range(FC):
                wait_used(k, act, n_sh)
                nc.scalar.activation(sh_silu[:, m], k.ps[:, 2 + m, 0:T], ACT.Silu).then_inc(s_shs, 1)
            for t, (_, n) in enumerate(TOKENS):
                act.wait_ge(s_nat, t + 1)
                src = k.ps[0:n, 6:8, :].rearrange("p b d -> p (b d)")
                nc.scalar.copy(parts[0:n, t, 0, :], src).then_inc(s_hi, 1)

        @block.vector
        def _(v):
            link = lambda ins: k.dve.link(v, ins)
            if layer == 0:
                nc.vector.memset(rows, 0.0).then_inc(s_zero, 1)
            nc.vector.memset(score[:, TT - 1, :], 0.0).then_inc(s_fill, 1)
            v.wait_ge(s_sc, 1)
            v.wait_ge(s_w, 32)
            link(nc.vector.tensor_tensor(biased, score, bias.unsqueeze(1).to_broadcast([P, TT, NE]), ALU.add))
            for t in range(TT):
                for g in range(NG):
                    ins = nc.vector.max(out=best[:, t, g, :], in_=biased[:, t, g * 8:(g + 1) * 8])
            link(ins)
            link(nc.vector.tensor_tensor(gscore, best[:, :, :, 0], best[:, :, :, 1], ALU.add))
            mine = gscore.unsqueeze(3).to_broadcast([P, TT, NG, NG])
            other = gscore.unsqueeze(2).to_broadcast([P, TT, NG, NG])
            nc.vector.tensor_tensor(beats, other, mine, ALU.is_gt)
            link(nc.vector.tensor_tensor(ties, other, mine, ALU.is_equal))
            tri = k.const("gtri").rearrange("p (g n) -> p g n", g=NG).unsqueeze(1).to_broadcast([P, TT, NG, NG])
            link(nc.vector.tensor_tensor(ties, ties, tri, ALU.mult))
            link(nc.vector.tensor_tensor(beats, beats, ties, ALU.add))
            link(nc.vector.tensor_reduce(gmask, beats, AX.X, ALU.add))
            link(nc.vector.tensor_scalar(gmask, gmask, TOPG - 0.5, None, ALU.is_lt))
            open_ = gmask.unsqueeze(3).to_broadcast([P, TT, NG, 8])
            b4 = biased.rearrange("p t (g n) -> p t g n", g=NG)
            link(nc.vector.tensor_tensor(b4, b4, open_, ALU.mult))
            link(nc.vector.tensor_scalar(gmask, gmask, 1.0, 1.0e30, ALU.subtract, ALU.mult))
            link(nc.vector.tensor_tensor(b4, b4, open_, ALU.add))
            for t in range(TT):
                ins = nc.vector.max(out=top[:, t, :], in_=biased[:, t, :])
            link(ins)
            for t in range(TT):
                ins = nc.vector.match_replace(out=left[:, t, :], in_to_replace=top[:, t, :], in_values=biased[:, t, :],
                                              imm_value=-3.0e38)
            link(ins)
            link(nc.vector.tensor_tensor(chosen, left, biased, ALU.not_equal))
            valid = k.const("valid").unsqueeze(2).to_broadcast([P, TT, NE])
            nc.vector.tensor_tensor(chosen, chosen, valid, ALU.mult).then_inc(s_ch, 1)
            v.wait_ge(s_ch, 1)
            for m in range(FC):
                v.wait_ge(s_shs, m + 1)
                wait_used(k, v, n_sh + 1)
                nc.vector.tensor_tensor(sh_hid[:, m], sh_silu[:, m], k.ps[:, 4 + m, 0:T], ALU.mult).then_inc(s_shh, 1)
            link(nc.vector.tensor_tensor(weight, score, chosen, ALU.mult))
            link(nc.vector.tensor_reduce(total[:, 0:TT], weight, AX.X, ALU.add))
            nv = total[:, TT:2 * TT]
            link(nc.vector.tensor_scalar(nv, k.const("valid"), -1.0, 1.0, ALU.mult, ALU.add))
            link(nc.vector.tensor_tensor(total[:, 0:TT], total[:, 0:TT], nv, ALU.add))
            link(nc.vector.reciprocal(total[:, 0:TT], total[:, 0:TT]))
            link(nc.vector.tensor_tensor(weight, weight, total[:, 0:TT].unsqueeze(2).to_broadcast([P, TT, NE]),
                                         ALU.mult))
            link(nc.vector.tensor_scalar(weight, weight, SCALE, None, ALU.mult))
            v.wait_ge(s_rk, 1)
            ranks = k.ps[:, 1, 0:TT * NE].rearrange("p (t e) -> p t e", t=TT)
            link(nc.vector.tensor_copy(rank, ranks))
            link(nc.vector.tensor_copy(count, k.ps[:, 1, TT * NE:(TT + 1) * NE]))
            link(nc.vector.tensor_scalar(blocks, count, CAP + 0.5, None, ALU.is_gt))
            for j in range(2, (T - 1) // CAP + 1):
                link(nc.vector.scalar_tensor_tensor(blocks, count, CAP * j + 0.5, blocks, ALU.is_gt, ALU.add))
            link(nc.vector.tensor_tensor_scan(ends, ones[:, 0:NE], blocks, 0.0, ALU.mult, ALU.add))
            link(nc.vector.tensor_tensor(shift, ends, blocks, ALU.subtract))
            link(nc.vector.tensor_tensor(shift, shift, iota, ALU.subtract))
            link(nc.vector.tensor_scalar(shift, shift, NE - 1.0, float(CAP), ALU.add, ALU.mult))
            link(nc.vector.scalar_tensor_tensor(key, rank, CAP - 0.5, shift.unsqueeze(1).to_broadcast([P, TT, NE]),
                                                ALU.is_gt, ALU.mult))
            link(nc.vector.tensor_tensor(key, key, rank, ALU.add))
            first = iota.unsqueeze(1).to_broadcast([P, TT, NE])
            link(nc.vector.scalar_tensor_tensor(key, first, float(CAP), key, ALU.mult, ALU.add))
            link(nc.vector.scalar_tensor_tensor(key, key, 1.0, chosen, ALU.add, ALU.mult))
            link(nc.vector.scalar_tensor_tensor(rank, rank, 1.0, chosen, ALU.add, ALU.mult))
            link(nc.vector.tensor_scalar(rank, rank, -1.0, None, ALU.add))
            link(nc.vector.tensor_copy(extra[0:1, 0:1], ends[0:1, NE - 1:NE]))
            link(nc.vector.tensor_tensor(compare, ends[0:1, :].unsqueeze(1).to_broadcast([1, XBP, NE]),
                                         iota[0:1, 0:XBP].unsqueeze(2).to_broadcast([1, XBP, NE]), ALU.is_le))
            link(nc.vector.tensor_reduce(lookup[0:1, :], compare, AX.X, ALU.add))
            link(nc.vector.tensor_scalar(lookup[0:1, :], lookup[0:1, :], NE - 1.0, None, ALU.min))
            link(nc.vector.tensor_copy(extra[0:1, 1:1 + XBP], lookup[0:1, :]))
            link(nc.vector.memset(low, NE * CAP + 1.0))
            link(nc.vector.memset(high, NE * CAP + 1.0 + CAP))
            for t, (_, n) in enumerate(TOKENS):
                v.wait_ge(s_hi, t + 1)
                src = k.ps[0:n, 6:8, :].rearrange("p b d -> p (b d)")
                link(nc.vector.tensor_tensor(rest[0:n], src, parts[0:n, t, 0, :], ALU.subtract))
                link(nc.vector.tensor_copy(parts[0:n, t, 1, :], rest[0:n]))
                nc.vector.tensor_tensor(parts[0:n, t, 2, :], rest[0:n], parts[0:n, t, 1, :],
                                        ALU.subtract).then_inc(s_natc, 1)
                v.wait_ge(s_natc, t + 1)
            for c in range(DC):
                if c < DC - 1:
                    v.wait_ge(s_shd, c + 1)
                else:
                    wait_used(k, v, n_sh + 2)
                add_gated(k, v, c, k.ps[:, 2 + c % 4, :], k.mod[:, layer, 5], keep_small).then_inc(s_shx, 1)
                v.wait_ge(s_shx, c + 1)

    s_hot, s_gat, g_even, g_odd, s_gu, s_sil, s_hid, s_dn, r_even, r_odd, s_store = (k.sem(f"{tag}_{n}") for n in (
        "one_hot", "gathered", "gathered_out_even", "gathered_out_odd", "gate_up", "silu", "hidden", "down",
        "rows_even", "rows_odd", "rows_stored"))
    PAIRS = EPI // 2

    def place(kind, e):
        n = n_moe + PLACE[(kind, e)]
        return n

    with nc.Block() as block:
        @block.sync
        def _(sp):
            with sp.Fori(1, ROUNDS) as r:
                for name, e in ROUND:
                    n = place(name, e)
                    src = inp[name][layer].rearrange("e (k p) n -> e p k n", p=P)[bass.ds(r * EPI + e, 1)]
                    src = src.rearrange("o p k n -> (o p) k n")
                    sp.wait_ge(k.ring_free[n % RING], r + n // RING)
                    sp.dma_start(slot(k, n, src.shape[2]), src).then_inc(k.ring_full[n % RING], 16)
            k.issued = n_moe + ROUNDS * RING
            load_until(k, sp, n_moe + ROUNDS * RING + RING)

        def gather(pe, r):
            pe.wait_ge(s_hot, r + 1)
            for c in range(DC):
                b = (c // 2) % 2
                if c % 2 == 0 and c >= 4:
                    pe.wait_ge(g_odd if b else g_even, 2 * r + 1)
                for t, (_, n) in enumerate(TOKENS):
                    for s in range(3):
                        mm = nc.tensor.matmul(k.ps[:, b, (c % 2) * 256:(c % 2 + 1) * 256],
                                              parts[0:n, t, s, c * P:(c + 1) * P],
                                              hot[0:n, t].rearrange("p e s -> p (e s)"),
                                              start=(t == 0 and s == 0), stop=(t == TT - 1 and s == 2))
                if c % 2:
                    mm.then_inc(s_gat, 1)

        def pe_round(pe, r, last):
            pe.wait_ge(g_even, 2 * r + 2)
            pe.wait_ge(g_odd, 2 * r + 2)
            for e in range(EPI):
                for j, name in enumerate(("moe_w_gate", "moe_w_up")):
                    n = place(name, e)
                    pe.wait_ge(k.ring_full[n % RING], 16 * (r + n // RING + 1))
                    w = slot(k, n, DE)
                    for m in range(FC):
                        for c in range(DC):
                            mm = nc.tensor.matmul(k.ps[:, 2 + e, (2 * j + m) * CAP:(2 * j + m + 1) * CAP],
                                                  w[:, c, m * P:(m + 1) * P], xg[:, c, e * CAP:(e + 1) * CAP],
                                                  start=(c == 0), stop=(c == DC - 1))
                    mm.then_inc(k.ring_free[n % RING], 1)
            if not last:
                gather(pe, r + 1)
            for p in range(PAIRS):
                pe.wait_ge(s_hid, EPI * r + 2 * p + 2)
                for e in (2 * p, 2 * p + 1):
                    n = place("moe_w_down", e)
                    pe.wait_ge(k.ring_full[n % RING], 16 * (r + n // RING + 1))
                pe.wait_ge(r_even, PAIRS * r + p + 1)
                pe.wait_ge(r_odd, PAIRS * r + p + 1)
                for half in range(2):
                    for m in range(FC):
                        for e in (2 * p, 2 * p + 1):
                            n = place("moe_w_down", e)
                            w = slot(k, n, D)
                            lo = CAP * (e % 2)
                            mm = nc.tensor.matmul(k.ps[lo:lo + CAP, 6 + half, :], hid[:, e, m * CAP:(m + 1) * CAP],
                                                  w[:, m, half * 512:(half + 1) * 512],
                                                  start=(m == 0), stop=(m == FC - 1))
                            if half == 1 and m == FC - 1:
                                mm.then_inc(k.ring_free[n % RING], 1)
                            elif half == 0 and m == FC - 1 and e % 2:
                                mm.then_inc(s_dn, 1)

        @block.tensor
        def _(pe):
            gather(pe, 0)
            with pe.Fori(0, ROUNDS - 1) as r:
                pe_round(pe, r, False)
            pe_round(pe, ROUNDS - 1, True)

        def one_hot(v, r):
            nc.vector.tensor_tensor(hot, rank[:, :, bass.ds(r * EPI, EPI)].unsqueeze(3).to_broadcast([P, TT, EPI, CAP]),
                                    iota[:, 0:CAP].unsqueeze(1).unsqueeze(1).to_broadcast([P, TT, EPI, CAP]),
                                    ALU.is_equal).then_inc(s_hot, 1)

        def take(eng, r, b, copy, sem):
            for q in range(2):
                eng.wait_ge(s_gat, DC // 2 * r + 2 * q + b + 1)
                c = 4 * q + 2 * b
                copy(xg[:, c:c + 2, :], k.ps[:, b, :].rearrange("p (c n) -> p c n", c=2)).then_inc(sem, 1)

        def pair_done(eng, r, p, half):
            if half == 0:
                eng.wait_ge(s_dn, PAIRS * r + p + 1)
            else:
                n = place("moe_w_down", 2 * p + 1)
                eng.wait_ge(k.ring_free[n % RING], r + n // RING + 1)

        @block.vector
        def _(v):
            def round_(r, last):
                for e in range(EPI):
                    v.wait_ge(s_sil, EPI * r + e + 1)
                    nc.vector.tensor_tensor(hid[:, e, :], silu[:, e, :], k.ps[:, 2 + e, 2 * CAP:4 * CAP],
                                            ALU.mult).then_inc(s_hid, 1)
                if not last:
                    take(v, r + 1, 0, nc.vector.tensor_copy, g_even)
                for p in range(PAIRS):
                    pair_done(v, r, p, 0)
                    v.wait_ge(s_store, 16 * (PAIRS * r + p + 1))
                    nc.vector.tensor_copy(rows[:, 0:512], k.ps[:, 6, :]).then_inc(r_even, 1)

            v.sem_inc(r_even, 1)
            one_hot(v, 0)
            take(v, 0, 0, nc.vector.tensor_copy, g_even)
            v.wait_ge(s_gat, DC // 2)
            one_hot(v, 1)
            with v.Fori(0, ROUNDS - 2) as r:
                round_(r, False)
                v.wait_ge(s_gat, DC // 2 * (r + 2))
                one_hot(v, r + 2)
            round_(ROUNDS - 2, False)
            round_(ROUNDS - 1, True)

        @block.scalar
        def _(act):
            def round_(r, last):
                for e in range(EPI):
                    n = place("moe_w_up", e)
                    act.wait_ge(k.ring_free[n % RING], r + n // RING + 1)
                    nc.scalar.activation(silu[:, e, :], k.ps[:, 2 + e, 0:2 * CAP], ACT.Silu).then_inc(s_sil, 1)
                if not last:
                    take(act, r + 1, 1, nc.scalar.copy, g_odd)
                for p in range(PAIRS):
                    pair_done(act, r, p, 1)
                    act.wait_ge(s_store, 16 * (PAIRS * r + p + 1))
                    nc.scalar.copy(rows[:, 512:1024], k.ps[:, 7, :]).then_inc(r_odd, 1)
                    act.wait_ge(r_even, PAIRS * r + p + 2)
                    act.wait_ge(r_odd, PAIRS * r + p + 2)
                    act.dma_start(k.y[bass.ds((EPI * r + 2 * p) * CAP, P), :], rows[:, :]).then_inc(s_store, 16)

            act.sem_inc(r_odd, 1)
            act.sem_inc(s_store, 16)
            take(act, 0, 1, nc.scalar.copy, g_odd)
            with act.Fori(0, ROUNDS - 1) as r:
                round_(r, False)
            round_(ROUNDS - 1, True)
            act.wait_ge(s_store, 16 * PAIRS * ROUNDS + 16)

    x_load, x_hot, x_gat, x_got, x_gu, x_sil, x_hid, x_dn, x_even, x_odd, x_store = (k.sem(f"{tag}_extra_{n}") for n in (
        "loaded", "one_hot", "gathered", "gathered_out", "gate_up", "silu", "hidden", "down", "rows_even",
        "rows_odd", "stored"))
    x_step = k.sem(f"{tag}_extra_vector_step")
    number = extra[0:1, 0:1]
    with nc.Block() as block:
        @block.sync
        def _(sp):
            total_ = sp.value_load(number, min_val=0, max_val=XB)
            with sp.If(total_ > 0):
                with sp.Fori(0, total_) as b:
                    e = sp.value_load(extra[0:1, bass.ds(b + 1, 1)], min_val=0, max_val=NE - 1)
                    sp.wait_ge(x_dn, b + 1)
                    for name, buf in zip(("moe_w_gate", "moe_w_up", "moe_w_down"), w_extra):
                        src = inp[name][layer].rearrange("e (k p) n -> e p k n", p=P)[bass.ds(e, 1)]
                        src = src.rearrange("o p k n -> (o p) k n")
                        sp.dma_start(buf.rearrange("p (k n) -> p k n", n=src.shape[2]), src).then_inc(x_load, 16)

        @block.tensor
        def _(pe):
            pe.sem_inc(x_dn, 1)
            total_ = pe.value_load(number, min_val=0, max_val=XB)
            with pe.If(total_ > 0):
                with pe.Fori(0, total_) as b:
                    pe.wait_ge(x_hot, b + 1)
                    for c in range(DC):
                        for t, (_, n) in enumerate(TOKENS):
                            for s in range(3):
                                mm = nc.tensor.matmul(k.ps[:, 0, c * CAP:(c + 1) * CAP],
                                                      parts[0:n, t, s, c * P:(c + 1) * P], hot[0:n, t, 0, :],
                                                      start=(t == 0 and s == 0), stop=(t == TT - 1 and s == 2))
                    mm.then_inc(x_gat, 1)
                    pe.wait_ge(x_got, b + 1)
                    pe.wait_ge(x_load, 48 * b + 48)
                    for j in range(2):
                        w = w_extra[j].rearrange("p (k n) -> p k n", n=DE)
                        for m in range(FC):
                            for c in range(DC):
                                mm = nc.tensor.matmul(k.ps[:, 2, (2 * j + m) * CAP:(2 * j + m + 1) * CAP],
                                                      w[:, c, m * P:(m + 1) * P], x_extra[:, c, :],
                                                      start=(c == 0), stop=(c == DC - 1))
                    mm.then_inc(x_gu, 1)
                    pe.wait_ge(x_hid, b + 1)
                    w = w_extra[2].rearrange("p (k n) -> p k n", n=D)
                    for half in range(2):
                        for m in range(FC):
                            mm = nc.tensor.matmul(k.ps[0:CAP, 6 + half, :], hid[:, 0, m * CAP:(m + 1) * CAP],
                                                  w[:, m, half * 512:(half + 1) * 512],
                                                  start=(m == 0), stop=(m == FC - 1))
                    mm.then_inc(x_dn, 1)

        @block.vector
        def _(v):
            total_ = v.value_load(number, min_val=0, max_val=XB)
            with v.If(total_ > 0):
                with v.Fori(0, total_) as b:
                    STEPS = 6
                    steps = [0]

                    def link(ins):
                        steps[0] += 1
                        ins.then_inc(x_step, 1)
                        v.wait_ge(x_step, STEPS * b + steps[0])

                    link(nc.vector.scalar_tensor_tensor(left, key, low, key, ALU.is_ge, ALU.mult))
                    link(nc.vector.scalar_tensor_tensor(left, left, high, left, ALU.is_lt, ALU.mult))
                    link(nc.vector.tensor_reduce(found[:, 0:TT], left, AX.X, ALU.add))
                    link(nc.vector.tensor_scalar(found[:, TT:2 * TT], found[:, 0:TT], low, None, ALU.subtract))
                    v.wait_ge(x_dn, b + 1)
                    link(nc.vector.tensor_tensor(hot[:, :, 0, :],
                                                 found[:, TT:2 * TT].unsqueeze(2).to_broadcast([P, TT, CAP]),
                                                 iota[:, 0:CAP].unsqueeze(1).to_broadcast([P, TT, CAP]),
                                                 ALU.is_equal))
                    nc.vector.tensor_scalar(low, low, float(CAP), None, ALU.add).then_inc(x_hot, 1)
                    v.wait_ge(x_hot, b + 1)
                    link(nc.vector.tensor_scalar(high, high, float(CAP), None, ALU.add))
                    v.wait_ge(x_sil, b + 1)
                    nc.vector.tensor_tensor(hid[:, 0, :], silu[:, 0, :], k.ps[:, 2, 2 * CAP:4 * CAP],
                                            ALU.mult).then_inc(x_hid, 1)
                    v.wait_ge(x_dn, b + 2)
                    v.wait_ge(x_store, 16 * b + 16)
                    nc.vector.tensor_copy(rows[0:CAP, 0:512], k.ps[0:CAP, 6, :]).then_inc(x_even, 1)
                    assert steps[0] == STEPS

        @block.scalar
        def _(act):
            act.sem_inc(x_store, 16)
            total_ = act.value_load(number, min_val=0, max_val=XB)
            with act.If(total_ > 0):
                with act.Fori(0, total_) as b:
                    act.wait_ge(x_gat, b + 1)
                    nc.scalar.copy(x_extra, k.ps[:, 0, :].rearrange("p (c n) -> p c n", c=DC)).then_inc(x_got, 1)
                    act.wait_ge(x_gu, b + 1)
                    nc.scalar.activation(silu[:, 0, :], k.ps[:, 2, 0:2 * CAP], ACT.Silu).then_inc(x_sil, 1)
                    act.wait_ge(x_dn, b + 2)
                    nc.scalar.copy(rows[0:CAP, 512:1024], k.ps[0:CAP, 7, :]).then_inc(x_odd, 1)
                    act.wait_ge(x_even, b + 1)
                    act.wait_ge(x_odd, b + 1)
                    act.dma_start(k.y[bass.ds((b + NE) * CAP, CAP), :], rows[0:CAP, :]).then_inc(x_store, 16)
                    act.wait_ge(x_store, 16 * b + 32)

    s_idx, s_use, s_acc = (k.sem(f"{tag}_{n}") for n in ("row_indices", "row_used", "token_sum"))
    items = [(t, j) for t in range(TT) for j in range(TOPK)]
    fetched_before = layer * len(items) // 3
    with nc.Block() as block:
        @block.sync
        def _(sp):
            load_until(k, sp, n_moe + ROUNDS * RING + RING)

        @block.vector
        def _(v):
            link = lambda ins: k.dve.link(v, ins)
            for t in range(TT):
                ins = nc.vector.max(out=at_rows[:, t, :], in_=key[:, t, :])
            link(ins)
            for t, (_, n) in enumerate(TOKENS):
                ins = nc.vector.tensor_scalar(row_index[0:n, t, :], at_rows[0:n, t, :], -1.0, None, ALU.add)
            ins.then_inc(s_idx, 1)
            for i, (t, j) in enumerate(items):
                link(nc.vector.scalar_tensor_tensor(left[:, t, :], key[:, t, :], at_rows[:, t, j:j + 1],
                                                    weight[:, t, :], ALU.is_equal, ALU.mult,
                                                    accum_out=row_weight[:, t, j:j + 1]))
            for i, (t, j) in enumerate(items):
                n = TOKENS[t][1]
                v.wait_ge(k.row_fetched[i % 3], 16 * (fetched_before + i // 3 + 1))
                if j == 0:
                    ins = nc.vector.tensor_scalar(acc[0:n, t, :], gath[0:n, i % 3, :], row_weight[0:n, t, j:j + 1],
                                                  None, ALU.mult)
                else:
                    ins = nc.vector.scalar_tensor_tensor(acc[0:n, t, :], gath[0:n, i % 3, :],
                                                         row_weight[0:n, t, j:j + 1], acc[0:n, t, :], ALU.mult,
                                                         ALU.add)
                ins.then_inc(s_use, 1)
                v.wait_ge(s_use, i + 1)
            for c in range(DC):
                v.wait_ge(s_acc, c + 1)
                link(add_gated(k, v, c, k.ps[:, c, :], k.mod[:, layer, 5], keep_small))

        @block.gpsimd
        def _(pool):
            pool.wait_ge(s_idx, 1)
            for i, (t, j) in enumerate(items):
                n = TOKENS[t][1]
                if i >= 3:
                    pool.wait_ge(s_use, i - 2)
                pool.indirect_dma_start(out=gath[0:n, i % 3, :], out_offset=None, in_=k.y,
                                        in_offset=bass.IndirectOffsetOnAxis(ap=row_index[0:n, t, j:j + 1], axis=0))\
                    .then_inc(k.row_fetched[i % 3], 16)

        @block.tensor
        def _(pe):
            pe.wait_ge(s_use, len(items))
            for c in range(DC):
                for t, (t0, n) in enumerate(TOKENS):
                    mm = nc.tensor.matmul(k.ps[:, c, t0:t0 + n], acc[0:n, t, c * P:(c + 1) * P], ident[0:n, 0:n],
                                          start=True, stop=True)
                mm.then_inc(s_acc, 1)



_INS = ["x_prompt", "x_sample", "state_ret", "state_gla", "c_prompt", "c_sample", "ret_w_in", "ret_norm_g",
        "ret_w_out", "gla_w_in", "gla_w_a1", "gla_w_a2", "gla_b_a", "gla_norm_g", "gla_w_out", "ada_w", "ada_b",
        "norm_mix_g", "norm_ffn_g", "moe_w_router", "moe_router_bias", "moe_w_gate", "moe_w_up", "moe_w_down",
        "sh_w_gate", "sh_w_up", "sh_w_down", "final_norm_g"]
_OUTS = [("y_prompt", (1, TP, D)), ("y_sample", (NS, 1, D)), ("ret_prompt", (1, 1, RH, RDK, RDV)),
         ("gla_prompt", (1, 1, GH, GDK, GDV)), ("ret_sample", (1, NS, RH, RDK, RDV)),
         ("gla_sample", (1, NS, GH, GDK, GDV))]


def kernel(**inputs):
    import concourse.bacc as bacc
    from concourse.bass_utils import run_bass_kernel_spmd

    nc = bacc.Bacc("TRN2", target_bir_lowering=False, num_devices=1)
    arrays, inp, out = {}, {}, {}
    for name in _INS + ["tables"]:
        a = np.ascontiguousarray(tables() if name == "tables" else inputs[name])
        arrays[f"in_{name}"] = a
        inp[name] = nc.dram_tensor(f"in_{name}", a.shape, mybir.dt.from_np(a.dtype), kind="ExternalInput").ap()
    for name, shape in _OUTS:
        out[name] = nc.dram_tensor(f"out_{name}", shape, F32, kind="ExternalOutput").ap()
    build(nc, inp, out)
    r = run_bass_kernel_spmd(nc, [arrays], core_ids=[0])
    return tuple(r.results[0][f"out_{name}"] for name, _ in _OUTS)
```

```python
import concourse.bass as bass
import numpy as np
from concourse import mybir
from contextlib import ExitStack

F32 = mybir.dt.float32
BF16 = mybir.dt.bfloat16
I32 = mybir.dt.int32
ALU = mybir.AluOpType
ACT = mybir.ActivationFunctionType
AX = mybir.AxisListType

P = 128
D = 1024
DC = D // P
TP = 256
NS = 8
T = TP + NS
NCOND = 1 + NS
DEPTH = 2
PAST = 2048
EPS = 1e-6

RH, RDK, RDV = 4, 256, 512
GH, GDK, GDV = 4, 128, 256
RANK = 16
TAU = 16.0

NE, TOPK, NG, TOPG = 64, 8, 8, 4
DE = D // 4
FC = DE // P
SCALE = 2.5
CAP = 64
XB = (T * TOPK) // (CAP + 1)
XBP = XB + 1
TT = 3
TOKENS = [(0, P), (P, P), (TP, NS)]

RING = 12
SLOT = 2048
EPI = 4
ROUNDS = NE // EPI

TAB = {}
_at = 0
for _name, _w in (("cos", T), ("sin", T), ("decay", RH * TP), ("kdec", 2 * RH), ("causal", P), ("ident", P),
                  ("before", P), ("ones", P), ("own", 6), ("gtri", NG * NG), ("iota", NE), ("valid", TT), ("zero", 1),
                  ("one", 1)):
    TAB[_name] = (_at, _at + _w)
    _at += _w
TABW = _at


def tables():
    t = np.zeros((P, TABW), np.float32)

    def put(name, a):
        a0, a1 = TAB[name]
        t[:, a0:a1] = np.asarray(a, np.float32).reshape(P, a1 - a0)

    half = RDK // 2
    inv = (np.float32(10000.0) ** (-np.arange(half, dtype=np.float32) / np.float32(half))).astype(np.float32)
    pos = np.concatenate([np.arange(TP), np.full(NS, PAST)]).astype(np.float32)
    ang = inv[:, None] * pos[None, :]
    put("cos", np.cos(ang.astype(np.float64)))
    put("sin", np.sin(ang.astype(np.float64)))
    lg = np.log1p(-np.power(2.0, -5.0 - np.arange(RH)))
    i, j = np.arange(TP)[None, :], np.arange(P)[:, None]
    put("decay", np.stack([np.where(i >= j, np.exp(lg[h] * (i - j)), 0.0) for h in range(RH)], 1))
    jj = np.arange(TP).reshape(2, P).T
    put("kdec", np.stack([np.exp(lg[h] * (TP - 1 - jj)) for h in range(RH)], 2))
    q, r = np.arange(P)[:, None], np.arange(P)[None, :]
    put("causal", q <= r)
    put("ident", q == r)
    put("before", q < r)
    put("ones", np.ones((P, P)))
    put("own", np.arange(6)[None, :] // 3 == np.arange(P)[:, None] // CAP)
    g = np.arange(NG)
    put("gtri", np.tile((g[None, :] < g[:, None]).reshape(1, -1), (P, 1)))
    put("iota", np.tile(np.arange(NE)[None], (P, 1)))
    put("valid", np.stack([np.arange(P) < n for _, n in TOKENS], 1))
    put("one", np.ones((P, 1)))
    return t


GAMMA = [float(1.0 - 2.0 ** (-5.0 - h)) for h in range(RH)]


class Chain:

    def __init__(self, sem):
        self.sem, self.n = sem, 0

    def link(self, eng, ins):
        self.n += 1
        ins.then_inc(self.sem, 1)
        eng.wait_ge(self.sem, self.n)


class Core:
    pass


def build(nc, inp, out, dbg=None):
    ctx = ExitStack()
    with ctx:
        k = Core()
        k.nc, k.inp, k.out = nc, inp, out

        def sb(name, cols, dt=F32, parts=P):
            return ctx.enter_context(nc.sbuf_tensor(name, [parts, cols], dt))

        k.persistent = [nc.alloc_semaphore(name=n) for n in
                        [f"ring_full{s}" for s in range(RING)] + [f"ring_free{s}" for s in range(RING)]
                        + ["vector_step"]]
        k.stored = {n: nc.alloc_semaphore(name=n) for n in
                    ["ret_state_stored"] + [f"ret_sample_state_stored{b}" for b in range(8)]
                    + ["gla_state_stored"] + [f"gla_sample_state_stored{b}" for b in range(2)]}
        k.mine = []
        k.sem = lambda name: k.mine.append(nc.alloc_semaphore(name=name)) or k.mine[-1]
        k.ring = sb("ring", RING * SLOT)
        k.tab = sb("tab", TABW)
        k.x = sb("xT", DC * T)[:, :].rearrange("p (c t) -> p c t", c=DC)
        k.h = sb("hT", DC * T)[:, :].rearrange("p (c t) -> p c t", c=DC)
        k.mod = sb("mod", DEPTH * 48 * NCOND)[:, :].rearrange("p (l g c s) -> p l g c s", l=DEPTH, g=6, c=DC)
        k.gain = sb("gain", DEPTH * 2 * DC * NCOND)[:, :].rearrange("p (l n c s) -> p l n c s", l=DEPTH, n=2, c=DC)
        k.vec = sb("vec", 164)
        k.rstd = sb("rstd", RH * T)
        k.size = 19700
        k.scratch = sb("scratch", k.size)
        k.ident16 = sb("ident16", P, BF16)
        k.ps = ctx.enter_context(nc.psum_tensor("ps", [P, 8, 512], F32))

        k.const = lambda name: k.tab[:, TAB[name][0]:TAB[name][1]]
        k.ident = k.const("ident")
        k.ones = k.const("ones")
        k.ada_b = k.vec[:, 0:96].rearrange("p (l g c) -> p l g c", l=DEPTH, g=6)
        k.norm_g = k.vec[:, 96:128].rearrange("p (n l c) -> p l n c", n=2, l=DEPTH)
        k.ret_g = k.vec[:, 128:144]
        k.gla_g = k.vec[:, 144:152]
        k.fin_g = k.vec[:, 152:160]
        k.b_a = k.vec[:, 160:164]

        k.ring_full, k.ring_free = k.persistent[0:RING], k.persistent[RING:2 * RING]
        k.plan, k.issued = plan_loads(inp), 0
        k.stage = {}
        for n, (what, _) in enumerate(k.plan):
            k.stage.setdefault(what, n)
        k.dve = Chain(k.persistent[2 * RING])

        setup(k)
        if dbg != "setup":
            conditioning(k)
        if dbg not in ("setup", "ada"):
            norm(k, 0, 0, "retention_in")
            retention(k)
            if dbg != "ret":
                norm(k, 0, 1, "moe0")
                experts(k, 0)
                reuse_semaphores(k)
                if dbg != "moe0":
                    norm(k, 1, 0, "gla_in")
                    gla(k)
                    if dbg != "gla":
                        norm(k, 1, 1, "moe1")
                        experts(k, 1)
                        final(k)
        if dbg:
            dump(k)


def reuse_semaphores(k):
    nc = k.nc
    with nc.Block() as block:
        @block.gpsimd
        def _(pool):
            for s in k.mine:
                pool.sem_clear(s)
    for s in k.mine:
        nc.release_semaphore(s)
    k.mine.clear()


def dump(k):
    nc, s = k.nc, k.sem("dumped")
    with nc.Block() as block:
        @block.sync
        def _(sp):
            sp.dma_start(k.out["dbg_x"], k.x.rearrange("p c t -> p (c t)")).then_inc(s, 16)
            sp.dma_start(k.out["dbg_h"], k.h.rearrange("p c t -> p (c t)")).then_inc(s, 16)
            sp.dma_start(k.out["dbg_mod"], k.mod.rearrange("p l g c s -> p (l g c s)")).then_inc(s, 16)
            sp.wait_ge(s, 48)



def plan_loads(inp):
    plan = []

    def columns(what, w, width):
        kc, n = w.shape[0] // P, w.shape[1] // width
        for j in range(n):
            plan.append((what, w[:, j * width:(j + 1) * width].rearrange("(k p) n -> p k n", k=kc)))

    def moe(layer):
        what = f"shared{layer}"
        for name in ("sh_w_gate", "sh_w_up", "sh_w_down"):
            w = inp[name][layer]
            plan.append((what, w.rearrange("(k p) n -> p k n", p=P)))
        for r in range(ROUNDS):
            for name, e in ROUND:
                plan.append((f"moe{layer}", inp[name][layer][r * EPI + e].rearrange("(k p) n -> p k n", p=P)))

    for layer in range(DEPTH):
        columns("ada", inp["ada_w"][layer], 256)
    columns("ret_in", inp["ret_w_in"][0], 256)
    columns("ret_out", inp["ret_w_out"][0], 128)
    moe(0)
    columns("gla_in", inp["gla_w_in"][0], 256)
    columns("gla_out", inp["gla_w_out"][0], 256)
    moe(1)
    return plan


ROUND = [(n, e) for e in range(EPI) for n in ("moe_w_gate", "moe_w_up")] + [("moe_w_down", e) for e in range(EPI)]
PLACE = {ne: i for i, ne in enumerate(ROUND)}


def slot(k, n, inner):
    s = n % RING
    return k.ring[:, s * SLOT:(s + 1) * SLOT].rearrange("p (k n) -> p k n", n=inner)


def load_until(k, sp, last):
    while k.issued < min(last, len(k.plan)):
        n = k.issued
        src = k.plan[n][1]
        if n >= RING:
            sp.wait_ge(k.ring_free[n % RING], n // RING)
        sp.dma_start(slot(k, n, src.shape[2]), src).then_inc(k.ring_full[n % RING], 16)
        k.issued += 1


def wait_slot(k, pe, n):
    pe.wait_ge(k.ring_full[n % RING], 16 * (n // RING + 1))


def wait_used(k, eng, n):
    eng.wait_ge(k.ring_free[n % RING], n // RING + 1)



def setup(k):
    nc, inp = k.nc, k.inp
    s_tab, s_in, s_cond = k.sem("tables_loaded"), k.sem("inputs_loaded"), k.sem("cond_loaded")
    s_silu, s_tr, s_cp = k.sem("cond_silu"), k.sem("inputs_transposed"), k.sem("transposed_copied")
    sc = k.scratch
    xn = sc[:, 0:TT * D].rearrange("p (t d) -> p t d", t=TT)
    vn = sc[:, 3072:3072 + 2 * P].rearrange("p (t d) -> p t d", t=2)
    cn = sc[0:NCOND, 3400:3400 + D]
    k.condT = sc[:, 5000:5000 + DC * 32].rearrange("p (c s) -> p c s", c=DC)
    with nc.Block() as block:
        @block.sync
        def _(sp):
            sp.dma_start(k.tab[:, :], inp["tables"]).then_inc(s_tab, 16)
            sp.dma_start(cn[0:1, :], inp["c_prompt"]).then_inc(s_cond, 16)
            sp.dma_start(cn[1:NCOND, :], inp["c_sample"]).then_inc(s_cond, 16)
            for t, (t0, n) in enumerate(TOKENS):
                src = inp["x_prompt"][0, t0:t0 + n] if t < 2 else inp["x_sample"].rearrange("b o d -> (b o) d")
                sp.dma_start(xn[0:n, t, :], src).then_inc(s_in, 16)
            at = 0
            for name, rows in (("ada_b", 96), ("norm_mix_g", 16), ("norm_ffn_g", 16), ("ret_norm_g", 16),
                               ("gla_norm_g", 8), ("final_norm_g", 8), ("gla_b_a", 4)):
                src = inp[name]
                src = (src.rearrange("(r p) -> r p", p=P) if len(src.shape) == 1
                       else src.rearrange("l (r p) -> (l r) p", p=P))
                sp.dma_start(vn[at % P:at % P + rows, at // P, :], src).then_inc(s_in, 16)
                at += rows
            load_until(k, sp, RING)

        @block.scalar
        def _(act):
            act.wait_ge(s_cond, 32)
            nc.scalar.activation(cn, cn, ACT.Silu).then_inc(s_silu, 1)

        @block.tensor
        def _(pe):
            pe.wait_ge(s_tab, 16)
            pe.wait_ge(s_silu, 1)
            for c in range(DC):
                mm = nc.tensor.transpose(k.ps[:, 0, c * NCOND:(c + 1) * NCOND], cn[:, c * P:(c + 1) * P],
                                         k.ident[0:NCOND, 0:NCOND])
            mm.then_inc(s_tr, 1)
            pe.wait_ge(s_in, 16 * 10)
            for t, rows in ((0, 128), (1, 36)):
                mm = nc.tensor.transpose(k.ps[:, 1, t * P:t * P + rows], vn[0:rows, t, :], k.ident[0:rows, 0:rows])
            mm.then_inc(s_tr, 1)
            for c in range(DC):
                if c >= 2:
                    pe.wait_ge(s_cp, c - 2 + 1 + 2)
                for t, (t0, n) in enumerate(TOKENS):
                    mm = nc.tensor.transpose(k.ps[:, 2 + c % 2, t0:t0 + n], xn[0:n, t, c * P:(c + 1) * P],
                                             k.ident[0:n, 0:n])
                mm.then_inc(s_tr, 1)

        @block.vector
        def _(v):
            k.dve.link(v, nc.vector.memset(k.condT, 0.0))
            v.wait_ge(s_tab, 16)
            nc.vector.tensor_copy(k.ident16[:, :], k.ident)
            v.wait_ge(s_tr, 1)
            nc.vector.tensor_copy(k.condT[:, :, 0:NCOND], k.ps[:, 0, 0:DC * NCOND].rearrange("p (c s) -> p c s", c=DC))\
                .then_inc(s_cp, 1)
            v.wait_ge(s_tr, 2)
            nc.vector.tensor_copy(k.vec[:, :], k.ps[:, 1, 0:164]).then_inc(s_cp, 1)
            for c in range(DC):
                v.wait_ge(s_tr, 3 + c)
                nc.vector.tensor_copy(k.x[:, c, :], k.ps[:, 2 + c % 2, 0:T]).then_inc(s_cp, 1)



def conditioning(k):
    nc = k.nc
    n0, rounds, groups = k.stage["ada"], 4, RING // 4
    s_mod, s_row, s_tr, s_out = (k.sem(f"mod_{n}") for n in ("products", "rows_out", "transposed", "out"))
    rows = k.scratch[:, 6000:6000 + groups * 256].rearrange("p (g n) -> p g n", g=groups)
    mod = k.mod.rearrange("p l g c s -> p (l g c) s")
    with nc.Block() as block:
        @block.sync
        def _(sp):
            load_until(k, sp, n0 + RING * rounds + RING)

        @block.tensor
        def _(pe):
            with pe.Fori(0, rounds) as r:
                for g in range(groups):
                    for j in range(4):
                        pe.wait_ge(k.ring_full[4 * g + j], r * 16 + 16)
                    pe.wait_ge(s_row, r * groups + g + 1)
                    for c in range(DC):
                        for j in range(4):
                            mm = nc.tensor.matmul(k.ps[32 * j:32 * j + 32, g, 0:256], k.condT[:, c, :],
                                                  slot(k, 4 * g + j, 256)[:, c, :], start=(c == 0),
                                                  stop=(c == DC - 1))
                            if c == DC - 1:
                                mm.then_inc(k.ring_free[4 * g + j], 1)
                    pe.wait_ge(s_row, r * groups + g + 1 + groups)
                    pe.wait_ge(s_out, r * groups + g + 1)
                    for m in range(2):
                        mm = nc.tensor.transpose(k.ps[:, 3 + g, m * P:(m + 1) * P], rows[:, g, m * P:(m + 1) * P],
                                                 k.ident)
                    mm.then_inc(s_tr, 1)

        @block.scalar
        def _(act):
            act.sem_inc(s_row, groups)
            with act.Fori(0, rounds) as r:
                for g in range(groups):
                    for j in range(4):
                        act.wait_ge(k.ring_free[4 * g + j], r + 1)
                    nc.scalar.copy(rows[:, g], k.ps[:, g, 0:256]).then_inc(s_row, 1)

        @block.vector
        def _(v):
            v.sem_inc(s_out, groups)
            with v.Fori(0, rounds) as r:
                for g in range(groups):
                    v.wait_ge(s_tr, r * groups + g + 1)
                    to = bass.ds(r * 24 + g * 8, 8)
                    src = k.ps[:, 3 + g, 0:256].rearrange("p (m j s) -> p j m s", m=2, j=4)[:, :, :, 0:NCOND]
                    nc.vector.tensor_tensor(mod[:, to, :].rearrange("p (j m) s -> p j m s", m=2), src,
                                            k.vec[:, to].rearrange("p (j m) -> p j m", m=2).unsqueeze(3)
                                            .to_broadcast([P, 4, 2, NCOND]), ALU.add).then_inc(s_out, 1)
            v.wait_ge(s_out, groups * rounds + groups)
            for layer in range(DEPTH):
                for n in range(2):
                    g = k.norm_g[:, layer, n, :].unsqueeze(2).to_broadcast([P, DC, NCOND])
                    ins = nc.vector.scalar_tensor_tensor(k.gain[:, layer, n], k.mod[:, layer, 3 * n + 1], 1.0, g,
                                                         ALU.add, ALU.mult)
            k.dve.link(v, ins)



def norm(k, layer, which, then):
    nc = k.nc
    tag = f"{layer}{which}"
    s_sq, s_sum, s_ms, s_rt = (k.sem(f"norm{tag}_{n}") for n in ("squared", "summed", "meansq", "root"))
    s_prod = k.sem(f"norm{tag}_scaled")
    sq = k.scratch[:, 0:DC * T].rearrange("p (c t) -> p c t", c=DC)
    tmp = k.scratch[:, DC * T:DC * T + T]
    root = k.scratch[:, DC * T + T:DC * T + 2 * T]
    rstd = k.rstd[:, 0:T]
    final_norm = layer == DEPTH

    with nc.Block() as block:
        @block.scalar
        def _(act):
            for c in range(DC):
                nc.scalar.activation(sq[:, c, :], k.x[:, c, :], ACT.Square).then_inc(s_sq, 1)
            act.wait_ge(s_ms, 1)
            nc.scalar.activation(root, tmp, ACT.Sqrt).then_inc(s_rt, 1)
            if not final_norm:
                for c in range(DC):
                    act.wait_ge(s_prod, c + 1)
                    nc.scalar.activation(k.h[:, c, 0:TP], k.h[:, c, 0:TP], ACT.Identity,
                                         bias=k.mod[:, layer, 3 * which, c, 0:1])

        @block.tensor
        def _(pe):
            for c in range(DC):
                pe.wait_ge(s_sq, c + 1)
                mm = nc.tensor.matmul(k.ps[:, 0, 0:T], k.ones, sq[:, c, :], start=(c == 0), stop=(c == DC - 1))
            mm.then_inc(s_sum, 1)

        @block.vector
        def _(v):
            v.wait_ge(s_sum, 1)
            nc.vector.tensor_scalar(tmp, k.ps[:, 0, 0:T], 1.0 / D, EPS, ALU.mult, ALU.add).then_inc(s_ms, 1)
            v.wait_ge(s_rt, 1)
            k.dve.link(v, nc.vector.reciprocal(rstd, root))
            if final_norm:
                for c in range(DC):
                    nc.vector.scalar_tensor_tensor(k.h[:, c, :], k.x[:, c, :], k.fin_g[:, c:c + 1], rstd,
                                                   ALU.mult, ALU.mult)
                return
            for c in range(DC):
                nc.vector.scalar_tensor_tensor(k.h[:, c, 0:TP], k.x[:, c, 0:TP], k.gain[:, layer, which, c, 0:1],
                                               rstd[:, 0:TP], ALU.mult, ALU.mult).then_inc(s_prod, 1)
            hs = k.h[:, :, TP:T]
            rs = rstd[:, TP:T].unsqueeze(1).to_broadcast([P, DC, NS])
            k.dve.link(v, nc.vector.tensor_tensor(hs, k.x[:, :, TP:T], rs, ALU.mult))
            k.dve.link(v, nc.vector.tensor_tensor(hs, hs, k.gain[:, layer, which, :, 1:NCOND], ALU.mult))
            nc.vector.tensor_tensor(hs, hs, k.mod[:, layer, 3 * which, :, 1:NCOND], ALU.add)


def add_gated(k, v, chunk, psum, gate, tmp):
    nc = k.nc
    nc.vector.scalar_tensor_tensor(k.x[:, chunk, 0:TP], psum[:, 0:TP], gate[:, chunk, 0:1], k.x[:, chunk, 0:TP],
                                   ALU.mult, ALU.add)
    k.dve.link(v, nc.vector.tensor_tensor(tmp, psum[:, TP:T], gate[:, chunk, 1:NCOND], ALU.mult))
    return nc.vector.tensor_tensor(k.x[:, chunk, TP:T], tmp, k.x[:, chunk, TP:T], ALU.add)



def retention(k):
    nc, inp, out = k.nc, k.inp, k.out
    sc = k.scratch
    at = [0]

    def area(cols):
        at[0] += cols
        assert at[0] <= k.size
        return sc[:, at[0] - cols:at[0]]

    vo = area(16 * T).rearrange("p (c t) -> p c t", c=16)
    vs = area(2048)[0:NS, :]
    qs = area(DC * NS).rearrange("p (c s) -> p c s", c=DC)
    ks = area(DC * NS).rearrange("p (c s) -> p c s", c=DC)
    here = at[0]
    q = area(DC * T).rearrange("p (c t) -> p c t", c=DC)
    kk = area(DC * T).rearrange("p (c t) -> p c t", c=DC)
    vn = area(2 * 1024).rearrange("p (b j n) -> p b j n", b=2, j=2)
    kn = area(2 * 512).rearrange("p (b j n) -> p b j n", b=2, j=2)
    att = area(384)
    sp_ = area(2 * 1024).rearrange("p (b c n) -> p b c n", b=2, c=2)
    tmp = area(4 * T).rearrange("p (b t) -> p b t", b=4)
    at[0] = here
    gate = area(16 * T).rearrange("p (c t) -> p c t", c=16)
    st = area(8 * 1024).rearrange("p (b c n) -> p b c n", b=8, c=2)
    qz = area(DC * NS * NS)
    n_in, n_out = k.stage["ret_in"], k.stage["ret_out"]
    cos, sin = k.const("cos"), k.const("sin")

    s_rot, s_vc = k.sem("ret_rotated"), k.sem("ret_values_copied")
    with nc.Block() as block:
        @block.sync
        def _(sp):
            load_until(k, sp, n_in + 16 + RING)

        @block.tensor
        def _(pe):
            for t in range(16):
                wait_slot(k, pe, n_in + t)
                if 2 <= t < 10:
                    pe.wait_ge(s_rot, t - 1)
                elif t >= 10:
                    pe.wait_ge(s_vc, t - 9)
                w = slot(k, n_in + t, 256)
                for m in range(2):
                    for c in range(DC):
                        mm = nc.tensor.matmul(k.ps[:, 2 * (t % 2) + m, 0:T], w[:, c, m * P:(m + 1) * P], k.h[:, c, :],
                                              start=(c == 0), stop=(c == DC - 1))
                mm.then_inc(k.ring_free[(n_in + t) % RING], 1)

        @block.vector
        def _(v):
            for t in range(8):
                wait_used(k, v, n_in + t)
                dst, scale = (q, 1.0) if t < 4 else (kk, RDK ** -0.5)
                h = t % 4
                x1, x2 = k.ps[:, 2 * (t % 2), 0:T], k.ps[:, 2 * (t % 2) + 1, 0:T]
                for j, (a, b) in enumerate(((x1, cos), (x2, sin), (x1, sin), (x2, cos))):
                    ins = nc.vector.scalar_tensor_tensor(tmp[:, j], a, scale, b, ALU.mult, ALU.mult)
                ins.then_inc(s_rot, 1)
                v.wait_ge(s_rot, t + 1)
                nc.vector.tensor_tensor(dst[:, 2 * h], tmp[:, 0], tmp[:, 1], ALU.subtract)
                k.dve.link(v, nc.vector.tensor_tensor(dst[:, 2 * h + 1], tmp[:, 2], tmp[:, 3], ALU.add))

        @block.scalar
        def _(act):
            for t in range(8, 16):
                wait_used(k, act, n_in + t)
                for m in range(2):
                    ins = nc.scalar.copy(vo[:, 2 * (t - 8) + m], k.ps[:, 2 * (t % 2) + m, 0:T])
                ins.then_inc(s_vc, 1)

    tr, trs, s_at, s_o, s_st = (k.sem(f"ret_{n}") for n in ("tokens_first", "keys_first", "scores", "heads", "state"))
    c_v, c_k, c_at, c_o, c_st = (k.sem(f"ret_{n}") for n in (
        "values_out", "keys_out", "scores_out", "heads_out", "state_out"))
    c_out = k.stored["ret_state_stored"]
    with nc.Block() as block:
        @block.tensor
        def _(pe):
            for h in range(RH):
                b = h % 2
                if h:
                    pe.wait_ge(c_v, h)
                for j in range(2):
                    for c in range(4):
                        mm = nc.tensor.transpose(k.ps[:, j, c * P:(c + 1) * P], vo[:, 4 * h + c, j * P:(j + 1) * P],
                                                 k.ident)
                for c in range(4):
                    mm = nc.tensor.transpose(k.ps[0:NS, 3, c * P:(c + 1) * P], vo[:, 4 * h + c, TP:T], k.ident)
                mm.then_inc(tr, 1)
                if h:
                    pe.wait_ge(c_k, h)
                for j in range(2):
                    for c in range(2):
                        mm = nc.tensor.transpose(k.ps[:, 2, (2 * j + c) * P:(2 * j + c + 1) * P],
                                                 kk[:, 2 * h + c, j * P:(j + 1) * P], k.ident)
                mm.then_inc(trs, 1)
                if h:
                    pe.wait_ge(c_at, h)
                for j in range(2):
                    for c in range(2):
                        mm = nc.tensor.matmul(k.ps[:, 4, j * TP:j * TP + TP - j * P],
                                              kk[:, 2 * h + c, j * P:(j + 1) * P], q[:, 2 * h + c, j * P:TP],
                                              start=(c == 0), stop=(c == 1))
                mm.then_inc(s_at, 1)
                pe.wait_ge(c_v, h + 1)
                pe.wait_ge(c_k, h + 1)
                if h:
                    pe.wait_ge(c_st, 2 * h - 1)
                for c in range(2):
                    if c:
                        pe.wait_ge(c_st, 2 * h + 1)
                    for j in range(2):
                        mm = nc.tensor.matmul(k.ps[:, 7, :], kn[:, b, j, c * P:(c + 1) * P], vn[:, b, j, :],
                                              start=(j == 0), stop=(j == 1))
                    mm.then_inc(s_st, 1)
                    if c == 0:
                        pe.wait_ge(c_at, h + 1)
                        if h:
                            pe.wait_ge(c_o, h)
                        for cc in range(4):
                            o = k.ps[:, 5 + cc // 2, (cc % 2) * TP:(cc % 2 + 1) * TP]
                            nc.tensor.matmul(o, vn[:, b, 0, cc * P:(cc + 1) * P], att[:, 0:TP], start=True, stop=False)
                            mm = nc.tensor.matmul(o[:, P:TP], vn[:, b, 1, cc * P:(cc + 1) * P], att[:, TP:TP + P],
                                                  start=False, stop=True)
                        mm.then_inc(s_o, 1)

        @block.scalar
        def _(act):
            for h in range(RH):
                act.wait_ge(tr, h + 1)
                if h >= 2:
                    act.wait_ge(s_st, 2 * h - 2)
                for j in range(2):
                    nc.scalar.copy(vn[:, h % 2, j, :], k.ps[:, j, :])
                nc.scalar.copy(vs[:, h * RDV:(h + 1) * RDV], k.ps[0:NS, 3, :]).then_inc(c_v, 1)
                act.wait_ge(s_o, h + 1)
                for c in range(2):
                    ins = nc.scalar.copy(vo[:, 4 * h + 2 * c:4 * h + 2 * c + 2, 0:TP],
                                         k.ps[:, 5 + c, :].rearrange("p (c t) -> p c t", c=2))
                ins.then_inc(c_o, 1)

        @block.vector
        def _(v):
            nc.vector.tensor_copy(qs, q[:, :, TP:T])
            nc.vector.tensor_copy(ks, kk[:, :, TP:T])
            for h in range(RH):
                v.wait_ge(trs, h + 1)
                if h >= 2:
                    v.wait_ge(s_st, 2 * h - 2)
                for j in range(2):
                    ins = nc.vector.tensor_scalar(kn[:, h % 2, j, :], k.ps[:, 2, j * TP:(j + 1) * TP],
                                                  k.const("kdec")[:, j * RH + h:j * RH + h + 1], None, ALU.mult)
                ins.then_inc(c_k, 1)
                v.wait_ge(s_at, h + 1)
                if h:
                    v.wait_ge(s_o, h)
                dec = k.const("decay")[:, h * TP:(h + 1) * TP]
                nc.vector.tensor_tensor(att[:, 0:TP], k.ps[:, 4, 0:TP], dec, ALU.mult)
                nc.vector.tensor_tensor(att[:, TP:TP + P], k.ps[:, 4, TP:TP + P], dec[:, 0:P],
                                        ALU.mult).then_inc(c_at, 1)
                for c in range(2):
                    v.wait_ge(s_st, 2 * h + c + 1)
                    if h >= 2 and c == 0:
                        v.wait_ge(c_out, 16 * (h - 1))
                    nc.vector.tensor_copy(sp_[:, h % 2, c, :], k.ps[:, 7, :]).then_inc(c_st, 1)

        @block.gpsimd
        def _(pool):
            for h in range(RH):
                pool.wait_ge(c_st, 2 * h + 2)
                pool.dma_start(out["ret_prompt"][0, 0, h].rearrange("(c p) n -> p c n", p=P),
                               sp_[:, h % 2]).then_inc(c_out, 16)
                pool.wait_ge(c_out, 16 * (h + 1))

    s_bc, s_out, s_new, s_q, s_sil, s_cm, s_or, s_ot = (k.sem(f"ret_sample_{n}") for n in (
        "values_spread", "outer", "state_new", "read", "gate_silu", "compacted", "rows_out", "rows_transposed"))
    s_ldb = [k.sem(f"ret_sample_state_loaded{b}") for b in range(8)]
    s_stb = [k.stored[f"ret_sample_state_stored{b}"] for b in range(8)]
    units = [(b, h) for b in range(NS) for h in range(RH)]
    n_gate = n_in + 16
    outer = k.rstd[:, 0:1024].rearrange("p (b n) -> p b n", b=2)
    orow = k.rstd[:, 0:512]
    qz4 = qz.rearrange("p (c b s) -> p c b s", c=DC, b=NS)
    with nc.Block() as block:
        @block.sync
        def _(sp):
            for u, (b, h) in enumerate(units):
                if u >= 8:
                    sp.wait_ge(s_stb[u % 8], 16 * (u // 8))
                    sp.wait_ge(s_q, (u - 8) // RH + 1)
                sp.dma_start(st[:, u % 8], inp["state_ret"][0, b, h].rearrange("(c p) n -> p c n", p=P))\
                    .then_inc(s_ldb[u % 8], 16)
                if u % 4 == 3 and u >= 7:
                    load_until(k, sp, n_gate + (u - 7) // 4 + RING)

        @block.gpsimd
        def _(pool):
            for u, (b, h) in enumerate(units):
                pool.wait_ge(s_new, 2 * u + 2)
                pool.dma_start(out["ret_sample"][0, b, h].rearrange("(c p) n -> p c n", p=P), st[:, u % 8])\
                    .then_inc(s_stb[u % 8], 16)
            for b in range(8):
                pool.wait_ge(s_stb[b], 16 * len(units) // 8)

        @block.tensor
        def _(pe):
            def read(b):
                for h in range(RH):
                    pe.wait_ge(s_new, 2 * (RH * b + h) + 2)
                for c in range(2):
                    for h in range(RH):
                        mm = nc.tensor.matmul(k.ps[32 * h:32 * h + NS, 2, :], qz4[:, 2 * h + c, b, :],
                                              st[:, (RH * b + h) % 8, c, :], start=(b == 0 and c == 0),
                                              stop=(b == NS - 1 and c == 1))
                mm.then_inc(s_q, 1)

            for u, (b, h) in enumerate(units):
                if u >= 2:
                    pe.wait_ge(s_out, 2 * (u - 1))
                nc.tensor.matmul(k.ps[:, u % 2, :], k.ident[0:NS, b:b + 1].to_broadcast([NS, P]),
                                 vs[:, h * RDV:(h + 1) * RDV], start=True, stop=True).then_inc(s_bc, 1)
                if u % 2:
                    n = u // 2
                    if n % 2 == 0:
                        wait_slot(k, pe, n_gate + n // 2)
                    if n >= 4:
                        pe.wait_ge(s_sil, n - 3)
                    w = slot(k, n_gate + n // 2, 256)
                    for c in range(DC):
                        mm = nc.tensor.matmul(k.ps[:, 4 + n % 4, 0:T], w[:, c, (n % 2) * P:(n % 2 + 1) * P],
                                              k.h[:, c, :], start=(c == 0), stop=(c == DC - 1))
                    if n % 2:
                        mm.then_inc(k.ring_free[(n_gate + n // 2) % RING], 1)
                if b and h == 1:
                    if b == 1:
                        pe.wait_ge(s_cm, 2)
                    read(b - 1)
            read(NS - 1)
            pe.wait_ge(s_or, RH)
            for c in range(4):
                mm = nc.tensor.transpose(k.ps[:, 3, c * P:(c + 1) * P], orow[:, c * P:(c + 1) * P], k.ident)
            mm.then_inc(s_ot, 1)

        @block.scalar
        def _(act):
            for u, (b, h) in enumerate(units):
                act.wait_ge(s_bc, u + 1)
                for c in range(2):
                    if u >= 1:
                        act.wait_ge(s_new, 2 * (u - 1) + c + 1)
                    nc.scalar.activation(outer[:, c, :], k.ps[:, u % 2, :], ACT.Copy,
                                         scale=ks[:, 2 * h + c, b:b + 1]).then_inc(s_out, 1)
                if u % 4 == 3:
                    wait_used(k, act, n_gate + u // 4)
                    for n in (u // 2 - 1, u // 2):
                        nc.scalar.activation(gate[:, n], k.ps[:, 4 + n % 4, 0:T], ACT.Silu).then_inc(s_sil, 1)

        @block.vector
        def _(v):
            nc.vector.memset(qz, 0.0).then_inc(s_cm, 1)
            v.wait_ge(s_cm, 1)
            diagonal = qz.rearrange("p (c n) -> p c n", c=DC)[:, :, 0:NS * NS:NS + 1]
            nc.vector.tensor_copy(diagonal, qs).then_inc(s_cm, 1)
            for u, (b, h) in enumerate(units):
                v.wait_ge(s_ldb[u % 8], 16 * (u // 8 + 1))
                for c in range(2):
                    v.wait_ge(s_out, 2 * u + c + 1)
                    nc.vector.scalar_tensor_tensor(st[:, u % 8, c, :], st[:, u % 8, c, :], GAMMA[h], outer[:, c, :],
                                                   ALU.mult, ALU.add).then_inc(s_new, 1)
            v.wait_ge(s_new, 2 * len(units))
            k.dve.link(v, nc.vector.memset(orow, 0.0))
            v.wait_ge(s_q, NS)
            for h in range(RH):
                nc.vector.tensor_copy(orow[32 * h:32 * h + NS, :], k.ps[32 * h:32 * h + NS, 2, :]).then_inc(s_or, 1)
            v.wait_ge(s_ot, 1)
            for h in range(RH):
                nc.vector.tensor_copy(vo[:, 4 * h:4 * h + 4, TP:T],
                                      k.ps[:, 3, :].rearrange("p (c n) -> p c n", c=4)[:, :, 32 * h:32 * h + NS])

    head_norm(k, "ret", vo, 4, RH, k.ret_g, gate, center=True)
    project_out(k, "ret", vo, n_out, 128, 16, 0)


def head_norm(k, tag, o, per, heads, gain, gate, center):
    nc = k.nc
    width = per * P
    s_mu, s_cen, s_sq, s_ss, s_ms, s_rt, s_sc = (k.sem(f"{tag}_norm_{n}") for n in (
        "sums", "centered", "squared", "square_sums", "meansq", "root", "scaled"))
    root = k.scratch[:, k.size - 2 * heads * T:k.size].rearrange("p (b h t) -> p b h t", b=2, h=heads)
    squares = k.scratch[:, k.size - 2 * heads * T - 2 * T:k.size - 2 * heads * T].rearrange("p (b t) -> p b t", b=2)
    rstd = k.rstd[:, 0:heads * T].rearrange("p (h t) -> p h t", h=heads)
    with nc.Block() as block:
        @block.tensor
        def _(pe):
            if center:
                for h in range(heads):
                    for c in range(per):
                        mm = nc.tensor.matmul(k.ps[:, h, 0:T], k.ones, o[:, per * h + c, :], start=(c == 0),
                                              stop=(c == per - 1))
                    mm.then_inc(s_mu, 1)
            for n in range(heads * per):
                h, c = divmod(n, per)
                pe.wait_ge(s_sq, n + 1)
                mm = nc.tensor.matmul(k.ps[:, 4 + h, 0:T], k.ones, squares[:, n % 2], start=(c == 0),
                                      stop=(c == per - 1))
                mm.then_inc(s_ss, 1)

        @block.scalar
        def _(act):
            for n in range(heads * per):
                if center:
                    act.wait_ge(s_cen, n + 1)
                if n >= 2:
                    act.wait_ge(s_ss, n - 1)
                nc.scalar.activation(squares[:, n % 2], o[:, n, :], ACT.Square).then_inc(s_sq, 1)
            act.wait_ge(s_ms, heads)
            nc.scalar.activation(root[:, 1].rearrange("p h t -> p (h t)"), root[:, 0].rearrange("p h t -> p (h t)"),
                                 ACT.Sqrt).then_inc(s_rt, 1)

        @block.vector
        def _(v):
            if center:
                for n in range(heads * per):
                    v.wait_ge(s_mu, n // per + 1)
                    nc.vector.scalar_tensor_tensor(o[:, n, :], k.ps[:, n // per, 0:T], -1.0 / width, o[:, n, :],
                                                   ALU.mult, ALU.add).then_inc(s_cen, 1)
                v.wait_ge(s_cen, heads * per)
            for h in range(heads):
                v.wait_ge(s_ss, per * (h + 1))
                nc.vector.tensor_scalar(root[:, 0, h, :], k.ps[:, 4 + h, 0:T], 1.0 / width, EPS, ALU.mult,
                                        ALU.add).then_inc(s_ms, 1)
            v.wait_ge(s_rt, 1)
            k.dve.link(v, nc.vector.reciprocal(rstd.rearrange("p h t -> p (h t)"),
                                               root[:, 1].rearrange("p h t -> p (h t)")))
            for n in range(heads * per):
                nc.vector.scalar_tensor_tensor(o[:, n, :], o[:, n, :], gain[:, n:n + 1], rstd[:, n // per, :],
                                               ALU.mult, ALU.mult).then_inc(s_sc, 1)
            for n in range(heads * per):
                v.wait_ge(s_sc, n + 1)
                nc.vector.tensor_tensor(o[:, n, :], o[:, n, :], gate[:, n, :], ALU.mult)


def project_out(k, tag, o, n_out, width, kc, layer):
    nc = k.nc
    s_add = k.sem(f"{tag}_residual_added")
    per = width // P
    outs = D // width
    small = k.scratch[:, k.size - NS:k.size]
    with nc.Block() as block:
        @block.sync
        def _(sp):
            load_until(k, sp, n_out + outs + RING)

        @block.tensor
        def _(pe):
            for t in range(outs):
                wait_slot(k, pe, n_out + t)
                w = slot(k, n_out + t, width)
                for m in range(per):
                    n = per * t + m
                    if n >= 4:
                        pe.wait_ge(s_add, n - 3)
                    for c in range(kc):
                        mm = nc.tensor.matmul(k.ps[:, 4 + n % 4, 0:T], w[:, c, m * P:(m + 1) * P], o[:, c, :],
                                              start=(c == 0), stop=(c == kc - 1))
                mm.then_inc(k.ring_free[(n_out + t) % RING], 1)

        @block.vector
        def _(v):
            for n in range(DC):
                wait_used(k, v, n_out + n // per)
                add_gated(k, v, n, k.ps[:, 4 + n % 4, :], k.mod[:, layer, 2], small).then_inc(s_add, 1)
                if n < DC - 1:
                    v.wait_ge(s_add, n + 1)



def gla(k):
    nc, inp, out = k.nc, k.inp, k.out
    sc = k.scratch
    at = [0]

    def area(cols):
        at[0] += cols
        assert at[0] <= k.size
        return sc[:, at[0] - cols:at[0]]

    q = area(GH * T).rearrange("p (c t) -> p c t", c=GH)
    kk = area(GH * T).rearrange("p (c t) -> p c t", c=GH)
    vo = area(8 * T).rearrange("p (c t) -> p c t", c=8)
    gate = sc[:, at[0]:at[0] + 8 * T].rearrange("p (c t) -> p c t", c=8)
    z = area(GH * T).rearrange("p (c t) -> p c t", c=GH)
    ez = area(GH * T).rearrange("p (c t) -> p c t", c=GH)
    az = area(GH * T).rearrange("p (c t) -> p c t", c=GH)
    alpha = area(GH * NS).rearrange("p (c t) -> p c t", c=GH)
    edge = area(GH * 2 * 3).rearrange("p (h j n) -> p h j n", h=GH, j=2)
    last_ = area(GH)
    qe = area(TP)
    ke = area(TP)
    q0 = area(P)
    kd = area(TP)
    fac = area(4 * TP).rearrange("p (b t) -> p b t", b=4)
    knat = area(TP).rearrange("p (j n) -> p j n", j=2)
    vn = area(2 * GDV).rearrange("p (j n) -> p j n", j=2)
    att = area(TP).rearrange("p (j n) -> p j n", j=2)
    s1 = area(GDV)
    s2 = area(2 * GDV).rearrange("p (b n) -> p b n", b=2)
    vs = area(GH * GDV)[0:NS, :]
    st = area(2 * GH * GDV).rearrange("p (b h n) -> p b h n", b=2, h=GH)
    outer = area(GH * GDV).rearrange("p (h n) -> p h n", h=GH)
    qz = area(GH * NS * NS)
    a1 = area(DC * RANK).rearrange("p (c r) -> p c r", c=DC)
    a2 = area(GH * GDK)[0:RANK, :]
    low = area(T)[0:RANK, :]
    n_in, n_out = k.stage["gla_in"], k.stage["gla_out"]

    s_w, s_low, s_lowc, s_z, s_zc, s_qk, s_abs, s_exp, s_ln, s_cum, s_edge, s_al = (k.sem(f"gla_{n}") for n in (
        "gate_weights", "low_rank", "low_rank_out", "logits", "logits_out", "copied", "absolute", "exp", "log",
        "cumulated", "edges", "alphas"))
    with nc.Block() as block:
        @block.sync
        def _(sp):
            sp.dma_start(a1, inp["gla_w_a1"][0].rearrange("(c p) r -> p c r", p=P)).then_inc(s_w, 16)
            sp.dma_start(a2, inp["gla_w_a2"][0]).then_inc(s_w, 16)
            load_until(k, sp, n_in + 8 + RING)

        @block.tensor
        def _(pe):
            pe.wait_ge(s_w, 32)
            for c in range(DC):
                mm = nc.tensor.matmul(k.ps[0:RANK, 4, 0:T], a1[:, c, :], k.h[:, c, :], start=(c == 0),
                                      stop=(c == DC - 1))
            mm.then_inc(s_low, 1)
            for t in range(8):
                wait_slot(k, pe, n_in + t)
                if t >= 2:
                    pe.wait_ge(s_qk, 2 * (t - 1))
                w = slot(k, n_in + t, 256)
                for m in range(2):
                    for c in range(DC):
                        mm = nc.tensor.matmul(k.ps[:, 2 * (t % 2) + m, 0:T], w[:, c, m * P:(m + 1) * P], k.h[:, c, :],
                                              start=(c == 0), stop=(c == DC - 1))
                mm.then_inc(k.ring_free[(n_in + t) % RING], 1)
                if t == 0:
                    pe.wait_ge(s_lowc, 1)
                    for h in range(GH):
                        if h >= 3:
                            pe.wait_ge(s_zc, h - 2)
                        nc.tensor.matmul(k.ps[:, 5 + h % 3, 0:T], a2[:, h * P:(h + 1) * P], low, start=True,
                                         stop=True).then_inc(s_z, 1)

        @block.scalar
        def _(act):
            act.wait_ge(s_low, 1)
            nc.scalar.copy(low, k.ps[0:RANK, 4, 0:T]).then_inc(s_lowc, 1)
            for h in range(GH):
                act.wait_ge(s_z, h + 1)
                nc.scalar.activation(z[:, h], k.ps[:, 5 + h % 3, 0:T], ACT.Identity,
                                     bias=k.b_a[:, h:h + 1]).then_inc(s_zc, 1)
            for t in range(8):
                wait_used(k, act, n_in + t)
                for m in range(2):
                    n = 2 * t + m
                    src = k.ps[:, 2 * (t % 2) + m, 0:T]
                    if t < 2:
                        ins = nc.scalar.activation(q[:, n], src, ACT.Copy, scale=GDK ** -0.5)
                    elif t < 4:
                        ins = nc.scalar.copy(kk[:, n - 4], src)
                    else:
                        ins = nc.scalar.copy(vo[:, n - 8], src)
                    ins.then_inc(s_qk, 1)
                if t == 1:
                    act.wait_ge(s_abs, 1)
                    flat = lambda a: a.rearrange("p c t -> p (c t)")
                    nc.scalar.activation(flat(ez), flat(az), ACT.Exp, scale=-1.0).then_inc(s_exp, 1)
                    act.wait_ge(s_exp, 1)
                    nc.scalar.activation(flat(az), flat(ez), ACT.Ln, bias=1.0).then_inc(s_ln, 1)
            act.wait_ge(s_cum, 1)
            nc.scalar.activation(alpha, z[:, :, TP:T], ACT.Exp, scale=1.0 / TAU)
            act.wait_ge(s_edge, 1)
            nc.scalar.activation(last_, edge[:, :, 1, 2], ACT.Exp)

        @block.vector
        def _(v):
            link = lambda ins: k.dve.link(v, ins)
            v.wait_ge(s_zc, GH)
            flat = lambda a: a.rearrange("p c t -> p (c t)")
            nc.vector.scalar_tensor_tensor(flat(az), flat(z), -1.0, flat(z), ALU.mult, ALU.max).then_inc(s_abs, 1)
            v.wait_ge(s_ln, 1)
            link(nc.vector.scalar_tensor_tensor(flat(ez), flat(z), 0.0, flat(az), ALU.min, ALU.subtract))
            for h in range(GH):
                for j in range(2):
                    nc.vector.tensor_tensor_scan(z[:, h, j * P:(j + 1) * P], k.ones, ez[:, h, j * P:(j + 1) * P], 0.0,
                                                 ALU.mult, ALU.add)
            nc.vector.tensor_copy(z[:, :, TP:T], ez[:, :, TP:T]).then_inc(s_cum, 1)
            v.wait_ge(s_cum, 1)
            zj = z[:, :, 0:TP].rearrange("p h (j t) -> p h j t", j=2)
            nc.vector.tensor_scalar(edge[:, :, :, 0], zj[:, :, :, P // 2 - 1], -1.0 / TAU, None, ALU.mult)
            nc.vector.tensor_scalar(edge[:, :, :, 1], zj[:, :, :, P // 2 - 1], 1.0 / TAU, None, ALU.mult)
            nc.vector.tensor_scalar(edge[:, :, :, 2], zj[:, :, :, P - 1], 1.0 / TAU, None, ALU.mult).then_inc(s_edge, 1)

    tv, s_f, s_e, s_kt, s_a, s_s1, s_o, s_s2 = (k.sem(f"gla_{n}") for n in (
        "tokens_first", "factors", "decayed", "keys_first", "scores", "state_mid", "heads", "state_last"))
    c_v, c_k, c_a, c_s1, c_o, c_s2 = (k.sem(f"gla_{n}") for n in (
        "values_out", "keys_out", "scores_out", "state_mid_out", "heads_out", "state_out"))
    c_out = k.stored["gla_state_stored"]
    with nc.Block() as block:
        @block.tensor
        def _(pe):
            for h in range(GH):
                if h:
                    pe.wait_ge(c_v, h)
                for j in range(2):
                    for c in range(2):
                        nc.tensor.transpose(k.ps[:, 0, (2 * j + c) * P:(2 * j + c + 1) * P],
                                            vo[:, 2 * h + c, j * P:(j + 1) * P], k.ident)
                for c in range(2):
                    mm = nc.tensor.transpose(k.ps[0:NS, 1, c * P:(c + 1) * P], vo[:, 2 * h + c, TP:T], k.ident)
                mm.then_inc(tv, 1)
                pe.wait_ge(s_e, h + 1)
                if h:
                    pe.wait_ge(c_k, h)
                    pe.wait_ge(c_a, h)
                for j in range(2):
                    mm = nc.tensor.transpose(k.ps[:, 2, j * P:(j + 1) * P], kd[:, j * P:(j + 1) * P], k.ident)
                mm.then_inc(s_kt, 1)
                for j in range(2):
                    mm = nc.tensor.matmul(k.ps[:, 3, j * P:(j + 1) * P], ke[:, j * P:(j + 1) * P],
                                          qe[:, j * P:(j + 1) * P], start=True, stop=True)
                mm.then_inc(s_a, 1)
                pe.wait_ge(c_v, h + 1)
                pe.wait_ge(c_k, h + 1)
                if h:
                    pe.wait_ge(c_s1, h)
                    pe.wait_ge(c_s2, h)
                nc.tensor.matmul(k.ps[:, 4, 0:GDV], knat[:, 0, :], vn[:, 0, :], start=True, stop=True).then_inc(s_s1, 1)
                nc.tensor.matmul(k.ps[:, 5, 0:GDV], knat[:, 1, :], vn[:, 1, :], start=True, stop=True).then_inc(s_s2, 1)
                pe.wait_ge(c_a, h + 1)
                pe.wait_ge(c_s1, h + 1)
                if h:
                    pe.wait_ge(c_o, h)
                for c in range(2):
                    o = k.ps[:, 6, c * TP:(c + 1) * TP]
                    nc.tensor.matmul(o[:, 0:P], vn[:, 0, c * P:(c + 1) * P], att[:, 0, :], start=True, stop=True)
                    nc.tensor.matmul(o[:, P:TP], vn[:, 1, c * P:(c + 1) * P], att[:, 1, :], start=True, stop=False)
                    mm = nc.tensor.matmul(o[:, P:TP], s1[:, c * P:(c + 1) * P], q0, start=False, stop=True)
                mm.then_inc(s_o, 1)

        @block.scalar
        def _(act):
            for h in range(GH):
                if h:
                    act.wait_ge(s_e, h)
                for j in range(2):
                    cols = slice(j * P, (j + 1) * P)
                    nc.scalar.activation(fac[:, 0, cols], z[:, h, cols], ACT.Exp, scale=1.0 / TAU,
                                         bias=edge[:, h, j, 0:1])
                    nc.scalar.activation(fac[:, 1, cols], z[:, h, cols], ACT.Exp, scale=-1.0 / TAU,
                                         bias=edge[:, h, j, 1:2])
                    nc.scalar.activation(fac[:, 2, cols], z[:, h, cols], ACT.Exp, scale=-1.0 / TAU,
                                         bias=edge[:, h, j, 2:3])
                nc.scalar.activation(fac[:, 3, 0:P], z[:, h, P:TP], ACT.Exp, scale=1.0 / TAU).then_inc(s_f, 1)
                act.wait_ge(tv, h + 1)
                if h:
                    act.wait_ge(s_o, h)
                nc.scalar.copy(vn.rearrange("p j n -> p (j n)"), k.ps[:, 0, :])
                nc.scalar.copy(vs[:, h * GDV:(h + 1) * GDV], k.ps[0:NS, 1, 0:GDV]).then_inc(c_v, 1)
                act.wait_ge(s_o, h + 1)
                nc.scalar.copy(vo[:, 2 * h:2 * h + 2, 0:TP], k.ps[:, 6, :].rearrange("p (c t) -> p c t", c=2))\
                    .then_inc(c_o, 1)

        @block.vector
        def _(v):
            for h in range(GH):
                v.wait_ge(s_f, h + 1)
                if h:
                    v.wait_ge(s_o, h)
                nc.vector.tensor_tensor(qe, q[:, h, 0:TP], fac[:, 0], ALU.mult)
                nc.vector.tensor_tensor(ke, kk[:, h, 0:TP], fac[:, 1], ALU.mult)
                nc.vector.tensor_tensor(kd, kk[:, h, 0:TP], fac[:, 2], ALU.mult)
                nc.vector.tensor_tensor(q0, q[:, h, P:TP], fac[:, 3, 0:P], ALU.mult).then_inc(s_e, 1)
                v.wait_ge(s_kt, h + 1)
                nc.vector.tensor_copy(knat.rearrange("p j n -> p (j n)"), k.ps[:, 2, 0:TP]).then_inc(c_k, 1)
                v.wait_ge(s_a, h + 1)
                nc.vector.tensor_tensor(att, k.ps[:, 3, 0:TP].rearrange("p (j n) -> p j n", j=2),
                                        k.const("causal").unsqueeze(1).to_broadcast([P, 2, P]),
                                        ALU.mult).then_inc(c_a, 1)
                v.wait_ge(s_s1, h + 1)
                nc.vector.tensor_copy(s1, k.ps[:, 4, 0:GDV]).then_inc(c_s1, 1)
                v.wait_ge(c_s1, h + 1)
                v.wait_ge(s_s2, h + 1)
                if h >= 2:
                    v.wait_ge(c_out, 16 * (h - 1))
                nc.vector.scalar_tensor_tensor(s2[:, h % 2], s1, last_[:, h:h + 1], k.ps[:, 5, 0:GDV], ALU.mult,
                                               ALU.add).then_inc(c_s2, 1)

        @block.gpsimd
        def _(pool):
            for h in range(GH):
                pool.wait_ge(c_s2, h + 1)
                pool.dma_start(out["gla_prompt"][0, 0, h], s2[:, h % 2]).then_inc(c_out, 16)
                pool.wait_ge(c_out, 16 * (h + 1))

    s_bc, s_out, s_new, s_q, s_sil, s_cm, s_or, s_ot = (k.sem(f"gla_sample_{n}") for n in (
        "values_spread", "outer", "state_new", "read", "gate_silu", "compacted", "rows_out", "rows_transposed"))
    s_ldb = [k.sem(f"gla_sample_state_loaded{b}") for b in range(2)]
    s_stb = [k.stored[f"gla_sample_state_stored{b}"] for b in range(2)]
    n_gate = n_in + 8
    orow = k.rstd[:, 0:GDV]
    qz4 = qz.rearrange("p (h b s) -> p h b s", h=GH, b=NS)
    with nc.Block() as block:
        @block.sync
        def _(sp):
            for b in range(NS):
                if b >= 2:
                    sp.wait_ge(s_stb[b % 2], 16 * (b // 2))
                    sp.wait_ge(s_q, b - 1)
                sp.dma_start(st[:, b % 2], inp["state_gla"][0, b].rearrange("h p n -> p h n")).then_inc(s_ldb[b % 2], 16)
                if b % 2 and b >= 3:
                    load_until(k, sp, n_gate + (b - 3) // 2 + RING)

        @block.gpsimd
        def _(pool):
            for b in range(NS):
                pool.wait_ge(s_new, GH * (b + 1))
                pool.dma_start(out["gla_sample"][0, b].rearrange("h p n -> p h n"), st[:, b % 2])\
                    .then_inc(s_stb[b % 2], 16)
            for b in range(2):
                pool.wait_ge(s_stb[b], 16 * NS // 2)

        @block.tensor
        def _(pe):
            for b in range(NS + 1):
                if b < NS:
                    for i in range(2):
                        if b >= 1:
                            pe.wait_ge(s_out, GH * (b - 1) + 2 * i + 2)
                        nc.tensor.matmul(k.ps[:, i, :], k.ident[0:NS, b:b + 1].to_broadcast([NS, P]),
                                         vs[:, i * 512:(i + 1) * 512], start=True, stop=True).then_inc(s_bc, 1)
                    if b % 2 == 0:
                        wait_slot(k, pe, n_gate + b // 2)
                    if b >= 4:
                        pe.wait_ge(s_sil, b - 3)
                    w = slot(k, n_gate + b // 2, 256)
                    for c in range(DC):
                        mm = nc.tensor.matmul(k.ps[:, 4 + b % 4, 0:T], w[:, c, (b % 2) * P:(b % 2 + 1) * P],
                                              k.h[:, c, :], start=(c == 0), stop=(c == DC - 1))
                    if b % 2:
                        mm.then_inc(k.ring_free[(n_gate + b // 2) % RING], 1)
                if b >= 1:
                    if b == 1:
                        pe.wait_ge(s_cm, 2)
                    pe.wait_ge(s_new, GH * b)
                    for h in range(GH):
                        mm = nc.tensor.matmul(k.ps[32 * h:32 * h + NS, 2, 0:GDV], qz4[:, h, b - 1, :],
                                              st[:, (b - 1) % 2, h, :], start=(b == 1), stop=(b == NS))
                    mm.then_inc(s_q, 1)
            pe.wait_ge(s_or, GH)
            for c in range(2):
                mm = nc.tensor.transpose(k.ps[:, 3, c * P:(c + 1) * P], orow[:, c * P:(c + 1) * P], k.ident)
            mm.then_inc(s_ot, 1)

        @block.scalar
        def _(act):
            for b in range(NS):
                for h in range(GH):
                    act.wait_ge(s_bc, 2 * b + h // 2 + 1)
                    if b:
                        act.wait_ge(s_new, GH * (b - 1) + h + 1)
                    nc.scalar.activation(outer[:, h, :], k.ps[:, h // 2, (h % 2) * GDV:(h % 2 + 1) * GDV], ACT.Copy,
                                         scale=kk[:, h, TP + b:TP + b + 1]).then_inc(s_out, 1)
                if b % 2:
                    wait_used(k, act, n_gate + b // 2)
                    for n in (b - 1, b):
                        nc.scalar.activation(gate[:, n], k.ps[:, 4 + n % 4, 0:T], ACT.Silu).then_inc(s_sil, 1)

        @block.vector
        def _(v):
            nc.vector.memset(qz, 0.0).then_inc(s_cm, 1)
            k.dve.link(v, nc.vector.memset(orow, 0.0))
            v.wait_ge(s_cm, 1)
            diagonal = qz.rearrange("p (h n) -> p h n", h=GH)[:, :, 0:NS * NS:NS + 1]
            nc.vector.tensor_copy(diagonal, q[:, :, TP:T]).then_inc(s_cm, 1)
            for b in range(NS):
                v.wait_ge(s_ldb[b % 2], 16 * (b // 2 + 1))
                for h in range(GH):
                    v.wait_ge(s_out, GH * b + h + 1)
                    nc.vector.scalar_tensor_tensor(st[:, b % 2, h, :], st[:, b % 2, h, :], alpha[:, h, b:b + 1],
                                                   outer[:, h, :], ALU.mult, ALU.add).then_inc(s_new, 1)
            v.wait_ge(s_q, NS)
            for h in range(GH):
                nc.vector.tensor_copy(orow[32 * h:32 * h + NS, :], k.ps[32 * h:32 * h + NS, 2, 0:GDV])\
                    .then_inc(s_or, 1)
            v.wait_ge(s_ot, 1)
            for h in range(GH):
                nc.vector.tensor_copy(vo[:, 2 * h:2 * h + 2, TP:T],
                                      k.ps[:, 3, 0:GDV].rearrange("p (c n) -> p c n", c=2)[:, :, 32 * h:32 * h + NS])

    head_norm(k, "gla", vo, 2, GH, k.gla_g, gate, center=False)
    project_out(k, "gla", vo, n_out, 256, 8, 1)



def final(k):
    nc, out = k.nc, k.out
    norm(k, DEPTH, 0, "")
    s_tr, s_cp, s_st = k.sem("y_token_major"), k.sem("y_copied"), k.sem("y_stored")
    y = k.scratch[:, 0:TT * D].rearrange("p (t d) -> p t d", t=TT)
    with nc.Block() as block:
        @block.tensor
        def _(pe):
            for t, (t0, n) in enumerate(TOKENS):
                for c in range(DC):
                    mm = nc.tensor.transpose(k.ps[0:n, 2 * t + c // 4, (c % 4) * P:(c % 4 + 1) * P],
                                             k.h[:, c, t0:t0 + n], k.ident)
                mm.then_inc(s_tr, 1)

        @block.vector
        def _(v):
            for t, (_, n) in enumerate(TOKENS):
                v.wait_ge(s_tr, t + 1)
                nc.vector.tensor_copy(y[0:n, t, :], k.ps[0:n, 2 * t:2 * t + 2, :].rearrange("p b d -> p (b d)"))\
                    .then_inc(s_cp, 1)

        @block.sync
        def _(sp):
            for t, (t0, n) in enumerate(TOKENS):
                sp.wait_ge(s_cp, t + 1)
                dst = out["y_prompt"][0, t0:t0 + n] if t < 2 else out["y_sample"].rearrange("b o d -> (b o) d")
                sp.dma_start(dst, y[0:n, t, :]).then_inc(s_st, 16)
            sp.wait_ge(s_st, 16 * TT)



def experts(k, layer):
    nc, inp = k.nc, k.inp
    sc = k.scratch
    at = [0]

    def area(cols):
        at[0] += cols
        assert at[0] <= k.size, at[0]
        return sc[:, at[0] - cols:at[0]]

    tag = f"moe{layer}"
    PAIRS = EPI // 2
    parts = area(TT * 3 * D // 2).bitcast(BF16).rearrange("p (t s d) -> p t s d", t=TT, s=3)
    xg = area(DC * EPI * CAP).rearrange("p (c n) -> p c n", c=DC)
    hot = area(TT * EPI * CAP // 2).bitcast(BF16).rearrange("p (t e s) -> p t e s", t=TT, e=EPI)
    slot_token = area(PAIRS * T // 2).bitcast(BF16).rearrange("p (b t) -> p b t", b=PAIRS)
    silu = area(PAIRS * DE).rearrange("p (b f) -> p b f", b=PAIRS)
    hid = area(PAIRS * DE).rearrange("p (b f) -> p b f", b=PAIRS)
    hid_t = area(PAIRS * DE).rearrange("p (b m s) -> p b m s", b=PAIRS, m=FC)
    row_parts = area(PAIRS * 3 * D // 2).bitcast(BF16).rearrange("p (b s d) -> p b s d", b=PAIRS, s=3)
    rest = area(2 * 512).rearrange("p (b n) -> p b n", b=2)
    acc = area(DC * T).rearrange("p (c t) -> p c t", c=DC)
    w_parts = area(TT * NE * 3 // 2).bitcast(BF16).rearrange("p (t e s) -> p t e s", t=TT, e=NE)
    w_now = area(TT * EPI * 3 // 2).bitcast(BF16).rearrange("p (t e s) -> p t e s", t=TT, e=EPI)
    w_sum = area(TT * 3).rearrange("p (t s) -> p t s", t=TT)
    own = area(PAIRS * 6).rearrange("p (b n) -> p b n", b=PAIRS)
    slot_weight = area(PAIRS)
    sh_silu = area(FC * T).rearrange("p (m t) -> p m t", m=FC)
    sh_hid = area(FC * T).rearrange("p (m t) -> p m t", m=FC)
    wr = area(DC * NE).rearrange("p (c e) -> p c e", c=DC)
    bias = area(NE)

    def grid():
        return area(TT * NE).rearrange("p (t e) -> p t e", t=TT)

    score, biased, left, chosen, weight, rank, key = (grid() for _ in range(7))
    w_rest, w_picked = grid(), rest.rearrange("p b n -> p (b n)")[:, 0:TT * NE * 3]
    w_picked = w_picked.rearrange("p (t e s) -> p t e s", t=TT, e=NE)
    best = area(TT * NG * 8).rearrange("p (t g n) -> p t g n", t=TT, g=NG)
    beats = area(TT * NG * NG).rearrange("p (t g n) -> p t g n", t=TT, g=NG)
    ties = w_rest.rearrange("p t (g n) -> p t g n", g=NG)
    gscore = area(TT * NG).rearrange("p (t g) -> p t g", t=TT)
    gmask = area(TT * NG).rearrange("p (t g) -> p t g", t=TT)
    top = area(TT * 8).rearrange("p (t n) -> p t n", t=TT)
    total = area(2 * TT)
    count, blocks, ends, shift = (area(NE) for _ in range(4))
    lookup = area(XBP)
    extra = area(1 + XBP).bitcast(I32)
    low, high = area(1), area(1)
    found = area(2 * TT)
    compare = xg.rearrange("p c n -> p (c n)")[0:1, 0:XB * NE].rearrange("p (b e) -> p b e", b=XB)
    keep_small = area(DC * NS).rearrange("p (c s) -> p c s", c=DC)

    n_sh, n_moe = k.stage[f"shared{layer}"], k.stage[f"moe{layer}"]
    n_end = n_moe + ROUNDS * RING
    ident16 = k.ident16[:, :]
    ident, ones, before, iota = k.ident, k.ones, k.const("before"), k.const("iota")

    s_w, s_log, s_sc, s_rk, s_ch, s_nat, s_natc, s_hi = (k.sem(f"{tag}_{n}") for n in (
        "router_loaded", "logits", "scores", "ranks", "chosen", "token_major", "parts", "high_part"))
    s_shs, s_shh, s_shd, s_shx, s_fill = (k.sem(f"{tag}_{n}") for n in (
        "shared_silu", "shared_hidden", "shared_down", "shared_out", "scores_filled"))
    with nc.Block() as block:
        @block.sync
        def _(sp):
            sp.dma_start(wr, inp["moe_w_router"][layer].rearrange("(c p) e -> p c e", p=P)).then_inc(s_w, 16)
            sp.dma_start(bias, inp["moe_router_bias"][layer:layer + 1, :].to_broadcast([P, NE])).then_inc(s_w, 16)
            load_until(k, sp, n_sh + 3 + RING)

        @block.tensor
        def _(pe):
            pe.wait_ge(s_w, 32)
            for t, (t0, n) in enumerate(TOKENS):
                for c in range(DC):
                    mm = nc.tensor.matmul(k.ps[0:n, 0, t * NE:(t + 1) * NE], k.h[:, c, t0:t0 + n], wr[:, c, :],
                                          start=(c == 0), stop=(c == DC - 1))
                mm.then_inc(s_log, 1)
            for j in range(2):
                wait_slot(k, pe, n_sh + j)
                w = slot(k, n_sh + j, DE)
                for m in range(FC):
                    for c in range(DC):
                        mm = nc.tensor.matmul(k.ps[:, 2 + 2 * j + m, 0:T], w[:, c, m * P:(m + 1) * P], k.h[:, c, :],
                                              start=(c == 0), stop=(c == DC - 1))
                mm.then_inc(k.ring_free[(n_sh + j) % RING], 1)
            for t, (t0, n) in enumerate(TOKENS):
                if t:
                    pe.wait_ge(s_natc, t)
                for c in range(DC):
                    mm = nc.tensor.transpose(k.ps[0:n, 6 + c // 4, (c % 4) * P:(c % 4 + 1) * P], k.h[:, c, t0:t0 + n],
                                             ident)
                mm.then_inc(s_nat, 1)
                if t == 0:
                    wait_slot(k, pe, n_sh + 2)
                    pe.wait_ge(s_shh, FC)
                    w = slot(k, n_sh + 2, D)
                    for c in range(DC):
                        if c >= 4:
                            pe.wait_ge(s_shx, c - 3)
                        for m in range(FC):
                            mm = nc.tensor.matmul(k.ps[:, 2 + c % 4, 0:T], w[:, m, c * P:(c + 1) * P], sh_hid[:, m],
                                                  start=(m == 0), stop=(m == FC - 1))
                        mm.then_inc(s_shd if c < DC - 1 else k.ring_free[(n_sh + 2) % RING], 1)
                    pe.wait_ge(s_ch, 1)
                    for u in range(TT + 1):
                        for s in range(min(u + 1, TT)):
                            mm = nc.tensor.matmul(k.ps[:, 1, u * NE:(u + 1) * NE], before if s == u else ones,
                                                  chosen[:, s, :], start=(s == 0), stop=(s == min(u, TT - 1)))
                    mm.then_inc(s_rk, 1)

        @block.scalar
        def _(act):
            act.wait_ge(s_fill, 1)
            for t, (_, n) in enumerate(TOKENS):
                act.wait_ge(s_log, 3)
                ins = nc.scalar.activation(score[0:n, t, :], k.ps[0:n, 0, t * NE:(t + 1) * NE], ACT.Sigmoid)
            ins.then_inc(s_sc, 1)
            for m in range(FC):
                wait_used(k, act, n_sh)
                nc.scalar.activation(sh_silu[:, m], k.ps[:, 2 + m, 0:T], ACT.Silu).then_inc(s_shs, 1)
            act.wait_ge(s_nat, 1)
            n = TOKENS[0][1]
            nc.scalar.copy(parts[0:n, 0, 0, :], k.ps[0:n, 6:8, :].rearrange("p b d -> p (b d)")).then_inc(s_hi, 1)
            for c in range(DC):
                if c < DC - 1:
                    act.wait_ge(s_shd, c + 1)
                else:
                    wait_used(k, act, n_sh + 2)
                nc.scalar.copy(acc[:, c, :], k.ps[:, 2 + c % 4, 0:T]).then_inc(s_shx, 1)
            for t, (_, n) in list(enumerate(TOKENS))[1:]:
                act.wait_ge(s_nat, t + 1)
                src = k.ps[0:n, 6:8, :].rearrange("p b d -> p (b d)")
                nc.scalar.copy(parts[0:n, t, 0, :], src).then_inc(s_hi, 1)

        @block.vector
        def _(v):
            link = lambda ins: k.dve.link(v, ins)

            def split_tokens(t):
                n = TOKENS[t][1]
                v.wait_ge(s_hi, t + 1)
                src = k.ps[0:n, 6:8, :].rearrange("p b d -> p (b d)")
                what_is_left = rest.rearrange("p b n -> p (b n)")[0:n]
                link(nc.vector.tensor_tensor(what_is_left, src, parts[0:n, t, 0, :], ALU.subtract))
                link(nc.vector.tensor_copy(parts[0:n, t, 1, :], what_is_left))
                nc.vector.tensor_tensor(parts[0:n, t, 2, :], what_is_left, parts[0:n, t, 1, :],
                                        ALU.subtract).then_inc(s_natc, 1)
                v.wait_ge(s_natc, t + 1)

            nc.vector.memset(score[:, TT - 1, :], 0.0).then_inc(s_fill, 1)
            v.wait_ge(s_sc, 1)
            v.wait_ge(s_w, 32)
            link(nc.vector.tensor_tensor(biased, score, bias.unsqueeze(1).to_broadcast([P, TT, NE]), ALU.add))
            for t in range(TT):
                for g in range(NG):
                    ins = nc.vector.max(out=best[:, t, g, :], in_=biased[:, t, g * 8:(g + 1) * 8])
            link(ins)
            link(nc.vector.tensor_tensor(gscore, best[:, :, :, 0], best[:, :, :, 1], ALU.add))
            mine = gscore.unsqueeze(3).to_broadcast([P, TT, NG, NG])
            other = gscore.unsqueeze(2).to_broadcast([P, TT, NG, NG])
            nc.vector.tensor_tensor(beats, other, mine, ALU.is_gt)
            link(nc.vector.tensor_tensor(ties, other, mine, ALU.is_equal))
            tri = k.const("gtri").rearrange("p (g n) -> p g n", g=NG).unsqueeze(1).to_broadcast([P, TT, NG, NG])
            link(nc.vector.tensor_tensor(ties, ties, tri, ALU.mult))
            link(nc.vector.tensor_tensor(beats, beats, ties, ALU.add))
            link(nc.vector.tensor_reduce(gmask, beats, AX.X, ALU.add))
            link(nc.vector.tensor_scalar(gmask, gmask, TOPG - 0.5, None, ALU.is_lt))
            open_ = gmask.unsqueeze(3).to_broadcast([P, TT, NG, 8])
            b4 = biased.rearrange("p t (g n) -> p t g n", g=NG)
            link(nc.vector.tensor_tensor(b4, b4, open_, ALU.mult))
            link(nc.vector.tensor_scalar(gmask, gmask, 1.0, 1.0e30, ALU.subtract, ALU.mult))
            link(nc.vector.tensor_tensor(b4, b4, open_, ALU.add))
            for t in range(TT):
                ins = nc.vector.max(out=top[:, t, :], in_=biased[:, t, :])
            link(ins)
            for t in range(TT):
                ins = nc.vector.match_replace(out=left[:, t, :], in_to_replace=top[:, t, :], in_values=biased[:, t, :],
                                              imm_value=-3.0e38)
            link(ins)
            link(nc.vector.tensor_tensor(chosen, left, biased, ALU.not_equal))
            valid = k.const("valid").unsqueeze(2).to_broadcast([P, TT, NE])
            nc.vector.tensor_tensor(chosen, chosen, valid, ALU.mult).then_inc(s_ch, 1)
            v.wait_ge(s_ch, 1)
            for m in range(FC):
                v.wait_ge(s_shs, m + 1)
                wait_used(k, v, n_sh + 1)
                nc.vector.tensor_tensor(sh_hid[:, m], sh_silu[:, m], k.ps[:, 4 + m, 0:T], ALU.mult).then_inc(s_shh, 1)
            split_tokens(0)
            v.wait_ge(s_rk, 1)
            ranks = k.ps[:, 1, 0:TT * NE].rearrange("p (t e) -> p t e", t=TT)
            link(nc.vector.tensor_copy(rank, ranks))
            link(nc.vector.tensor_copy(count, k.ps[:, 1, TT * NE:(TT + 1) * NE]))
            link(nc.vector.scalar_tensor_tensor(left, rank, 1.0, chosen, ALU.add, ALU.mult))
            link(nc.vector.tensor_scalar(left, left, -1.0, None, ALU.add))
            link(nc.vector.tensor_tensor(weight, score, chosen, ALU.mult))
            link(nc.vector.tensor_reduce(total[:, 0:TT], weight, AX.X, ALU.add))
            nv = total[:, TT:2 * TT]
            link(nc.vector.tensor_scalar(nv, k.const("valid"), -1.0, 1.0, ALU.mult, ALU.add))
            link(nc.vector.tensor_tensor(total[:, 0:TT], total[:, 0:TT], nv, ALU.add))
            link(nc.vector.reciprocal(total[:, 0:TT], total[:, 0:TT]))
            link(nc.vector.tensor_tensor(weight, weight, total[:, 0:TT].unsqueeze(2).to_broadcast([P, TT, NE]),
                                         ALU.mult))
            link(nc.vector.tensor_scalar(weight, weight, SCALE, None, ALU.mult))
            link(nc.vector.tensor_copy(w_parts[:, :, :, 0], weight))
            link(nc.vector.tensor_tensor(w_rest, weight, w_parts[:, :, :, 0], ALU.subtract))
            link(nc.vector.tensor_copy(w_parts[:, :, :, 1], w_rest))
            link(nc.vector.tensor_tensor(w_parts[:, :, :, 2], w_rest, w_parts[:, :, :, 1], ALU.subtract))
            link(nc.vector.tensor_scalar(blocks, count, CAP + 0.5, None, ALU.is_gt))
            for j in range(2, (T - 1) // CAP + 1):
                link(nc.vector.scalar_tensor_tensor(blocks, count, CAP * j + 0.5, blocks, ALU.is_gt, ALU.add))
            link(nc.vector.tensor_tensor_scan(ends, ones[:, 0:NE], blocks, 0.0, ALU.mult, ALU.add))
            link(nc.vector.tensor_tensor(shift, ends, blocks, ALU.subtract))
            link(nc.vector.tensor_scalar(shift, shift, float(CAP), 1.0 - CAP, ALU.mult, ALU.add))
            link(nc.vector.tensor_tensor(key, rank, shift.unsqueeze(1).to_broadcast([P, TT, NE]), ALU.add))
            link(nc.vector.scalar_tensor_tensor(key, left, CAP - 0.5, key, ALU.is_gt, ALU.mult))
            link(nc.vector.tensor_copy(extra[0:1, 0:1], ends[0:1, NE - 1:NE]))
            link(nc.vector.tensor_tensor(compare, ends[0:1, :].unsqueeze(1).to_broadcast([1, XB, NE]),
                                         iota[0:1, 0:XB].unsqueeze(2).to_broadcast([1, XB, NE]), ALU.is_le))
            link(nc.vector.tensor_reduce(lookup[0:1, 0:XB], compare, AX.X, ALU.add))
            link(nc.vector.tensor_scalar(lookup[0:1, 0:XB], lookup[0:1, 0:XB], NE - 1.0, None, ALU.min))
            link(nc.vector.tensor_copy(extra[0:1, 1:1 + XB], lookup[0:1, 0:XB]))
            link(nc.vector.memset(low, 1.0))
            link(nc.vector.memset(high, 1.0 + CAP))
            for t in range(1, TT):
                split_tokens(t)

    (s_hot, s_gat, g_even, g_odd, s_ht, s_htc, s_own, s_sil, s_hid, s_hidt, s_hidtc, s_dn, s_rhi, s_rest, s_mid,
     s_part, s_scat, s_add) = (k.sem(f"{tag}_{n}") for n in (
         "one_hot", "gathered", "gathered_out_even", "gathered_out_odd", "slots_first", "slots_first_out",
         "slot_weight", "silu", "hidden", "hidden_transposed", "hidden_transposed_out", "down", "row_high",
         "row_rest", "row_middle", "row_parts", "spread", "added"))
    x_gu_load, x_dn_load = k.sem(f"{tag}_extra_gate_up_loaded"), k.sem(f"{tag}_extra_down_loaded")
    x_slots = [(n_end + i) % RING for i in range(3)]
    number = extra[0:1, 0:1]

    def place(kind, e):
        return n_moe + PLACE[(kind, e)]

    def load_extra(sp, kinds, e):
        for i in kinds:
            src = inp[("moe_w_gate", "moe_w_up", "moe_w_down")[i]][layer].rearrange("e (k p) n -> e p k n", p=P)
            src = src[bass.ds(e, 1)].rearrange("o p k n -> (o p) k n")
            sp.dma_start(slot(k, x_slots[i], src.shape[2]), src).then_inc(x_dn_load if i == 2 else x_gu_load, 16)

    with nc.Block() as block:
        @block.sync
        def _(sp):
            with sp.Fori(1, ROUNDS) as r:
                for name, e in ROUND:
                    n = place(name, e)
                    src = inp[name][layer].rearrange("e (k p) n -> e p k n", p=P)[bass.ds(r * EPI + e, 1)]
                    src = src.rearrange("o p k n -> (o p) k n")
                    sp.wait_ge(k.ring_free[n % RING], r + n // RING)
                    sp.dma_start(slot(k, n, src.shape[2]), src).then_inc(k.ring_full[n % RING], 16)
            for i in range(3):
                sp.wait_ge(k.ring_free[x_slots[i]], (n_end + i) // RING)
            with sp.If(sp.value_load(number, min_val=0, max_val=XB) > 0):
                load_extra(sp, range(3), sp.value_load(extra[0:1, 1:2], min_val=0, max_val=NE - 1))
            k.issued = n_end + 3
            load_until(k, sp, n_end + RING)

        def gather(pe, r):
            pe.wait_ge(s_hot, r + 1)
            for c in range(DC):
                b = (c // 2) % 2
                if c % 2 == 0 and c >= 4:
                    pe.wait_ge(g_odd if b else g_even, 2 * r + 1)
                for t, (_, n) in enumerate(TOKENS):
                    for s in range(3):
                        mm = nc.tensor.matmul(k.ps[:, b, (c % 2) * 256:(c % 2 + 1) * 256],
                                              parts[0:n, t, s, c * P:(c + 1) * P],
                                              hot[0:n, t].rearrange("p e s -> p (e s)"),
                                              start=(t == 0 and s == 0), stop=(t == TT - 1 and s == 2))
                if c % 2:
                    mm.then_inc(s_gat, 1)

        def slots_first(pe):
            for p in range(PAIRS):
                for t, (t0, n) in enumerate(TOKENS):
                    pair = hot[0:n, t, 2 * p:2 * p + 2, :].rearrange("p e s -> p (e s)")
                    nc.tensor.matmul(k.ps[:, 4 + p, t0:t0 + n], pair, ident16[0:n, 0:n], start=True, stop=True)
                for t, (_, n) in enumerate(TOKENS):
                    pair = hot[0:n, t, 2 * p:2 * p + 2, :].rearrange("p e s -> p (e s)")
                    mm = nc.tensor.matmul(k.ps[:, 4 + p, T:T + 6], pair,
                                          w_now[0:n, t, 2 * p:2 * p + 2, :].rearrange("p e s -> p (e s)"),
                                          start=(t == 0), stop=(t == TT - 1))
            mm.then_inc(s_ht, 1)

        def spread(pe, r):
            pe.wait_ge(s_htc, r + 1)
            pe.wait_ge(s_part, 4 * r + 4)
            for c in range(DC):
                pe.wait_ge(s_add, DC * (r + 1) + c - 1)
                for p in range(PAIRS):
                    for s in range(3):
                        mm = nc.tensor.matmul(k.ps[:, c % 2, 0:T], row_parts[:, p, s, c * P:(c + 1) * P],
                                              slot_token[:, p, :], start=(p == 0 and s == 0),
                                              stop=(p == PAIRS - 1 and s == 2))
                mm.then_inc(s_scat, 1)

        def pe_round(pe, r, first, last):
            pe.wait_ge(g_even, 2 * r + 2)
            pe.wait_ge(g_odd, 2 * r + 2)
            for p in range(PAIRS):
                for e in (2 * p, 2 * p + 1):
                    for name in ("moe_w_gate", "moe_w_up"):
                        n = place(name, e)
                        pe.wait_ge(k.ring_full[n % RING], 16 * (r + n // RING + 1))
                for j, name in enumerate(("moe_w_gate", "moe_w_up")):
                    for c in range(DC):
                        for e in (2 * p, 2 * p + 1):
                            n, lo = place(name, e), CAP * (e % 2)
                            mm = nc.tensor.matmul(k.ps[lo:lo + CAP, 2 + p, j * DE:(j + 1) * DE],
                                                  xg[:, c, e * CAP:(e + 1) * CAP], slot(k, n, DE)[:, c, :],
                                                  start=(c == 0), stop=(c == DC - 1))
                            if c == DC - 1:
                                mm.then_inc(k.ring_free[n % RING], 1)
            if not first:
                spread(pe, r - 1)
                pe.wait_ge(s_part, 4 * r)
            for p in range(PAIRS):
                pe.wait_ge(s_hid, PAIRS * r + p + 1)
                for m in range(FC):
                    mm = nc.tensor.transpose(k.ps[:, 6 + p, m * P:(m + 1) * P],
                                             hid[:, p, m * P:(m + 1) * P], ident)
                mm.then_inc(s_hidt, 1)
            if not last:
                if not first:
                    pe.wait_ge(s_add, DC * r + DC)
                gather(pe, r + 1)
            for p in range(PAIRS):
                pe.wait_ge(s_hidtc, PAIRS * r + 2)
                for e in (2 * p, 2 * p + 1):
                    n = place("moe_w_down", e)
                    pe.wait_ge(k.ring_full[n % RING], 16 * (r + n // RING + 1))
                for half in range(2):
                    if p:
                        pe.wait_ge(s_rest, 4 * r + 2 * (p - 1) + half + 1)
                    for m in range(FC):
                        for e in (2 * p, 2 * p + 1):
                            n, lo = place("moe_w_down", e), CAP * (e % 2)
                            mm = nc.tensor.matmul(k.ps[lo:lo + CAP, 6 + half, :], hid_t[:, p, m, lo:lo + CAP],
                                                  slot(k, n, D)[:, m, half * 512:(half + 1) * 512],
                                                  start=(m == 0), stop=(m == FC - 1))
                            if half == 1 and m == FC - 1:
                                mm.then_inc(k.ring_free[n % RING], 1)
                            elif half == 0 and m == FC - 1 and e % 2:
                                mm.then_inc(s_dn, 1)
            if not last:
                pe.wait_ge(s_htc, r + 1)
                slots_first(pe)

        @block.tensor
        def _(pe):
            gather(pe, 0)
            slots_first(pe)
            pe_round(pe, 0, True, False)
            with pe.Fori(1, ROUNDS - 1) as r:
                pe_round(pe, r, False, False)
            pe_round(pe, ROUNDS - 1, False, True)
            spread(pe, ROUNDS - 1)

        def one_hot(v, r):
            nc.vector.tensor_copy(w_now, w_parts[:, :, bass.ds(r * EPI, EPI), :])
            nc.vector.tensor_tensor(hot, left[:, :, bass.ds(r * EPI, EPI)].unsqueeze(3).to_broadcast([P, TT, EPI, CAP]),
                                    iota[:, 0:CAP].unsqueeze(1).unsqueeze(1).to_broadcast([P, TT, EPI, CAP]),
                                    ALU.is_equal).then_inc(s_hot, 1)

        def take(eng, r, b, copy, sem):
            for q in range(2):
                eng.wait_ge(s_gat, DC // 2 * r + 2 * q + b + 1)
                c = 4 * q + 2 * b
                copy(xg[:, c:c + 2, :], k.ps[:, b, :].rearrange("p (c n) -> p c n", c=2)).then_inc(sem, 1)

        def rows_done(eng, r, p, half):
            if half == 0:
                eng.wait_ge(s_dn, PAIRS * r + p + 1)
            else:
                n = place("moe_w_down", 2 * p + 1)
                eng.wait_ge(k.ring_free[n % RING], r + n // RING + 1)

        @block.vector
        def _(v):
            def add_spread(r):
                v.wait_ge(s_add, DC * (r + 1))
                for c in range(DC):
                    v.wait_ge(s_scat, DC * r + c + 1)
                    nc.vector.tensor_tensor(acc[:, c, :], acc[:, c, :], k.ps[:, c % 2, 0:T], ALU.add).then_inc(s_add, 1)

            def round_(r, first, last):
                v.wait_ge(s_ht, r + 1)
                for p in range(PAIRS):
                    nc.vector.scalar_tensor_tensor(own[:, p, :], k.ps[:, 4 + p, T:T + 6], 1.0, k.const("own"), ALU.mult,
                                                   ALU.mult, accum_out=slot_weight[:, p:p + 1]).then_inc(s_own, 1)
                v.wait_ge(s_own, PAIRS * r + PAIRS)
                for p in range(PAIRS):
                    v.wait_ge(s_sil, PAIRS * r + p + 1)
                    nc.vector.scalar_tensor_tensor(hid[:, p, :], silu[:, p, :], slot_weight[:, p:p + 1],
                                                   k.ps[:, 2 + p, DE:2 * DE], ALU.mult, ALU.mult).then_inc(s_hid, 1)
                if not first:
                    add_spread(r - 1)
                if not last:
                    take(v, r + 1, 0, nc.vector.tensor_copy, g_even)
                for q in range(2 * PAIRS):
                    p, half = divmod(q, 2)
                    cols = slice(half * 512, (half + 1) * 512)
                    v.wait_ge(s_rhi, 4 * r + q + 1)
                    if not first or q >= 2:
                        v.wait_ge(s_part, 4 * r + q - 1)
                    nc.vector.tensor_tensor(rest[:, half], k.ps[:, 6 + half, :], row_parts[:, p, 0, cols],
                                            ALU.subtract).then_inc(s_rest, 1)
                    v.wait_ge(s_rest, 4 * r + q + 1)
                    nc.vector.tensor_copy(row_parts[:, p, 1, cols], rest[:, half]).then_inc(s_mid, 1)
                    v.wait_ge(s_mid, 4 * r + q + 1)
                    nc.vector.tensor_tensor(row_parts[:, p, 2, cols], rest[:, half], row_parts[:, p, 1, cols],
                                            ALU.subtract).then_inc(s_part, 1)

            v.sem_inc(s_add, DC)
            one_hot(v, 0)
            take(v, 0, 0, nc.vector.tensor_copy, g_even)
            v.wait_ge(s_ht, 1)
            one_hot(v, 1)
            round_(0, True, False)
            v.wait_ge(s_ht, 2)
            one_hot(v, 2)
            with v.Fori(1, ROUNDS - 2) as r:
                round_(r, False, False)
                v.wait_ge(s_ht, r + 2)
                one_hot(v, r + 2)
            round_(ROUNDS - 2, False, False)
            round_(ROUNDS - 1, False, True)
            add_spread(ROUNDS - 1)

        @block.scalar
        def _(act):
            def slots_out(r):
                act.wait_ge(s_own, PAIRS * r + PAIRS)
                for p in range(PAIRS):
                    ins = nc.scalar.copy(slot_token[:, p, :], k.ps[:, 4 + p, 0:T])
                ins.then_inc(s_htc, 1)

            def round_(r, first, last):
                for p in range(PAIRS):
                    n = place("moe_w_up", 2 * p + 1)
                    act.wait_ge(k.ring_free[n % RING], r + n // RING + 1)
                    nc.scalar.activation(silu[:, p, :], k.ps[:, 2 + p, 0:DE], ACT.Silu).then_inc(s_sil, 1)
                if first:
                    act.wait_ge(s_ht, 1)
                else:
                    act.wait_ge(s_scat, DC * r)
                slots_out(r)
                for p in range(PAIRS):
                    act.wait_ge(s_hidt, PAIRS * r + p + 1)
                    nc.scalar.copy(hid_t[:, p].rearrange("p m s -> p (m s)"), k.ps[:, 6 + p, 0:DE])\
                        .then_inc(s_hidtc, 1)
                if not last:
                    take(act, r + 1, 1, nc.scalar.copy, g_odd)
                for q in range(2 * PAIRS):
                    p, half = divmod(q, 2)
                    rows_done(act, r, p, half)
                    nc.scalar.copy(row_parts[:, p, 0, half * 512:(half + 1) * 512], k.ps[:, 6 + half, :])\
                        .then_inc(s_rhi, 1)

            take(act, 0, 1, nc.scalar.copy, g_odd)
            round_(0, True, False)
            with act.Fori(1, ROUNDS - 1) as r:
                round_(r, False, False)
            round_(ROUNDS - 1, False, True)

    (x_hot, x_gat, x_ht, x_got, x_tok, x_gu, x_sil, x_hid, x_hidt, x_hidtc, x_dn, x_hi, x_rest, x_part, x_scat,
     x_add, x_step) = (k.sem(f"{tag}_extra_{n}") for n in (
         "one_hot", "gathered", "slots_first", "gathered_out", "slots_first_out", "gate_up", "silu", "hidden",
         "hidden_transposed", "hidden_transposed_out", "down", "row_high", "row_rest", "row_parts", "spread",
         "added", "vector_step"))
    XSTEPS = 11
    with nc.Block() as block:
        @block.sync
        def _(sp):
            total_ = sp.value_load(number, min_val=0, max_val=XB)
            with sp.If(total_ > 1):
                with sp.Fori(1, total_) as b:
                    e = sp.value_load(extra[0:1, bass.ds(b + 1, 1)], min_val=0, max_val=NE - 1)
                    sp.wait_ge(x_gu, b)
                    load_extra(sp, (0, 1), e)
                    sp.wait_ge(x_dn, 2 * b)
                    load_extra(sp, (2,), e)

        @block.tensor
        def _(pe):
            total_ = pe.value_load(number, min_val=0, max_val=XB)
            with pe.If(total_ > 0):
                with pe.Fori(0, total_) as b:
                    pe.wait_ge(x_hot, b + 1)
                    pe.wait_ge(x_add, DC * b + DC)
                    for c in range(DC):
                        for t, (_, n) in enumerate(TOKENS):
                            for s in range(3):
                                mm = nc.tensor.matmul(k.ps[:, 0, c * CAP:(c + 1) * CAP],
                                                      parts[0:n, t, s, c * P:(c + 1) * P], hot[0:n, t, 0, :],
                                                      start=(t == 0 and s == 0), stop=(t == TT - 1 and s == 2))
                    mm.then_inc(x_gat, 1)
                    for t, (t0, n) in enumerate(TOKENS):
                        nc.tensor.matmul(k.ps[0:CAP, 4, t0:t0 + n], hot[0:n, t, 0, :], ident16[0:n, 0:n], start=True,
                                         stop=True)
                    for t, (_, n) in enumerate(TOKENS):
                        mm = nc.tensor.matmul(k.ps[0:CAP, 4, T:T + 3], hot[0:n, t, 0, :], w_now[0:n, t, 0, :],
                                              start=(t == 0), stop=(t == TT - 1))
                    mm.then_inc(x_ht, 1)
                    pe.wait_ge(x_got, b + 1)
                    pe.wait_ge(x_gu_load, 32 * b + 32)
                    for j in range(2):
                        for c in range(DC):
                            mm = nc.tensor.matmul(k.ps[0:CAP, 2, j * DE:(j + 1) * DE], xg[:, c, 0:CAP],
                                                  slot(k, x_slots[j], DE)[:, c, :], start=(c == 0), stop=(c == DC - 1))
                    mm.then_inc(x_gu, 1)
                    pe.wait_ge(x_hid, b + 1)
                    for m in range(FC):
                        mm = nc.tensor.matmul(k.ps[:, 3, m * CAP:(m + 1) * CAP], hid[0:CAP, 0, m * P:(m + 1) * P],
                                              ident[0:CAP, 0:CAP], start=True, stop=True)
                    mm.then_inc(x_hidt, 1)
                    pe.wait_ge(x_hidtc, b + 1)
                    pe.wait_ge(x_dn_load, 16 * b + 16)
                    for half in range(2):
                        for m in range(FC):
                            mm = nc.tensor.matmul(k.ps[0:CAP, 6 + half, :], hid_t[:, 0, m, 0:CAP],
                                                  slot(k, x_slots[2], D)[:, m, half * 512:(half + 1) * 512],
                                                  start=(m == 0), stop=(m == FC - 1))
                        mm.then_inc(x_dn, 1)
                    pe.wait_ge(x_tok, b + 1)
                    pe.wait_ge(x_part, 2 * b + 2)
                    for c in range(DC):
                        if c >= 2:
                            pe.wait_ge(x_add, DC * b + DC + c - 1)
                        for s in range(3):
                            mm = nc.tensor.matmul(k.ps[:, c % 2, 0:T], row_parts[0:CAP, 0, s, c * P:(c + 1) * P],
                                                  slot_token[0:CAP, 0, :], start=(s == 0), stop=(s == 2))
                        mm.then_inc(x_scat, 1)

        @block.vector
        def _(v):
            v.sem_inc(x_add, DC)
            total_ = v.value_load(number, min_val=0, max_val=XB)
            with v.If(total_ > 0):
                with v.Fori(0, total_) as b:
                    steps = [0]

                    def link(ins):
                        steps[0] += 1
                        ins.then_inc(x_step, 1)
                        v.wait_ge(x_step, XSTEPS * b + steps[0])

                    link(nc.vector.scalar_tensor_tensor(biased, key, low, key, ALU.is_ge, ALU.mult))
                    link(nc.vector.scalar_tensor_tensor(biased, biased, high, biased, ALU.is_lt, ALU.mult))
                    link(nc.vector.tensor_reduce(found[:, 0:TT], biased, AX.X, ALU.add))
                    link(nc.vector.tensor_scalar(found[:, TT:2 * TT], found[:, 0:TT], low, None, ALU.subtract))
                    link(nc.vector.tensor_tensor(hot[:, :, 0, :],
                                                 found[:, TT:2 * TT].unsqueeze(2).to_broadcast([P, TT, CAP]),
                                                 iota[:, 0:CAP].unsqueeze(1).to_broadcast([P, TT, CAP]),
                                                 ALU.is_equal))
                    link(nc.vector.tensor_scalar(biased, biased, 0.5, None, ALU.is_gt))
                    link(nc.vector.tensor_tensor(w_picked, w_parts,
                                                 biased.unsqueeze(3).to_broadcast([P, TT, NE, 3]), ALU.mult))
                    link(nc.vector.tensor_reduce(w_sum, w_picked.rearrange("p t e s -> p t s e"), AX.X, ALU.add))
                    link(nc.vector.tensor_copy(w_now[:, :, 0, :], w_sum))
                    nc.vector.tensor_scalar(low, low, float(CAP), None, ALU.add).then_inc(x_hot, 1)
                    v.wait_ge(x_hot, b + 1)
                    link(nc.vector.tensor_scalar(high, high, float(CAP), None, ALU.add))
                    v.wait_ge(x_ht, b + 1)
                    link(nc.vector.tensor_reduce(slot_weight[0:CAP, 0:1], k.ps[0:CAP, 4, T:T + 3], AX.X, ALU.add))
                    v.wait_ge(x_sil, b + 1)
                    nc.vector.scalar_tensor_tensor(hid[0:CAP, 0, :], silu[0:CAP, 0, :], slot_weight[0:CAP, 0:1],
                                                   k.ps[0:CAP, 2, DE:2 * DE], ALU.mult, ALU.mult).then_inc(x_hid, 1)
                    for half in range(2):
                        cols = slice(half * 512, (half + 1) * 512)
                        v.wait_ge(x_hi, 2 * b + half + 1)
                        nc.vector.tensor_tensor(rest[0:CAP, half], k.ps[0:CAP, 6 + half, :],
                                                row_parts[0:CAP, 0, 0, cols], ALU.subtract).then_inc(x_rest, 1)
                        v.wait_ge(x_rest, 4 * b + 2 * half + 1)
                        nc.vector.tensor_copy(row_parts[0:CAP, 0, 1, cols], rest[0:CAP, half]).then_inc(x_rest, 1)
                        v.wait_ge(x_rest, 4 * b + 2 * half + 2)
                        nc.vector.tensor_tensor(row_parts[0:CAP, 0, 2, cols], rest[0:CAP, half],
                                                row_parts[0:CAP, 0, 1, cols], ALU.subtract).then_inc(x_part, 1)
                    v.wait_ge(x_part, 2 * b + 2)
                    v.wait_ge(x_add, DC * b + DC)
                    for c in range(DC):
                        v.wait_ge(x_scat, DC * b + c + 1)
                        nc.vector.tensor_tensor(acc[:, c, :], acc[:, c, :], k.ps[:, c % 2, 0:T],
                                                ALU.add).then_inc(x_add, 1)
                    assert steps[0] == XSTEPS

        @block.scalar
        def _(act):
            total_ = act.value_load(number, min_val=0, max_val=XB)
            with act.If(total_ > 0):
                with act.Fori(0, total_) as b:
                    act.wait_ge(x_gat, b + 1)
                    nc.scalar.copy(xg[:, :, 0:CAP], k.ps[:, 0, :].rearrange("p (c n) -> p c n", c=DC)).then_inc(x_got, 1)
                    act.wait_ge(x_ht, b + 1)
                    act.wait_ge(x_step, XSTEPS * b + XSTEPS)
                    nc.scalar.copy(slot_token[0:CAP, 0, :], k.ps[0:CAP, 4, 0:T]).then_inc(x_tok, 1)
                    act.wait_ge(x_gu, b + 1)
                    nc.scalar.activation(silu[0:CAP, 0, :], k.ps[0:CAP, 2, 0:DE], ACT.Silu).then_inc(x_sil, 1)
                    act.wait_ge(x_hidt, b + 1)
                    nc.scalar.copy(hid_t[:, 0, :, 0:CAP], k.ps[:, 3, 0:FC * CAP].rearrange("p (m s) -> p m s", m=FC))\
                        .then_inc(x_hidtc, 1)
                    for half in range(2):
                        act.wait_ge(x_dn, 2 * b + half + 1)
                        nc.scalar.copy(row_parts[0:CAP, 0, 0, half * 512:(half + 1) * 512], k.ps[0:CAP, 6 + half, :])\
                            .then_inc(x_hi, 1)

    with nc.Block() as block:
        @block.sync
        def _(sp):
            k.issued = n_end
            load_until(k, sp, n_end + 3)
            k.issued = n_end + RING

        @block.vector
        def _(v):
            gate = k.mod[:, layer, 5]
            for c in range(DC):
                nc.vector.scalar_tensor_tensor(k.x[:, c, 0:TP], acc[:, c, 0:TP], gate[:, c, 0:1], k.x[:, c, 0:TP],
                                               ALU.mult, ALU.add)
            k.dve.link(v, nc.vector.tensor_tensor(keep_small, acc[:, :, TP:T], gate[:, :, 1:NCOND], ALU.mult))
            nc.vector.tensor_tensor(k.x[:, :, TP:T], keep_small, k.x[:, :, TP:T], ALU.add)



_INS = ["x_prompt", "x_sample", "state_ret", "state_gla", "c_prompt", "c_sample", "ret_w_in", "ret_norm_g",
        "ret_w_out", "gla_w_in", "gla_w_a1", "gla_w_a2", "gla_b_a", "gla_norm_g", "gla_w_out", "ada_w", "ada_b",
        "norm_mix_g", "norm_ffn_g", "moe_w_router", "moe_router_bias", "moe_w_gate", "moe_w_up", "moe_w_down",
        "sh_w_gate", "sh_w_up", "sh_w_down", "final_norm_g"]
_OUTS = [("y_prompt", (1, TP, D)), ("y_sample", (NS, 1, D)), ("ret_prompt", (1, 1, RH, RDK, RDV)),
         ("gla_prompt", (1, 1, GH, GDK, GDV)), ("ret_sample", (1, NS, RH, RDK, RDV)),
         ("gla_sample", (1, NS, GH, GDK, GDV))]


def kernel(**inputs):
    import concourse.bacc as bacc
    from concourse.bass_utils import run_bass_kernel_spmd

    nc = bacc.Bacc("TRN2", target_bir_lowering=False, num_devices=1)
    arrays, inp, out = {}, {}, {}
    for name in _INS + ["tables"]:
        a = np.ascontiguousarray(tables() if name == "tables" else inputs[name])
        arrays[f"in_{name}"] = a
        inp[name] = nc.dram_tensor(f"in_{name}", a.shape, mybir.dt.from_np(a.dtype), kind="ExternalInput").ap()
    for name, shape in _OUTS:
        out[name] = nc.dram_tensor(f"out_{name}", shape, F32, kind="ExternalOutput").ap()
    build(nc, inp, out)
    r = run_bass_kernel_spmd(nc, [arrays], core_ids=[0])
    return tuple(r.results[0][f"out_{name}"] for name, _ in _OUTS)
```

```python
import concourse.bass as bass
import numpy as np
from concourse import mybir
from contextlib import ExitStack

F32 = mybir.dt.float32
BF16 = mybir.dt.bfloat16
I32 = mybir.dt.int32
ALU = mybir.AluOpType
ACT = mybir.ActivationFunctionType
AX = mybir.AxisListType

P = 128
D = 1024
DC = D // P
TP = 256
NS = 8
T = TP + NS
NCOND = 1 + NS
DEPTH = 2
PAST = 2048
EPS = 1e-6

RH, RDK, RDV = 4, 256, 512
GH, GDK, GDV = 4, 128, 256
RANK = 16
TAU = 16.0

NE, TOPK, NG, TOPG = 64, 8, 8, 4
DE = D // 4
FC = DE // P
SCALE = 2.5
CAP = 64
XB = (T * TOPK - 1) // CAP
XPAIRS = (XB + 1) // 2
assert XB % 2 == 0
TT = 3
TOKENS = [(0, P), (P, P), (TP, NS)]
COPY, COPIES = 32, 96

RING = 12
SLOT = 2048
EPI = 4
ROUNDS = NE // EPI

TAB = {}
_at = 0
for _name, _w in (("cos", T), ("sin", T), ("decay", RH * TP), ("kdec", 2 * RH), ("causal", P), ("ident", P),
                  ("before", P), ("before_sample", P), ("ones", P), ("pick", NS), ("own", 6), ("gtri", NG * NG),
                  ("iota", NE), ("valid", TT)):
    TAB[_name] = (_at, _at + _w)
    _at += _w
TABW = _at


def tables():
    t = np.zeros((P, TABW), np.float32)

    def put(name, a):
        a0, a1 = TAB[name]
        t[:, a0:a1] = np.asarray(a, np.float32).reshape(P, a1 - a0)

    half = RDK // 2
    inv = (np.float32(10000.0) ** (-np.arange(half, dtype=np.float32) / np.float32(half))).astype(np.float32)
    pos = np.concatenate([np.arange(TP), np.full(NS, PAST)]).astype(np.float32)
    ang = inv[:, None] * pos[None, :]
    put("cos", np.cos(ang.astype(np.float64)))
    put("sin", np.sin(ang.astype(np.float64)))
    lg = np.log1p(-np.power(2.0, -5.0 - np.arange(RH)))
    i, j = np.arange(TP)[None, :], np.arange(P)[:, None]
    put("decay", np.stack([np.where(i >= j, np.exp(lg[h] * (i - j)), 0.0) for h in range(RH)], 1))
    jj = np.arange(TP).reshape(2, P).T
    put("kdec", np.stack([np.exp(lg[h] * (TP - 1 - jj)) for h in range(RH)], 2))
    q, r = np.arange(P)[:, None], np.arange(P)[None, :]
    put("causal", q <= r)
    put("ident", q == r)
    put("before", q < r)
    put("before_sample", (q < r % COPY) & (q < NS))
    put("ones", np.ones((P, P)))
    put("pick", np.arange(P)[:, None] % COPY == np.arange(NS)[None, :])
    put("own", np.arange(6)[None, :] // 3 == np.arange(P)[:, None] // CAP)
    g = np.arange(NG)
    put("gtri", np.tile((g[None, :] < g[:, None]).reshape(1, -1), (P, 1)))
    put("iota", np.tile(np.arange(NE)[None], (P, 1)))
    put("valid", np.stack([np.arange(P) < n for _, n in TOKENS[:2]]
                          + [(np.arange(P) % COPY < NS) & (np.arange(P) < COPIES)], 1))
    return t


GAMMA = [float(1.0 - 2.0 ** (-5.0 - h)) for h in range(RH)]


class Chain:

    def __init__(self, sem):
        self.sem, self.n = sem, 0

    def link(self, eng, ins):
        self.n += 1
        ins.then_inc(self.sem, 1)
        eng.wait_ge(self.sem, self.n)


class Core:
    pass


def build(nc, inp, out):
    ctx = ExitStack()
    with ctx:
        k = Core()
        k.nc, k.inp, k.out = nc, inp, out

        def sb(name, cols, dt=F32, parts=P):
            return ctx.enter_context(nc.sbuf_tensor(name, [parts, cols], dt))

        k.persistent = [nc.alloc_semaphore(name=n) for n in
                        [f"ring_full{s}" for s in range(RING)] + [f"ring_free{s}" for s in range(RING)]
                        + ["vector_step"]]
        k.stored = {n: nc.alloc_semaphore(name=n) for n in
                    ["ret_state_stored"] + [f"ret_sample_state_stored{b}" for b in range(8)]
                    + ["gla_state_stored"] + [f"gla_sample_state_stored{b}" for b in range(2)]}
        k.mine = []
        k.pending = None
        k.sem = lambda name: k.mine.append(nc.alloc_semaphore(name=name)) or k.mine[-1]
        k.ring = sb("ring", RING * SLOT)
        k.tab = sb("tab", TABW)
        k.x = sb("xT", DC * T)[:, :].rearrange("p (c t) -> p c t", c=DC)
        k.h = sb("hT", DC * T)[:, :].rearrange("p (c t) -> p c t", c=DC)
        k.mod = sb("mod", DEPTH * 48 * NCOND)[:, :].rearrange("p (l g c s) -> p l g c s", l=DEPTH, g=6, c=DC)
        k.gain = sb("gain", DEPTH * 2 * DC * NCOND)[:, :].rearrange("p (l n c s) -> p l n c s", l=DEPTH, n=2, c=DC)
        k.vec = sb("vec", 164)
        k.rstd = sb("rstd", RH * T)
        k.size = 19344
        k.scratch = sb("scratch", k.size)
        k.ident16 = sb("ident16", P, BF16)
        k.pick16 = sb("pick16", NS, BF16)
        k.condT = sb("condT", DC * 32)[:, :].rearrange("p (c s) -> p c s", c=DC)
        k.ps = ctx.enter_context(nc.psum_tensor("ps", [P, 8, 512], F32))

        k.const = lambda name: k.tab[:, TAB[name][0]:TAB[name][1]]
        k.ident = k.const("ident")
        k.ones = k.const("ones")
        k.ada_b = k.vec[:, 0:96].rearrange("p (l g c) -> p l g c", l=DEPTH, g=6)
        k.norm_g = k.vec[:, 96:128].rearrange("p (n l c) -> p l n c", n=2, l=DEPTH)
        k.ret_g = k.vec[:, 128:144]
        k.gla_g = k.vec[:, 144:152]
        k.fin_g = k.vec[:, 152:160]
        k.b_a = k.vec[:, 160:164]

        k.ring_full, k.ring_free = k.persistent[0:RING], k.persistent[RING:2 * RING]
        k.plan, k.issued = plan_loads(inp), 0
        k.stage, k.places = {}, {}
        for n, (what, _) in enumerate(k.plan):
            k.stage.setdefault(what, n)
            k.places.setdefault(what, []).append(n)
        k.dve = Chain(k.persistent[2 * RING])

        setup(k)
        conditioning(k)
        norm(k, 0, 0)
        retention(k)
        experts(k, 0)
        reuse_semaphores(k)
        gla(k)
        experts(k, 1)
        final(k)


def reuse_semaphores(k):
    nc = k.nc
    with nc.Block() as block:
        @block.gpsimd
        def _(pool):
            for s in k.mine:
                pool.sem_clear(s)
    for s in k.mine:
        nc.release_semaphore(s)
    k.mine.clear()



def plan_loads(inp):
    plan = []

    def columns(what, w, width, order="(k p) n -> p k n"):
        kc, n = w.shape[0] // P, w.shape[1] // width
        for j in range(n):
            plan.append((what, w[:, j * width:(j + 1) * width].rearrange(order, k=kc)))

    def moe(layer):
        what = f"shared{layer}"
        for name in ("sh_w_gate", "sh_w_up", "sh_w_down"):
            w = inp[name][layer]
            plan.append((what, w.rearrange("(k p) n -> p k n", p=P)))
        for r in range(ROUNDS):
            for name, e in ROUND:
                plan.append((f"moe{layer}", inp[name][layer][r * EPI + e].rearrange(rows_of(name).format("p"), p=P)))

    for layer in range(DEPTH):
        columns("ada", inp["ada_w"][layer], 256, "(p k) n -> p k n")
    later = plan[4 * FIRST:]
    del plan[4 * FIRST:]
    columns("ret_in", inp["ret_w_in"][0], 256)
    projections = plan[4 * FIRST:]
    del plan[4 * FIRST:]
    for t, item in enumerate(projections):
        plan.append(item)
        if t in AFTER:
            plan += later[4 * AFTER.index(t):4 * AFTER.index(t) + 4]
    columns("ret_out", inp["ret_w_out"][0], 128)
    moe(0)
    columns("gla_in", inp["gla_w_in"][0], 256)
    columns("gla_out", inp["gla_w_out"][0], 256)
    moe(1)
    return plan


FIRST = 2
AFTER = [1, 2, 4, 5, 7, 8, 10, 11, 13, 14]
assert FIRST + len(AFTER) == DEPTH * 6
ROUND = [(n, e) for e in range(EPI) for n in ("moe_w_gate", "moe_w_up")] + [("moe_w_down", e) for e in range(EPI)]
PLACE = {ne: i for i, ne in enumerate(ROUND)}


def rows_of(name):
    return "(k p) n -> {} k n" if name == "moe_w_down" else "(p k) n -> {} k n"


def slot(k, n, inner):
    s = n % RING
    return k.ring[:, s * SLOT:(s + 1) * SLOT].rearrange("p (k n) -> p k n", n=inner)


def load_until(k, sp, last):
    while k.issued < min(last, len(k.plan)):
        n = k.issued
        src = k.plan[n][1]
        if n >= RING:
            sp.wait_ge(k.ring_free[n % RING], n // RING)
        sp.dma_start(slot(k, n, src.shape[2]), src).then_inc(k.ring_full[n % RING], 16)
        k.issued += 1


def load_skipped(k, sp):
    issued, (k.issued, last) = k.issued, k.skipped
    load_until(k, sp, last)
    k.issued = issued


def wait_slot(k, pe, n):
    pe.wait_ge(k.ring_full[n % RING], 16 * (n // RING + 1))


def wait_used(k, eng, n):
    eng.wait_ge(k.ring_free[n % RING], n // RING + 1)



def setup(k):
    nc, inp = k.nc, k.inp
    s_tab, s_in, s_cond = k.sem("tables_loaded"), k.sem("inputs_loaded"), k.sem("cond_loaded")
    s_silu, s_tr, s_cp = k.sem("cond_silu"), k.sem("inputs_transposed"), k.sem("transposed_copied")
    sc = k.scratch
    xn = sc[:, 0:TT * D].rearrange("p (t d) -> p t d", t=TT)
    vn = sc[:, 3072:3072 + 2 * P].rearrange("p (t d) -> p t d", t=2)
    cn = sc[0:NCOND, 3400:3400 + D]
    cn_c = cn.rearrange("s (q c) -> s q c", c=DC)
    with nc.Block() as block:
        @block.sync
        def _(sp):
            sp.dma_start(k.tab[:, :], inp["tables"]).then_inc(s_tab, 16)
            sp.dma_start(cn[0:1, :], inp["c_prompt"]).then_inc(s_cond, 16)
            sp.dma_start(cn[1:NCOND, :], inp["c_sample"]).then_inc(s_cond, 16)
            for t, (t0, n) in enumerate(TOKENS):
                src = inp["x_prompt"][0, t0:t0 + n] if t < 2 else inp["x_sample"].rearrange("b o d -> (b o) d")
                sp.dma_start(xn[0:n, t, :], src).then_inc(s_in, 16)
            at = 0
            for name, rows in (("ada_b", 96), ("norm_mix_g", 16), ("norm_ffn_g", 16), ("ret_norm_g", 16),
                               ("gla_norm_g", 8), ("final_norm_g", 8), ("gla_b_a", 4)):
                src = inp[name]
                src = (src.rearrange("(r p) -> r p", p=P) if len(src.shape) == 1
                       else src.rearrange("l (r p) -> (l r) p", p=P))
                sp.dma_start(vn[at % P:at % P + rows, at // P, :], src).then_inc(s_in, 16)
                at += rows
            load_until(k, sp, RING)

        @block.scalar
        def _(act):
            act.wait_ge(s_cond, 32)
            nc.scalar.activation(cn, cn, ACT.Silu).then_inc(s_silu, 1)

        @block.tensor
        def _(pe):
            pe.wait_ge(s_tab, 16)
            pe.wait_ge(s_silu, 1)
            for c in range(DC):
                mm = nc.tensor.transpose(k.ps[:, 0, c * NCOND:(c + 1) * NCOND], cn_c[:, :, c],
                                         k.ident[0:NCOND, 0:NCOND])
            mm.then_inc(s_tr, 1)
            pe.wait_ge(s_in, 16 * 10)
            for t, rows in ((0, 128), (1, 36)):
                mm = nc.tensor.transpose(k.ps[:, 1, t * P:t * P + rows], vn[0:rows, t, :], k.ident[0:rows, 0:rows])
            mm.then_inc(s_tr, 1)
            for c in range(DC):
                if c >= 2:
                    pe.wait_ge(s_cp, c - 2 + 1 + 2)
                for t, (t0, n) in enumerate(TOKENS):
                    mm = nc.tensor.transpose(k.ps[:, 2 + c % 2, t0:t0 + n], xn[0:n, t, c * P:(c + 1) * P],
                                             k.ident[0:n, 0:n])
                mm.then_inc(s_tr, 1)

        @block.vector
        def _(v):
            k.dve.link(v, nc.vector.memset(k.condT, 0.0))
            v.wait_ge(s_tab, 16)
            nc.vector.tensor_copy(k.ident16[:, :], k.ident)
            nc.vector.tensor_copy(k.pick16[:, :], k.const("pick"))
            v.wait_ge(s_tr, 1)
            nc.vector.tensor_copy(k.condT[:, :, 0:NCOND], k.ps[:, 0, 0:DC * NCOND].rearrange("p (c s) -> p c s", c=DC))\
                .then_inc(s_cp, 1)
            v.wait_ge(s_tr, 2)
            nc.vector.tensor_copy(k.vec[:, :], k.ps[:, 1, 0:164]).then_inc(s_cp, 1)
            for c in range(DC):
                v.wait_ge(s_tr, 3 + c)
                nc.vector.tensor_copy(k.x[:, c, :], k.ps[:, 2 + c % 2, 0:T]).then_inc(s_cp, 1)



def cond_products(k, pe, out, loads):
    for c in range(DC):
        for j, n in enumerate(loads):
            mm = k.nc.tensor.matmul(out[32 * j:32 * j + 32, 0:256], k.condT[:, c, :],
                                    slot(k, n, 256)[:, c, :], start=(c == 0), stop=(c == DC - 1))
            if c == DC - 1:
                mm.then_inc(k.ring_free[n % RING], 1)


def cond_transpose(k, out, rows):
    for m in range(2):
        mm = k.nc.tensor.transpose(out[:, m * P:(m + 1) * P], rows[:, m * P:(m + 1) * P], k.ident)
    return mm


def cond_store(k, layer, group, src):
    mod = k.mod[:, layer].rearrange("p g c s -> p (g c) s")
    bias = k.ada_b[:, layer].rearrange("p g c -> p (g c)")
    to = bass.ds(group * 8, 8)
    src = src[:, 0:256].rearrange("p (m j s) -> p j m s", m=2, j=4)[:, :, :, 0:NCOND]
    return k.nc.vector.tensor_tensor(mod[:, to, :].rearrange("p (j m) s -> p j m s", m=2), src,
                                     bias[:, to].rearrange("p (j m) -> p j m", m=2).unsqueeze(3)
                                     .to_broadcast([P, 4, 2, NCOND]), ALU.add)


def cond_gains(k, layer, n):
    g = k.norm_g[:, layer, n, :].unsqueeze(2).to_broadcast([P, DC, NCOND])
    return k.nc.vector.scalar_tensor_tensor(k.gain[:, layer, n], k.mod[:, layer, 3 * n + 1], 1.0, g, ALU.add, ALU.mult)


def conditioning(k):
    nc = k.nc
    s_row, s_tr, s_out = (k.sem(f"mod_{n}") for n in ("rows_out", "transposed", "out"))
    rows = k.scratch[:, 6000:6000 + FIRST * 256].rearrange("p (g n) -> p g n", g=FIRST)
    groups = [k.places["ada"][4 * g:4 * g + 4] for g in range(FIRST)]
    with nc.Block() as block:
        @block.sync
        def _(sp):
            load_until(k, sp, 4 * FIRST + RING)

        @block.tensor
        def _(pe):
            for g in range(FIRST):
                for n in groups[g]:
                    wait_slot(k, pe, n)
                cond_products(k, pe, k.ps[:, g], groups[g])
            for g in range(FIRST):
                pe.wait_ge(s_row, g + 1)
                cond_transpose(k, k.ps[:, 4 + g], rows[:, g]).then_inc(s_tr, 1)

        @block.scalar
        def _(act):
            for g in range(FIRST):
                for n in groups[g]:
                    wait_used(k, act, n)
                nc.scalar.copy(rows[:, g], k.ps[:, g, 0:256]).then_inc(s_row, 1)

        @block.vector
        def _(v):
            for g in range(FIRST):
                v.wait_ge(s_tr, g + 1)
                cond_store(k, 0, g, k.ps[:, 4 + g]).then_inc(s_out, 1)
            v.wait_ge(s_out, FIRST)
            k.dve.link(v, cond_gains(k, 0, 0))



def norm(k, layer, which, fetch=None):
    nc = k.nc
    tag = f"{layer}{which}"
    s_sq, s_sum, s_ms, s_rt = (k.sem(f"norm{tag}_{n}") for n in ("squared", "summed", "meansq", "root"))
    s_prod = k.sem(f"norm{tag}_scaled")
    sq = k.scratch[:, 0:DC * T].rearrange("p (c t) -> p c t", c=DC)
    tmp = k.scratch[:, DC * T:DC * T + T]
    root = k.scratch[:, DC * T + T:DC * T + 2 * T]
    rstd = k.rstd[:, 0:T]
    final_norm = layer == DEPTH
    pending, k.pending = k.pending, None
    s_new = k.sem(f"norm{tag}_experts_added")

    with nc.Block() as block:
        @block.sync
        def _(sp):
            if fetch:
                fetch(sp)
            if pending:
                load_skipped(k, sp)

        @block.scalar
        def _(act):
            for c in range(DC):
                if pending:
                    act.wait_ge(s_new, c + 2)
                nc.scalar.activation(sq[:, c, :], k.x[:, c, :], ACT.Square).then_inc(s_sq, 1)
            act.wait_ge(s_ms, 1)
            nc.scalar.activation(root, tmp, ACT.Sqrt).then_inc(s_rt, 1)
            if not final_norm:
                for c in range(DC):
                    act.wait_ge(s_prod, c + 1)
                    nc.scalar.activation(k.h[:, c, 0:TP], k.h[:, c, 0:TP], ACT.Identity,
                                         bias=k.mod[:, layer, 3 * which, c, 0:1])

        @block.tensor
        def _(pe):
            for c in range(DC):
                pe.wait_ge(s_sq, c + 1)
                mm = nc.tensor.matmul(k.ps[:, 0, 0:T], k.ones, sq[:, c, :], start=(c == 0), stop=(c == DC - 1))
            mm.then_inc(s_sum, 1)

        @block.vector
        def _(v):
            if pending:
                acc, gate, small = pending
                k.dve.link(v, nc.vector.tensor_tensor(small, acc[:, :, TP:T], gate[:, :, 1:NCOND], ALU.mult))
                nc.vector.tensor_tensor(k.x[:, :, TP:T], small, k.x[:, :, TP:T], ALU.add).then_inc(s_new, 1)
                for c in range(DC):
                    nc.vector.scalar_tensor_tensor(k.x[:, c, 0:TP], acc[:, c, 0:TP], gate[:, c, 0:1], k.x[:, c, 0:TP],
                                                   ALU.mult, ALU.add).then_inc(s_new, 1)
                v.wait_ge(s_new, DC + 1)
            v.wait_ge(s_sum, 1)
            nc.vector.tensor_scalar(tmp, k.ps[:, 0, 0:T], 1.0 / D, EPS, ALU.mult, ALU.add).then_inc(s_ms, 1)
            v.wait_ge(s_rt, 1)
            k.dve.link(v, nc.vector.reciprocal(rstd, root))
            if final_norm:
                for c in range(DC):
                    nc.vector.scalar_tensor_tensor(k.h[:, c, :], k.x[:, c, :], k.fin_g[:, c:c + 1], rstd,
                                                   ALU.mult, ALU.mult)
                return
            for c in range(DC):
                nc.vector.scalar_tensor_tensor(k.h[:, c, 0:TP], k.x[:, c, 0:TP], k.gain[:, layer, which, c, 0:1],
                                               rstd[:, 0:TP], ALU.mult, ALU.mult).then_inc(s_prod, 1)
            hs = k.h[:, :, TP:T]
            rs = rstd[:, TP:T].unsqueeze(1).to_broadcast([P, DC, NS])
            k.dve.link(v, nc.vector.tensor_tensor(hs, k.x[:, :, TP:T], rs, ALU.mult))
            k.dve.link(v, nc.vector.tensor_tensor(hs, hs, k.gain[:, layer, which, :, 1:NCOND], ALU.mult))
            nc.vector.tensor_tensor(hs, hs, k.mod[:, layer, 3 * which, :, 1:NCOND], ALU.add)


def add_gated(k, v, chunk, psum, gate, tmp):
    nc = k.nc
    nc.vector.scalar_tensor_tensor(k.x[:, chunk, 0:TP], psum[:, 0:TP], gate[:, chunk, 0:1], k.x[:, chunk, 0:TP],
                                   ALU.mult, ALU.add)
    k.dve.link(v, nc.vector.tensor_tensor(tmp, psum[:, TP:T], gate[:, chunk, 1:NCOND], ALU.mult))
    return nc.vector.tensor_tensor(k.x[:, chunk, TP:T], tmp, k.x[:, chunk, TP:T], ALU.add)


def spread_samples(k, v, dst, src, chunks):
    k.dve.link(v, k.nc.vector.memset(dst, 0.0))
    return k.nc.vector.tensor_copy(dst.rearrange("p c (s n) -> p c s n", s=3)[:, :, :, 0:NS],
                                   src.unsqueeze(2).to_broadcast([P, chunks, 3, NS]))


def split_rows(k, v, dst, src, rest, mid):
    mid_rows, low_rows = slice(COPY, 2 * COPY), slice(2 * COPY, 3 * COPY)
    k.dve.link(v, k.nc.vector.tensor_tensor(rest[0:COPIES], src[0:COPIES], dst[0:COPIES], ALU.subtract))
    k.nc.vector.tensor_copy(dst[mid_rows], rest[mid_rows])
    k.dve.link(v, k.nc.vector.tensor_copy(mid[low_rows], rest[low_rows]))
    return k.nc.vector.tensor_tensor(dst[low_rows], rest[low_rows], mid[low_rows], ALU.subtract)



def retention(k):
    nc, inp, out = k.nc, k.inp, k.out
    sc = k.scratch
    at = [0]

    def area(cols):
        at[0] += cols
        assert at[0] <= k.size
        return sc[:, at[0] - cols:at[0]]

    vo = area(16 * T).rearrange("p (c t) -> p c t", c=16)
    vs = area(1024).bitcast(BF16)
    qs = area(DC * NS).rearrange("p (c s) -> p c s", c=DC)
    ks = area(DC * NS).rearrange("p (c s) -> p c s", c=DC)
    here = at[0]
    q = area(DC * T).rearrange("p (c t) -> p c t", c=DC)
    kk = area(DC * T).rearrange("p (c t) -> p c t", c=DC)
    vn = area(2 * 1024).rearrange("p (b j n) -> p b j n", b=2, j=2)
    kn = area(2 * 512).rearrange("p (b j n) -> p b j n", b=2, j=2)
    att = area(384)
    sp_ = area(2 * 1024).rearrange("p (b c n) -> p b c n", b=2, c=2)
    tmp = area(4 * T).rearrange("p (b t) -> p b t", b=4)
    v3 = area(16 * COPIES).rearrange("p (c s) -> p c s", c=16)
    v_rest = area(512)
    v_mid = area(256).bitcast(BF16)
    cond_rows = area(2 * 256).rearrange("p (b n) -> p b n", b=2)
    at[0] = here
    gate = area(16 * T).rearrange("p (c t) -> p c t", c=16)
    st = area(8 * 1024).rearrange("p (b c n) -> p b c n", b=8, c=2)
    qz = area(DC * NS * NS)
    n_in, n_out = k.stage["ret_in"], k.stage["ret_out"]
    cos, sin = k.const("cos"), k.const("sin")

    s_rot, s_vc = k.sem("ret_rotated"), k.sem("ret_values_copied")
    s_row, s_crt, s_mod = k.sem("mod_later_rows_out"), k.sem("mod_later_transposed"), k.sem("mod_later_out")
    loads = k.places["ret_in"]
    groups = [k.places["ada"][4 * g:4 * g + 4] for g in range(FIRST, DEPTH * 6)]
    with nc.Block() as block:
        @block.sync
        def _(sp):
            load_until(k, sp, loads[16] + RING)

        @block.tensor
        def _(pe):
            for t in range(16):
                wait_slot(k, pe, loads[t])
                if 2 <= t < 10:
                    pe.wait_ge(s_rot, t - 1)
                elif t >= 10:
                    pe.wait_ge(s_vc, t - 9)
                w = slot(k, loads[t], 256)
                for m in range(2):
                    for c in range(DC):
                        mm = nc.tensor.matmul(k.ps[:, 2 * (t % 2) + m, 0:T], w[:, c, m * P:(m + 1) * P], k.h[:, c, :],
                                              start=(c == 0), stop=(c == DC - 1))
                mm.then_inc(k.ring_free[loads[t] % RING], 1)
                if t - 1 in AFTER:
                    g = AFTER.index(t - 1)
                    pe.wait_ge(s_row, g + 1)
                    if g >= 2:
                        pe.wait_ge(s_mod, g - 1)
                    cond_transpose(k, k.ps[:, 6 + g % 2], cond_rows[:, g % 2]).then_inc(s_crt, 1)
                if t in AFTER:
                    g = AFTER.index(t)
                    for n in groups[g]:
                        wait_slot(k, pe, n)
                    if g >= 2:
                        pe.wait_ge(s_row, g - 1)
                    cond_products(k, pe, k.ps[:, 4 + g % 2], groups[g])

        @block.vector
        def _(v):
            for t in range(16):
                if t - 1 in AFTER:
                    g = AFTER.index(t - 1)
                    v.wait_ge(s_crt, g + 1)
                    cond_store(k, (FIRST + g) // 6, (FIRST + g) % 6, k.ps[:, 6 + g % 2]).then_inc(s_mod, 1)
                if t >= 8:
                    continue
                wait_used(k, v, loads[t])
                dst, scale = (q, 1.0) if t < 4 else (kk, RDK ** -0.5)
                h = t % 4
                x1, x2 = k.ps[:, 2 * (t % 2), 0:T], k.ps[:, 2 * (t % 2) + 1, 0:T]
                for j, (a, b) in enumerate(((x1, cos), (x2, sin), (x1, sin), (x2, cos))):
                    ins = nc.vector.scalar_tensor_tensor(tmp[:, j], a, scale, b, ALU.mult, ALU.mult)
                ins.then_inc(s_rot, 1)
                v.wait_ge(s_rot, t + 1)
                nc.vector.tensor_tensor(dst[:, 2 * h], tmp[:, 0], tmp[:, 1], ALU.subtract)
                k.dve.link(v, nc.vector.tensor_tensor(dst[:, 2 * h + 1], tmp[:, 2], tmp[:, 3], ALU.add))
            v.wait_ge(s_mod, len(AFTER))
            for layer, n in ((0, 1), (1, 0), (1, 1)):
                cond_gains(k, layer, n)

        @block.scalar
        def _(act):
            for t in range(16):
                if t >= 8:
                    wait_used(k, act, loads[t])
                    for m in range(2):
                        ins = nc.scalar.copy(vo[:, 2 * (t - 8) + m], k.ps[:, 2 * (t % 2) + m, 0:T])
                    ins.then_inc(s_vc, 1)
                if t in AFTER:
                    g = AFTER.index(t)
                    for n in groups[g]:
                        wait_used(k, act, n)
                    if g >= 2:
                        act.wait_ge(s_crt, g - 1)
                    nc.scalar.copy(cond_rows[:, g % 2], k.ps[:, 4 + g % 2, 0:256]).then_inc(s_row, 1)

    tr, trs, s_at, s_o, s_st = (k.sem(f"ret_{n}") for n in ("tokens_first", "keys_first", "scores", "heads", "state"))
    c_v, c_k, c_at, c_o, c_st = (k.sem(f"ret_{n}") for n in (
        "values_out", "keys_out", "scores_out", "heads_out", "state_out"))
    s_v3 = k.sem("ret_sample_values_split")
    c_out = k.stored["ret_state_stored"]
    with nc.Block() as block:
        @block.tensor
        def _(pe):
            for h in range(RH):
                b = h % 2
                if h:
                    pe.wait_ge(c_v, h)
                for j in range(2):
                    for c in range(4):
                        mm = nc.tensor.transpose(k.ps[:, j, c * P:(c + 1) * P], vo[:, 4 * h + c, j * P:(j + 1) * P],
                                                 k.ident)
                pe.wait_ge(s_v3, h + 1)
                for c in range(4):
                    mm = nc.tensor.transpose(k.ps[0:COPIES, 3, c * P:(c + 1) * P], v3[:, 4 * h + c, :], k.ident)
                mm.then_inc(tr, 1)
                if h:
                    pe.wait_ge(c_k, h)
                for j in range(2):
                    for c in range(2):
                        mm = nc.tensor.transpose(k.ps[:, 2, (2 * j + c) * P:(2 * j + c + 1) * P],
                                                 kk[:, 2 * h + c, j * P:(j + 1) * P], k.ident)
                mm.then_inc(trs, 1)
                if h:
                    pe.wait_ge(c_at, h)
                for j in range(2):
                    for c in range(2):
                        mm = nc.tensor.matmul(k.ps[:, 4, j * TP:j * TP + TP - j * P],
                                              kk[:, 2 * h + c, j * P:(j + 1) * P], q[:, 2 * h + c, j * P:TP],
                                              start=(c == 0), stop=(c == 1))
                mm.then_inc(s_at, 1)
                pe.wait_ge(c_v, h + 1)
                pe.wait_ge(c_k, h + 1)
                if h:
                    pe.wait_ge(c_st, 2 * h - 1)
                for c in range(2):
                    if c:
                        pe.wait_ge(c_st, 2 * h + 1)
                    for j in range(2):
                        mm = nc.tensor.matmul(k.ps[:, 7, :], kn[:, b, j, c * P:(c + 1) * P], vn[:, b, j, :],
                                              start=(j == 0), stop=(j == 1))
                    mm.then_inc(s_st, 1)
                    if c == 0:
                        pe.wait_ge(c_at, h + 1)
                        if h:
                            pe.wait_ge(c_o, h)
                        for cc in range(4):
                            o = k.ps[:, 5 + cc // 2, (cc % 2) * TP:(cc % 2 + 1) * TP]
                            nc.tensor.matmul(o, vn[:, b, 0, cc * P:(cc + 1) * P], att[:, 0:TP], start=True, stop=False)
                            mm = nc.tensor.matmul(o[:, P:TP], vn[:, b, 1, cc * P:(cc + 1) * P], att[:, TP:TP + P],
                                                  start=False, stop=True)
                        mm.then_inc(s_o, 1)

        @block.scalar
        def _(act):
            for h in range(RH):
                act.wait_ge(tr, h + 1)
                if h >= 2:
                    act.wait_ge(s_st, 2 * h - 2)
                for j in range(2):
                    nc.scalar.copy(vn[:, h % 2, j, :], k.ps[:, j, :])
                nc.scalar.copy(vs[0:COPIES, h * RDV:(h + 1) * RDV], k.ps[0:COPIES, 3, :]).then_inc(c_v, 1)
                act.wait_ge(s_o, h + 1)
                for c in range(2):
                    ins = nc.scalar.copy(vo[:, 4 * h + 2 * c:4 * h + 2 * c + 2, 0:TP],
                                         k.ps[:, 5 + c, :].rearrange("p (c t) -> p c t", c=2))
                ins.then_inc(c_o, 1)

        @block.vector
        def _(v):
            spread_samples(k, v, v3, vo[:, :, TP:T], 16).then_inc(s_v3, 1)
            nc.vector.tensor_copy(qs, q[:, :, TP:T])
            nc.vector.tensor_copy(ks, kk[:, :, TP:T])
            for h in range(RH):
                v.wait_ge(trs, h + 1)
                if h >= 2:
                    v.wait_ge(s_st, 2 * h - 2)
                for j in range(2):
                    ins = nc.vector.tensor_scalar(kn[:, h % 2, j, :], k.ps[:, 2, j * TP:(j + 1) * TP],
                                                  k.const("kdec")[:, j * RH + h:j * RH + h + 1], None, ALU.mult)
                ins.then_inc(c_k, 1)
                v.wait_ge(s_at, h + 1)
                if h:
                    v.wait_ge(s_o, h)
                dec = k.const("decay")[:, h * TP:(h + 1) * TP]
                nc.vector.tensor_tensor(att[:, 0:TP], k.ps[:, 4, 0:TP], dec, ALU.mult)
                nc.vector.tensor_tensor(att[:, TP:TP + P], k.ps[:, 4, TP:TP + P], dec[:, 0:P],
                                        ALU.mult).then_inc(c_at, 1)
                v.wait_ge(c_v, h + 1)
                split_rows(k, v, vs[:, h * RDV:(h + 1) * RDV], k.ps[:, 3, :], v_rest, v_mid).then_inc(s_v3, 1)
                v.wait_ge(s_v3, h + 2)
                for c in range(2):
                    v.wait_ge(s_st, 2 * h + c + 1)
                    if h >= 2 and c == 0:
                        v.wait_ge(c_out, 16 * (h - 1))
                    nc.vector.tensor_copy(sp_[:, h % 2, c, :], k.ps[:, 7, :]).then_inc(c_st, 1)

        @block.gpsimd
        def _(pool):
            for h in range(RH):
                pool.wait_ge(c_st, 2 * h + 2)
                pool.dma_start(out["ret_prompt"][0, 0, h].rearrange("(c p) n -> p c n", p=P),
                               sp_[:, h % 2]).then_inc(c_out, 16)
                pool.wait_ge(c_out, 16 * (h + 1))

    s_bc, s_out, s_new, s_q, s_sil, s_cm, s_or, s_ot = (k.sem(f"ret_sample_{n}") for n in (
        "values_spread", "outer", "state_new", "read", "gate_silu", "compacted", "rows_out", "rows_transposed"))
    s_ldb = [k.sem(f"ret_sample_state_loaded{b}") for b in range(8)]
    s_stb = [k.stored[f"ret_sample_state_stored{b}"] for b in range(8)]
    units = [(b, h) for b in range(NS) for h in range(RH)]
    n_gate = loads[16]
    outer = k.rstd[:, 0:1024].rearrange("p (b n) -> p b n", b=2)
    orow = k.rstd[:, 0:512]
    qz4 = qz.rearrange("p (c b s) -> p c b s", c=DC, b=NS)
    with nc.Block() as block:
        @block.sync
        def _(sp):
            for u, (b, h) in enumerate(units):
                if u >= 8:
                    sp.wait_ge(s_stb[u % 8], 16 * (u // 8))
                    sp.wait_ge(s_q, (u - 8) // RH + 1)
                sp.dma_start(st[:, u % 8], inp["state_ret"][0, b, h].rearrange("(c p) n -> p c n", p=P))\
                    .then_inc(s_ldb[u % 8], 16)

        @block.gpsimd
        def _(pool):
            for u, (b, h) in enumerate(units):
                pool.wait_ge(s_new, 2 * u + 2)
                pool.dma_start(out["ret_sample"][0, b, h].rearrange("(c p) n -> p c n", p=P), st[:, u % 8])\
                    .then_inc(s_stb[u % 8], 16)
            for b in range(8):
                pool.wait_ge(s_stb[b], 16 * len(units) // 8)

        @block.tensor
        def _(pe):
            def read(b):
                for h in range(RH):
                    pe.wait_ge(s_new, 2 * (RH * b + h) + 2)
                for c in range(2):
                    for h in range(RH):
                        mm = nc.tensor.matmul(k.ps[32 * h:32 * h + NS, 2, :], qz4[:, 2 * h + c, b, :],
                                              st[:, (RH * b + h) % 8, c, :], start=(b == 0 and c == 0),
                                              stop=(b == NS - 1 and c == 1))
                mm.then_inc(s_q, 1)

            for u, (b, h) in enumerate(units):
                if u >= 2:
                    pe.wait_ge(s_out, 2 * (u - 1))
                nc.tensor.matmul(k.ps[:, u % 2, :], k.pick16[0:COPIES, b:b + 1].to_broadcast([COPIES, P]),
                                 vs[0:COPIES, h * RDV:(h + 1) * RDV], start=True, stop=True).then_inc(s_bc, 1)
                if u % 2:
                    n = u // 2
                    if n % 2 == 0:
                        wait_slot(k, pe, n_gate + n // 2)
                    if n >= 4:
                        pe.wait_ge(s_sil, n - 3)
                    w = slot(k, n_gate + n // 2, 256)
                    for c in range(DC):
                        mm = nc.tensor.matmul(k.ps[:, 4 + n % 4, 0:T], w[:, c, (n % 2) * P:(n % 2 + 1) * P],
                                              k.h[:, c, :], start=(c == 0), stop=(c == DC - 1))
                    if n % 2:
                        mm.then_inc(k.ring_free[(n_gate + n // 2) % RING], 1)
                if b and h == 1:
                    if b == 1:
                        pe.wait_ge(s_cm, 2)
                    read(b - 1)
            read(NS - 1)
            pe.wait_ge(s_or, RH)
            for c in range(4):
                mm = nc.tensor.transpose(k.ps[:, 3, c * P:(c + 1) * P], orow[:, c * P:(c + 1) * P], k.ident)
            mm.then_inc(s_ot, 1)

        @block.scalar
        def _(act):
            for u, (b, h) in enumerate(units):
                act.wait_ge(s_bc, u + 1)
                for c in range(2):
                    if u >= 1:
                        act.wait_ge(s_new, 2 * (u - 1) + c + 1)
                    nc.scalar.activation(outer[:, c, :], k.ps[:, u % 2, :], ACT.Copy,
                                         scale=ks[:, 2 * h + c, b:b + 1]).then_inc(s_out, 1)
                if u % 4 == 3:
                    wait_used(k, act, n_gate + u // 4)
                    for n in (u // 2 - 1, u // 2):
                        nc.scalar.activation(gate[:, n], k.ps[:, 4 + n % 4, 0:T], ACT.Silu).then_inc(s_sil, 1)

        @block.vector
        def _(v):
            nc.vector.memset(qz, 0.0).then_inc(s_cm, 1)
            v.wait_ge(s_cm, 1)
            diagonal = qz.rearrange("p (c n) -> p c n", c=DC)[:, :, 0:NS * NS:NS + 1]
            nc.vector.tensor_copy(diagonal, qs).then_inc(s_cm, 1)
            for u, (b, h) in enumerate(units):
                v.wait_ge(s_ldb[u % 8], 16 * (u // 8 + 1))
                for c in range(2):
                    v.wait_ge(s_out, 2 * u + c + 1)
                    nc.vector.scalar_tensor_tensor(st[:, u % 8, c, :], st[:, u % 8, c, :], GAMMA[h], outer[:, c, :],
                                                   ALU.mult, ALU.add).then_inc(s_new, 1)
            v.wait_ge(s_new, 2 * len(units))
            k.dve.link(v, nc.vector.memset(orow, 0.0))
            v.wait_ge(s_q, NS)
            for h in range(RH):
                nc.vector.tensor_copy(orow[32 * h:32 * h + NS, :], k.ps[32 * h:32 * h + NS, 2, :]).then_inc(s_or, 1)
            v.wait_ge(s_ot, 1)
            for h in range(RH):
                nc.vector.tensor_copy(vo[:, 4 * h:4 * h + 4, TP:T],
                                      k.ps[:, 3, :].rearrange("p (c n) -> p c n", c=4)[:, :, 32 * h:32 * h + NS])

    project_heads(k, "ret", vo, 4, RH, k.ret_g, gate, True, n_out, 128, 0)


def project_heads(k, tag, o, per, heads, gain, gate, center, n_out, width, layer):
    nc = k.nc
    head_width = per * P
    kc = heads * per
    s_mu, s_cen, s_sq, s_ss, s_ms, s_rt, s_rs, s_sc, s_on, s_add = (k.sem(f"{tag}_norm_{n}") for n in (
        "sums", "centered", "squared", "square_sums", "meansq", "root", "reciprocal", "scaled", "gated",
        "residual_added"))
    s_half = k.sem(f"{tag}_first_half_projected")
    at_root = k.size - 2 * heads * T
    root = k.scratch[:, at_root:k.size].rearrange("p (b h t) -> p b h t", b=2, h=heads)
    squares = k.scratch[:, at_root - 2 * T:at_root].rearrange("p (b t) -> p b t", b=2)
    small = k.scratch[:, at_root - 2 * T - NS:at_root - 2 * T]
    rstd = k.rstd[:, 0:heads * T].rearrange("p (h t) -> p h t", h=heads)
    chunks = lambda h: range(per * h, per * h + per)
    outs, per_slot = D // P, width // P
    bank = lambda n: 4 + n if n < 4 else n - 4
    with nc.Block() as block:
        @block.sync
        def _(sp):
            load_until(k, sp, n_out + D // width + RING)

        @block.tensor
        def _(pe):
            def sums(h):
                if center and h < heads:
                    if h >= 2:
                        pe.wait_ge(s_cen, per * (h - 1))
                    for c in chunks(h):
                        mm = nc.tensor.matmul(k.ps[:, h % 2, 0:T], k.ones, o[:, c, :], start=(c == per * h),
                                              stop=(c == per * h + per - 1))
                    mm.then_inc(s_mu, 1)

            def product(n, c):
                w = slot(k, n_out + n // per_slot, width)
                m = n % per_slot
                mm = nc.tensor.matmul(k.ps[:, bank(n), 0:T], w[:, c, m * P:(m + 1) * P], o[:, c, :], start=(c == 0),
                                      stop=(c == kc - 1))
                if c == kc - 1 and m == per_slot - 1:
                    mm.then_inc(k.ring_free[(n_out + n // per_slot) % RING], 1)
                elif c == kc - 1:
                    mm.then_inc(s_half, 1)

            sums(0)
            sums(1)
            for h in range(heads):
                if h >= 2:
                    pe.wait_ge(s_ms, h - 1)
                for c in chunks(h):
                    pe.wait_ge(s_sq, c + 1)
                    nc.tensor.matmul(k.ps[:, 2 + h % 2, 0:T], k.ones, squares[:, c % 2], start=(c == per * h),
                                     stop=(c == per * h + per - 1)).then_inc(s_ss, 1)
                sums(h + 2)
            for n in range(0, 4, per_slot):
                wait_slot(k, pe, n_out + n // per_slot)
            for h in range(heads):
                pe.wait_ge(s_on, per * (h + 1))
                for n in range(4):
                    for c in chunks(h):
                        product(n, c)
            for n in range(4, outs):
                wait_slot(k, pe, n_out + n // per_slot)
                for c in range(kc):
                    product(n, c)

        @block.scalar
        def _(act):
            def square(h):
                for c in chunks(h):
                    if center:
                        act.wait_ge(s_cen, c + 1)
                    if c >= 2:
                        act.wait_ge(s_ss, c - 1)
                    nc.scalar.activation(squares[:, c % 2], o[:, c, :], ACT.Square).then_inc(s_sq, 1)

            square(0)
            for h in range(heads):
                if h + 1 < heads:
                    square(h + 1)
                act.wait_ge(s_ms, h + 1)
                nc.scalar.activation(root[:, 1, h, :], root[:, 0, h, :], ACT.Sqrt).then_inc(s_rt, 1)

        @block.vector
        def _(v):
            def subtract_mean(h):
                if center and h < heads:
                    v.wait_ge(s_mu, h + 1)
                    for c in chunks(h):
                        nc.vector.scalar_tensor_tensor(o[:, c, :], k.ps[:, h % 2, 0:T], -1.0 / head_width, o[:, c, :],
                                                       ALU.mult, ALU.add).then_inc(s_cen, 1)

            def mean_square(h):
                v.wait_ge(s_ss, per * (h + 1))
                nc.vector.tensor_scalar(root[:, 0, h, :], k.ps[:, 2 + h % 2, 0:T], 1.0 / head_width, EPS, ALU.mult,
                                        ALU.add).then_inc(s_ms, 1)

            subtract_mean(0)
            subtract_mean(1)
            mean_square(0)
            for h in range(heads):
                subtract_mean(h + 2)
                if h + 1 < heads:
                    mean_square(h + 1)
                v.wait_ge(s_rt, h + 1)
                nc.vector.reciprocal(rstd[:, h, :], root[:, 1, h, :]).then_inc(s_rs, 1)
                v.wait_ge(s_rs, h + 1)
                for c in chunks(h):
                    if center:
                        v.wait_ge(s_cen, c + 1)
                    nc.vector.scalar_tensor_tensor(o[:, c, :], o[:, c, :], gain[:, c:c + 1], rstd[:, h, :], ALU.mult,
                                                   ALU.mult).then_inc(s_sc, 1)
                for c in chunks(h):
                    v.wait_ge(s_sc, c + 1)
                    nc.vector.tensor_tensor(o[:, c, :], o[:, c, :], gate[:, c, :], ALU.mult).then_inc(s_on, 1)
            for n in range(outs):
                if n % per_slot == per_slot - 1:
                    wait_used(k, v, n_out + n // per_slot)
                else:
                    v.wait_ge(s_half, n // per_slot + 1)
                add_gated(k, v, n, k.ps[:, bank(n), :], k.mod[:, layer, 2], small).then_inc(s_add, 1)
                if n < outs - 1:
                    v.wait_ge(s_add, n + 1)



def gla(k):
    nc, inp, out = k.nc, k.inp, k.out
    sc = k.scratch
    at = [0]

    def area(cols):
        at[0] += cols
        assert at[0] <= k.size
        return sc[:, at[0] - cols:at[0]]

    q = area(GH * T).rearrange("p (c t) -> p c t", c=GH)
    kk = area(GH * T).rearrange("p (c t) -> p c t", c=GH)
    vo = area(8 * T).rearrange("p (c t) -> p c t", c=8)
    gate = sc[:, at[0]:at[0] + 8 * T].rearrange("p (c t) -> p c t", c=8)
    z = area(GH * T).rearrange("p (c t) -> p c t", c=GH)
    ez = area(GH * T).rearrange("p (c t) -> p c t", c=GH)
    az = area(GH * T).rearrange("p (c t) -> p c t", c=GH)
    alpha = area(GH * NS).rearrange("p (c t) -> p c t", c=GH)
    edge = area(GH * 2 * 3).rearrange("p (h j n) -> p h j n", h=GH, j=2)
    last_ = area(GH)
    qe, ke, kd = ([area(TP) for _ in range(2)] for _ in range(3))
    q0 = [area(P) for _ in range(2)]
    fac = [area(4 * TP).rearrange("p (b t) -> p b t", b=4) for _ in range(2)]
    knat = area(TP).rearrange("p (j n) -> p j n", j=2)
    vn = area(2 * GDV).rearrange("p (j n) -> p j n", j=2)
    att = area(TP).rearrange("p (j n) -> p j n", j=2)
    s1 = area(GDV)
    s2 = area(2 * GDV).rearrange("p (b n) -> p b n", b=2)
    vs = area(GH * GDV // 2).bitcast(BF16)
    v3 = ez.rearrange("p c t -> p (c t)")[:, 0:8 * COPIES].rearrange("p (c s) -> p c s", c=8)
    v_rest, v_mid = az.rearrange("p c t -> p (c t)")[:, 0:GDV], area(GDV // 2).bitcast(BF16)
    st = area(2 * GH * GDV).rearrange("p (b h n) -> p b h n", b=2, h=GH)
    outer = area(GH * GDV).rearrange("p (h n) -> p h n", h=GH)
    qz = area(GH * NS * NS)
    a1 = area(DC * RANK).rearrange("p (c r) -> p c r", c=DC)
    a2 = area(GH * GDK)[0:RANK, :]
    low = area(T)[0:RANK, :]
    n_in, n_out = k.stage["gla_in"], k.stage["gla_out"]

    s_w, s_low, s_lowc, s_z, s_zc, s_qk, s_abs, s_exp, s_ln, s_cum, s_edge = (k.sem(f"gla_{n}") for n in (
        "gate_weights", "low_rank", "low_rank_out", "logits", "logits_out", "copied", "absolute", "exp", "log",
        "cumulated", "edges"))
    def fetch(sp):
        sp.dma_start(a1, inp["gla_w_a1"][0].rearrange("(c p) r -> p c r", p=P)).then_inc(s_w, 16)
        sp.dma_start(a2, inp["gla_w_a2"][0]).then_inc(s_w, 16)

    norm(k, 1, 0, fetch)
    with nc.Block() as block:
        @block.sync
        def _(sp):
            load_until(k, sp, n_in + 8 + RING)

        @block.tensor
        def _(pe):
            pe.wait_ge(s_w, 32)
            for c in range(DC):
                mm = nc.tensor.matmul(k.ps[0:RANK, 4, 0:T], a1[:, c, :], k.h[:, c, :], start=(c == 0),
                                      stop=(c == DC - 1))
            mm.then_inc(s_low, 1)
            for t in range(8):
                wait_slot(k, pe, n_in + t)
                if t >= 2:
                    pe.wait_ge(s_qk, 2 * (t - 1))
                w = slot(k, n_in + t, 256)
                for m in range(2):
                    for c in range(DC):
                        mm = nc.tensor.matmul(k.ps[:, 2 * (t % 2) + m, 0:T], w[:, c, m * P:(m + 1) * P], k.h[:, c, :],
                                              start=(c == 0), stop=(c == DC - 1))
                mm.then_inc(k.ring_free[(n_in + t) % RING], 1)
                if t == 0:
                    pe.wait_ge(s_lowc, 1)
                    for h in range(GH):
                        if h >= 3:
                            pe.wait_ge(s_zc, h - 2)
                        nc.tensor.matmul(k.ps[:, 5 + h % 3, 0:T], a2[:, h * P:(h + 1) * P], low, start=True,
                                         stop=True).then_inc(s_z, 1)

        @block.scalar
        def _(act):
            act.wait_ge(s_low, 1)
            nc.scalar.copy(low, k.ps[0:RANK, 4, 0:T]).then_inc(s_lowc, 1)
            for h in range(GH):
                act.wait_ge(s_z, h + 1)
                nc.scalar.activation(z[:, h], k.ps[:, 5 + h % 3, 0:T], ACT.Identity,
                                     bias=k.b_a[:, h:h + 1]).then_inc(s_zc, 1)
            for t in range(8):
                wait_used(k, act, n_in + t)
                for m in range(2):
                    n = 2 * t + m
                    src = k.ps[:, 2 * (t % 2) + m, 0:T]
                    if t < 2:
                        ins = nc.scalar.activation(q[:, n], src, ACT.Copy, scale=GDK ** -0.5)
                    elif t < 4:
                        ins = nc.scalar.copy(kk[:, n - 4], src)
                    else:
                        ins = nc.scalar.copy(vo[:, n - 8], src)
                    ins.then_inc(s_qk, 1)
                if t == 1:
                    act.wait_ge(s_abs, 1)
                    flat = lambda a: a.rearrange("p c t -> p (c t)")
                    nc.scalar.activation(flat(ez), flat(az), ACT.Exp, scale=-1.0).then_inc(s_exp, 1)
                    act.wait_ge(s_exp, 1)
                    nc.scalar.activation(flat(az), flat(ez), ACT.Ln, bias=1.0).then_inc(s_ln, 1)
            act.wait_ge(s_cum, 1)
            nc.scalar.activation(alpha, z[:, :, TP:T], ACT.Exp, scale=1.0 / TAU)
            act.wait_ge(s_edge, 1)
            nc.scalar.activation(last_, edge[:, :, 1, 2], ACT.Exp)

        @block.vector
        def _(v):
            link = lambda ins: k.dve.link(v, ins)
            v.wait_ge(s_zc, GH)
            flat = lambda a: a.rearrange("p c t -> p (c t)")
            nc.vector.scalar_tensor_tensor(flat(az), flat(z), -1.0, flat(z), ALU.mult, ALU.max).then_inc(s_abs, 1)
            v.wait_ge(s_ln, 1)
            link(nc.vector.scalar_tensor_tensor(flat(ez), flat(z), 0.0, flat(az), ALU.min, ALU.subtract))
            for h in range(GH):
                for j in range(2):
                    nc.vector.tensor_tensor_scan(z[:, h, j * P:(j + 1) * P], k.ones, ez[:, h, j * P:(j + 1) * P], 0.0,
                                                 ALU.mult, ALU.add)
            nc.vector.tensor_copy(z[:, :, TP:T], ez[:, :, TP:T]).then_inc(s_cum, 1)
            v.wait_ge(s_cum, 1)
            zj = z[:, :, 0:TP].rearrange("p h (j t) -> p h j t", j=2)
            nc.vector.tensor_scalar(edge[:, :, :, 0], zj[:, :, :, P // 2 - 1], -1.0 / TAU, None, ALU.mult)
            nc.vector.tensor_scalar(edge[:, :, :, 1], zj[:, :, :, P // 2 - 1], 1.0 / TAU, None, ALU.mult)
            nc.vector.tensor_scalar(edge[:, :, :, 2], zj[:, :, :, P - 1], 1.0 / TAU, None, ALU.mult).then_inc(s_edge, 1)

    tv, s_f, s_e, s_kt, s_a, s_s1, s_o, s_s2 = (k.sem(f"gla_{n}") for n in (
        "tokens_first", "factors", "decayed", "keys_first", "scores", "state_mid", "heads", "state_last"))
    c_v, c_k, c_a, c_s1, c_o, c_s2 = (k.sem(f"gla_{n}") for n in (
        "values_out", "keys_out", "scores_out", "state_mid_out", "heads_out", "state_out"))
    s_v3 = k.sem("gla_sample_values_split")
    c_out = k.stored["gla_state_stored"]
    with nc.Block() as block:
        @block.tensor
        def _(pe):
            for h in range(GH):
                if h:
                    pe.wait_ge(c_v, h)
                for j in range(2):
                    for c in range(2):
                        nc.tensor.transpose(k.ps[:, 0, (2 * j + c) * P:(2 * j + c + 1) * P],
                                            vo[:, 2 * h + c, j * P:(j + 1) * P], k.ident)
                pe.wait_ge(s_v3, h + 1)
                for c in range(2):
                    mm = nc.tensor.transpose(k.ps[0:COPIES, 1, c * P:(c + 1) * P], v3[:, 2 * h + c, :], k.ident)
                mm.then_inc(tv, 1)
                pe.wait_ge(s_e, h + 1)
                if h:
                    pe.wait_ge(c_k, h)
                    pe.wait_ge(c_a, h)
                for j in range(2):
                    mm = nc.tensor.transpose(k.ps[:, 2, j * P:(j + 1) * P], kd[h % 2][:, j * P:(j + 1) * P], k.ident)
                mm.then_inc(s_kt, 1)
                for j in range(2):
                    mm = nc.tensor.matmul(k.ps[:, 3, j * P:(j + 1) * P], ke[h % 2][:, j * P:(j + 1) * P],
                                          qe[h % 2][:, j * P:(j + 1) * P], start=True, stop=True)
                mm.then_inc(s_a, 1)
                pe.wait_ge(c_v, h + 1)
                pe.wait_ge(c_k, h + 1)
                if h:
                    pe.wait_ge(c_s1, h)
                    pe.wait_ge(c_s2, h)
                nc.tensor.matmul(k.ps[:, 4, 0:GDV], knat[:, 0, :], vn[:, 0, :], start=True, stop=True).then_inc(s_s1, 1)
                nc.tensor.matmul(k.ps[:, 5, 0:GDV], knat[:, 1, :], vn[:, 1, :], start=True, stop=True).then_inc(s_s2, 1)
                pe.wait_ge(c_a, h + 1)
                pe.wait_ge(c_s1, h + 1)
                if h:
                    pe.wait_ge(c_o, h)
                for c in range(2):
                    o = k.ps[:, 6, c * TP:(c + 1) * TP]
                    nc.tensor.matmul(o[:, 0:P], vn[:, 0, c * P:(c + 1) * P], att[:, 0, :], start=True, stop=True)
                    nc.tensor.matmul(o[:, P:TP], vn[:, 1, c * P:(c + 1) * P], att[:, 1, :], start=True, stop=False)
                    mm = nc.tensor.matmul(o[:, P:TP], s1[:, c * P:(c + 1) * P], q0[h % 2], start=False, stop=True)
                mm.then_inc(s_o, 1)

        @block.scalar
        def _(act):
            def factors(h):
                f = fac[h % 2]
                if h >= 2:
                    act.wait_ge(s_e, h - 1)
                for j in range(2):
                    cols = slice(j * P, (j + 1) * P)
                    nc.scalar.activation(f[:, 0, cols], z[:, h, cols], ACT.Exp, scale=1.0 / TAU,
                                         bias=edge[:, h, j, 0:1])
                    nc.scalar.activation(f[:, 1, cols], z[:, h, cols], ACT.Exp, scale=-1.0 / TAU,
                                         bias=edge[:, h, j, 1:2])
                    nc.scalar.activation(f[:, 2, cols], z[:, h, cols], ACT.Exp, scale=-1.0 / TAU,
                                         bias=edge[:, h, j, 2:3])
                nc.scalar.activation(f[:, 3, 0:P], z[:, h, P:TP], ACT.Exp, scale=1.0 / TAU).then_inc(s_f, 1)

            factors(0)
            for h in range(GH):
                if h + 1 < GH:
                    factors(h + 1)
                act.wait_ge(tv, h + 1)
                if h:
                    act.wait_ge(s_o, h)
                nc.scalar.copy(vn.rearrange("p j n -> p (j n)"), k.ps[:, 0, :])
                nc.scalar.copy(vs[0:COPIES, h * GDV:(h + 1) * GDV], k.ps[0:COPIES, 1, 0:GDV]).then_inc(c_v, 1)
                act.wait_ge(s_o, h + 1)
                nc.scalar.copy(vo[:, 2 * h:2 * h + 2, 0:TP], k.ps[:, 6, :].rearrange("p (c t) -> p c t", c=2))\
                    .then_inc(c_o, 1)

        @block.vector
        def _(v):
            spread_samples(k, v, v3, vo[:, :, TP:T], 8).then_inc(s_v3, 1)

            def decay(h):
                b = h % 2
                v.wait_ge(s_f, h + 1)
                if h >= 2:
                    v.wait_ge(s_o, h - 1)
                nc.vector.tensor_tensor(qe[b], q[:, h, 0:TP], fac[b][:, 0], ALU.mult)
                nc.vector.tensor_tensor(ke[b], kk[:, h, 0:TP], fac[b][:, 1], ALU.mult)
                nc.vector.tensor_tensor(kd[b], kk[:, h, 0:TP], fac[b][:, 2], ALU.mult)
                nc.vector.tensor_tensor(q0[b], q[:, h, P:TP], fac[b][:, 3, 0:P], ALU.mult).then_inc(s_e, 1)

            decay(0)
            for h in range(GH):
                if h + 1 < GH:
                    decay(h + 1)
                v.wait_ge(s_kt, h + 1)
                nc.vector.tensor_copy(knat.rearrange("p j n -> p (j n)"), k.ps[:, 2, 0:TP]).then_inc(c_k, 1)
                v.wait_ge(s_a, h + 1)
                nc.vector.tensor_tensor(att, k.ps[:, 3, 0:TP].rearrange("p (j n) -> p j n", j=2),
                                        k.const("causal").unsqueeze(1).to_broadcast([P, 2, P]),
                                        ALU.mult).then_inc(c_a, 1)
                v.wait_ge(c_v, h + 1)
                split_rows(k, v, vs[:, h * GDV:(h + 1) * GDV], k.ps[:, 1, 0:GDV], v_rest, v_mid).then_inc(s_v3, 1)
                v.wait_ge(s_v3, h + 2)
                v.wait_ge(s_s1, h + 1)
                nc.vector.tensor_copy(s1, k.ps[:, 4, 0:GDV]).then_inc(c_s1, 1)
                v.wait_ge(c_s1, h + 1)
                v.wait_ge(s_s2, h + 1)
                if h >= 2:
                    v.wait_ge(c_out, 16 * (h - 1))
                nc.vector.scalar_tensor_tensor(s2[:, h % 2], s1, last_[:, h:h + 1], k.ps[:, 5, 0:GDV], ALU.mult,
                                               ALU.add).then_inc(c_s2, 1)

        @block.gpsimd
        def _(pool):
            for h in range(GH):
                pool.wait_ge(c_s2, h + 1)
                pool.dma_start(out["gla_prompt"][0, 0, h], s2[:, h % 2]).then_inc(c_out, 16)
                pool.wait_ge(c_out, 16 * (h + 1))

    s_bc, s_out, s_new, s_q, s_sil, s_cm, s_or, s_ot = (k.sem(f"gla_sample_{n}") for n in (
        "values_spread", "outer", "state_new", "read", "gate_silu", "compacted", "rows_out", "rows_transposed"))
    s_ldb = [k.sem(f"gla_sample_state_loaded{b}") for b in range(2)]
    s_stb = [k.stored[f"gla_sample_state_stored{b}"] for b in range(2)]
    n_gate = n_in + 8
    orow = k.rstd[:, 0:GDV]
    qz4 = qz.rearrange("p (h b s) -> p h b s", h=GH, b=NS)
    with nc.Block() as block:
        @block.sync
        def _(sp):
            for b in range(NS):
                if b >= 2:
                    sp.wait_ge(s_stb[b % 2], 16 * (b // 2))
                    sp.wait_ge(s_q, b - 1)
                sp.dma_start(st[:, b % 2], inp["state_gla"][0, b].rearrange("h p n -> p h n"))\
                    .then_inc(s_ldb[b % 2], 16)
                if b % 2 and b >= 3:
                    load_until(k, sp, n_gate + (b - 3) // 2 + RING)

        @block.gpsimd
        def _(pool):
            for b in range(NS):
                pool.wait_ge(s_new, GH * (b + 1))
                pool.dma_start(out["gla_sample"][0, b].rearrange("h p n -> p h n"), st[:, b % 2])\
                    .then_inc(s_stb[b % 2], 16)
            for b in range(2):
                pool.wait_ge(s_stb[b], 16 * NS // 2)

        @block.tensor
        def _(pe):
            for b in range(NS + 1):
                if b < NS:
                    for i in range(2):
                        if b >= 1:
                            pe.wait_ge(s_out, GH * (b - 1) + 2 * i + 2)
                        nc.tensor.matmul(k.ps[:, i, :], k.pick16[0:COPIES, b:b + 1].to_broadcast([COPIES, P]),
                                         vs[0:COPIES, i * 512:(i + 1) * 512], start=True, stop=True).then_inc(s_bc, 1)
                    if b % 2 == 0:
                        wait_slot(k, pe, n_gate + b // 2)
                    if b >= 4:
                        pe.wait_ge(s_sil, b - 3)
                    w = slot(k, n_gate + b // 2, 256)
                    for c in range(DC):
                        mm = nc.tensor.matmul(k.ps[:, 4 + b % 4, 0:T], w[:, c, (b % 2) * P:(b % 2 + 1) * P],
                                              k.h[:, c, :], start=(c == 0), stop=(c == DC - 1))
                    if b % 2:
                        mm.then_inc(k.ring_free[(n_gate + b // 2) % RING], 1)
                if b >= 1:
                    if b == 1:
                        pe.wait_ge(s_cm, 2)
                    pe.wait_ge(s_new, GH * b)
                    for h in range(GH):
                        mm = nc.tensor.matmul(k.ps[32 * h:32 * h + NS, 2, 0:GDV], qz4[:, h, b - 1, :],
                                              st[:, (b - 1) % 2, h, :], start=(b == 1), stop=(b == NS))
                    mm.then_inc(s_q, 1)
            pe.wait_ge(s_or, GH)
            for c in range(2):
                mm = nc.tensor.transpose(k.ps[:, 3, c * P:(c + 1) * P], orow[:, c * P:(c + 1) * P], k.ident)
            mm.then_inc(s_ot, 1)

        @block.scalar
        def _(act):
            for b in range(NS):
                for h in range(GH):
                    act.wait_ge(s_bc, 2 * b + h // 2 + 1)
                    if b:
                        act.wait_ge(s_new, GH * (b - 1) + h + 1)
                    nc.scalar.activation(outer[:, h, :], k.ps[:, h // 2, (h % 2) * GDV:(h % 2 + 1) * GDV], ACT.Copy,
                                         scale=kk[:, h, TP + b:TP + b + 1]).then_inc(s_out, 1)
                if b % 2:
                    wait_used(k, act, n_gate + b // 2)
                    for n in (b - 1, b):
                        nc.scalar.activation(gate[:, n], k.ps[:, 4 + n % 4, 0:T], ACT.Silu).then_inc(s_sil, 1)

        @block.vector
        def _(v):
            nc.vector.memset(qz, 0.0).then_inc(s_cm, 1)
            k.dve.link(v, nc.vector.memset(orow, 0.0))
            v.wait_ge(s_cm, 1)
            diagonal = qz.rearrange("p (h n) -> p h n", h=GH)[:, :, 0:NS * NS:NS + 1]
            nc.vector.tensor_copy(diagonal, q[:, :, TP:T]).then_inc(s_cm, 1)
            for b in range(NS):
                v.wait_ge(s_ldb[b % 2], 16 * (b // 2 + 1))
                for h in range(GH):
                    v.wait_ge(s_out, GH * b + h + 1)
                    nc.vector.scalar_tensor_tensor(st[:, b % 2, h, :], st[:, b % 2, h, :], alpha[:, h, b:b + 1],
                                                   outer[:, h, :], ALU.mult, ALU.add).then_inc(s_new, 1)
            v.wait_ge(s_q, NS)
            for h in range(GH):
                nc.vector.tensor_copy(orow[32 * h:32 * h + NS, :], k.ps[32 * h:32 * h + NS, 2, 0:GDV])\
                    .then_inc(s_or, 1)
            v.wait_ge(s_ot, 1)
            for h in range(GH):
                nc.vector.tensor_copy(vo[:, 2 * h:2 * h + 2, TP:T],
                                      k.ps[:, 3, 0:GDV].rearrange("p (c n) -> p c n", c=2)[:, :, 32 * h:32 * h + NS])

    project_heads(k, "gla", vo, 2, GH, k.gla_g, gate, False, n_out, 256, 1)



def final(k):
    nc, out = k.nc, k.out
    norm(k, DEPTH, 0)
    s_tr, s_cp, s_st = k.sem("y_token_major"), k.sem("y_copied"), k.sem("y_stored")
    y = k.scratch[:, 0:TT * D].rearrange("p (t d) -> p t d", t=TT)
    with nc.Block() as block:
        @block.tensor
        def _(pe):
            for t, (t0, n) in enumerate(TOKENS):
                for c in range(DC):
                    mm = nc.tensor.transpose(k.ps[0:n, 2 * t + c // 4, (c % 4) * P:(c % 4 + 1) * P],
                                             k.h[:, c, t0:t0 + n], k.ident)
                mm.then_inc(s_tr, 1)

        @block.vector
        def _(v):
            for t, (_, n) in enumerate(TOKENS):
                v.wait_ge(s_tr, t + 1)
                nc.vector.tensor_copy(y[0:n, t, :], k.ps[0:n, 2 * t:2 * t + 2, :].rearrange("p b d -> p (b d)"))\
                    .then_inc(s_cp, 1)

        @block.sync
        def _(sp):
            for t, (t0, n) in enumerate(TOKENS):
                sp.wait_ge(s_cp, t + 1)
                dst = out["y_prompt"][0, t0:t0 + n] if t < 2 else out["y_sample"].rearrange("b o d -> (b o) d")
                sp.dma_start(dst, y[0:n, t, :]).then_inc(s_st, 16)
            sp.wait_ge(s_st, 16 * TT)



def experts(k, layer):
    nc, inp = k.nc, k.inp
    sc = k.scratch
    at = [0]

    def area(cols):
        at[0] += cols
        assert at[0] <= k.size, at[0]
        return sc[:, at[0] - cols:at[0]]

    tag = f"moe{layer}"
    PAIRS = EPI // 2
    parts = area(TT * 3 * D // 2).bitcast(BF16).rearrange("p (t s d) -> p t s d", t=TT, s=3)
    xg = area(DC * EPI * CAP).rearrange("p (c n) -> p c n", c=DC)
    xg_pair = xg.rearrange("p c n -> p (c n)")[:, 0:DC * P].rearrange("p (c n) -> p c n", c=DC)
    hot = area(TT * EPI * CAP // 2).bitcast(BF16).rearrange("p (t e s) -> p t e s", t=TT, e=EPI)
    slot_token = area(PAIRS * T // 2).bitcast(BF16).rearrange("p (b t) -> p b t", b=PAIRS)
    sh_silu = sc[:, at[0]:at[0] + FC * T].rearrange("p (m t) -> p m t", m=FC)
    sh_hid = sc[:, at[0] + FC * T:at[0] + 2 * FC * T].rearrange("p (m t) -> p m t", m=FC)
    silu = area(PAIRS * DE).rearrange("p (b f) -> p b f", b=PAIRS)
    hid = area(PAIRS * DE).rearrange("p (b f) -> p b f", b=PAIRS)
    hid_t = area(PAIRS * DE).rearrange("p (b m s) -> p b m s", b=PAIRS, m=FC)
    row_area = area(PAIRS * 3 * D // 2)
    copies = row_area[:, 0:DC * COPIES].rearrange("p (c s) -> p c s", c=DC)
    row_parts = row_area.bitcast(BF16).rearrange("p (b s d) -> p b s d", b=PAIRS, s=3)
    rest = area(2 * 512).rearrange("p (b n) -> p b n", b=2)
    parts_c = parts.rearrange("p t s (q c) -> p t s q c", c=DC)
    acc = area(DC * T).rearrange("p (c t) -> p c t", c=DC)
    w_parts = area(TT * NE * 3 // 2).bitcast(BF16).rearrange("p (t e s) -> p t e s", t=TT, e=NE)
    w_now = area(TT * EPI * 3 // 2).bitcast(BF16).rearrange("p (t e s) -> p t e s", t=TT, e=EPI)
    w_sum = area(2 * TT * 3).rearrange("p (b t s) -> p b t s", b=2, t=TT)
    own = area(PAIRS * 6).rearrange("p (b n) -> p b n", b=PAIRS)
    slot_weight = area(PAIRS)
    wr = area(DC * NE).rearrange("p (c e) -> p c e", c=DC)
    bias = area(NE)

    def grid():
        return area(TT * NE).rearrange("p (t e) -> p t e", t=TT)

    at_grids = at[0]
    score, biased, left, chosen, weight, rank, key = (grid() for _ in range(7))
    picked, picked_key = (sc[:, a:a + 2 * TT * NE].rearrange("p (b t e) -> p b t e", b=2, t=TT)
                          for a in (at_grids, at_grids + 2 * TT * NE))
    w_rest, w_picked = grid(), rest.rearrange("p b n -> p (b n)")[:, 0:TT * NE * 3]
    w_picked = w_picked.rearrange("p (t e s) -> p t e s", t=TT, e=NE)
    best = area(TT * NG * 8).rearrange("p (t g n) -> p t g n", t=TT, g=NG)
    beats = area(TT * NG * NG).rearrange("p (t g n) -> p t g n", t=TT, g=NG)
    ties = w_rest.rearrange("p t (g n) -> p t g n", g=NG)
    gscore = area(TT * NG).rearrange("p (t g) -> p t g", t=TT)
    gmask = area(TT * NG).rearrange("p (t g) -> p t g", t=TT)
    top = area(TT * 8).rearrange("p (t n) -> p t n", t=TT)
    total = area(2 * TT)
    count, blocks, ends, shift = (area(NE) for _ in range(4))
    lookup = area(XB)
    extra = area(1 + XB).bitcast(I32)
    limits = area(4)
    low, high = limits[:, 0:2], limits[:, 2:4]
    found = area(2 * TT).rearrange("p (b t) -> p b t", b=2)
    compare = row_area[0:1, 0:XB * NE].rearrange("p (b e) -> p b e", b=XB)
    keep_small = area(DC * NS).rearrange("p (c s) -> p c s", c=DC)

    n_sh, n_moe = k.stage[f"shared{layer}"], k.stage[f"moe{layer}"]
    n_end = n_moe + ROUNDS * RING
    ident16 = k.ident16[:, :]
    ident, ones, before, iota = k.ident, k.ones, k.const("before"), k.const("iota")

    s_w, s_log, s_sc, s_rk, s_ch, s_nat, s_natc, s_hi = (k.sem(f"{tag}_{n}") for n in (
        "router_loaded", "logits", "scores", "ranks", "chosen", "token_major", "parts", "high_part"))
    s_shs, s_shh, s_shd, s_shx, s_fill = (k.sem(f"{tag}_{n}") for n in (
        "shared_silu", "shared_hidden", "shared_down", "shared_out", "scores_filled"))
    def fetch(sp):
        sp.dma_start(wr, inp["moe_w_router"][layer].rearrange("(c p) e -> p c e", p=P)).then_inc(s_w, 16)
        sp.dma_start(bias, inp["moe_router_bias"][layer:layer + 1, :].to_broadcast([P, NE])).then_inc(s_w, 16)

    norm(k, layer, 1, fetch)

    def tile(t):
        return (lambda c: k.h[:, c, t * P:(t + 1) * P]) if t < 2 else (lambda c: copies[:, c, :])

    ROWS = (P, P, COPIES)
    PRODUCTS = [(t, s) for t in range(2) for s in range(3)] + [(2, 0)]
    with nc.Block() as block:
        @block.sync
        def _(sp):
            load_until(k, sp, n_sh + 3 + RING)

        @block.tensor
        def _(pe):
            def token_major(t):
                if t:
                    pe.wait_ge(s_natc, t)
                for c in range(DC):
                    mm = nc.tensor.transpose(k.ps[0:ROWS[t], 6 + c // 4, (c % 4) * P:(c % 4 + 1) * P], tile(t)(c),
                                             ident)
                mm.then_inc(s_nat, 1)

            token_major(0)
            pe.wait_ge(s_w, 32)
            pe.wait_ge(s_fill, 2)
            for t in range(TT):
                for c in range(DC):
                    mm = nc.tensor.matmul(k.ps[0:ROWS[t], 0, t * NE:(t + 1) * NE], tile(t)(c), wr[:, c, :],
                                          start=(c == 0), stop=(c == DC - 1))
                mm.then_inc(s_log, 1)
            token_major(1)
            for j in range(2):
                wait_slot(k, pe, n_sh + j)
                w = slot(k, n_sh + j, DE)
                for m in range(FC):
                    for c in range(DC):
                        mm = nc.tensor.matmul(k.ps[:, 2 + 2 * j + m, 0:T], w[:, c, m * P:(m + 1) * P], k.h[:, c, :],
                                              start=(c == 0), stop=(c == DC - 1))
                mm.then_inc(k.ring_free[(n_sh + j) % RING], 1)
            pe.wait_ge(s_ch, 1)
            for u in range(TT + 1):
                for s in range(min(u + 1, TT)):
                    n = TOKENS[s][1]
                    w = ones if s != u else before if s < 2 else k.const("before_sample")
                    mm = nc.tensor.matmul(k.ps[:, 1, u * NE:(u + 1) * NE], w[0:n, :], chosen[0:n, s, :],
                                          start=(s == 0), stop=(s == min(u, TT - 1)))
            mm.then_inc(s_rk, 1)
            token_major(2)
            wait_slot(k, pe, n_sh + 2)
            pe.wait_ge(s_shh, FC)
            w = slot(k, n_sh + 2, D)
            for c in range(DC):
                if c >= 4:
                    pe.wait_ge(s_shx, c - 3)
                for m in range(FC):
                    mm = nc.tensor.matmul(k.ps[:, 2 + c % 4, 0:T], w[:, m, c * P:(c + 1) * P], sh_hid[:, m],
                                          start=(m == 0), stop=(m == FC - 1))
                mm.then_inc(s_shd if c < DC - 1 else k.ring_free[(n_sh + 2) % RING], 1)

        @block.scalar
        def _(act):
            def high_part(t):
                act.wait_ge(s_nat, t + 1)
                src = k.ps[0:ROWS[t], 6:8, :].rearrange("p b d -> p (b d)")
                nc.scalar.copy(parts[0:ROWS[t], t, 0, :], src).then_inc(s_hi, 1)

            high_part(0)
            act.wait_ge(s_fill, 2)
            act.wait_ge(s_log, 3)
            for t in range(TT):
                ins = nc.scalar.activation(score[0:ROWS[t], t, :], k.ps[0:ROWS[t], 0, t * NE:(t + 1) * NE], ACT.Sigmoid)
            ins.then_inc(s_sc, 1)
            high_part(1)
            for m in range(FC):
                wait_used(k, act, n_sh)
                nc.scalar.activation(sh_silu[:, m], k.ps[:, 2 + m, 0:T], ACT.Silu).then_inc(s_shs, 1)
            high_part(2)
            for c in range(DC):
                if c < DC - 1:
                    act.wait_ge(s_shd, c + 1)
                else:
                    wait_used(k, act, n_sh + 2)
                nc.scalar.copy(acc[:, c, :], k.ps[:, 2 + c % 4, 0:T]).then_inc(s_shx, 1)

        @block.vector
        def _(v):
            link = lambda ins: k.dve.link(v, ins)
            left_over = rest.rearrange("p b n -> p (b n)")

            def split_tokens(t):
                v.wait_ge(s_hi, t + 1)
                src = k.ps[0:ROWS[t], 6:8, :].rearrange("p b d -> p (b d)")
                link(nc.vector.tensor_tensor(left_over[0:ROWS[t]], src, parts[0:ROWS[t], t, 0, :], ALU.subtract))
                if t < 2:
                    link(nc.vector.tensor_copy(parts[:, t, 1, :], left_over))
                    ins = nc.vector.tensor_tensor(parts[:, t, 2, :], left_over, parts[:, t, 1, :], ALU.subtract)
                else:
                    mid, lo = slice(COPY, 2 * COPY), slice(2 * COPY, 3 * COPY)
                    nc.vector.tensor_copy(parts[mid, t, 0, :], left_over[mid])
                    link(nc.vector.tensor_copy(parts[lo, t, 1, :], left_over[lo]))
                    ins = nc.vector.tensor_tensor(parts[lo, t, 0, :], left_over[lo], parts[lo, t, 1, :], ALU.subtract)
                ins.then_inc(s_natc, 1)
                v.wait_ge(s_natc, t + 1)

            nc.vector.memset(score[:, TT - 1, :], 0.0).then_inc(s_fill, 1)
            link(nc.vector.memset(copies, 0.0))
            nc.vector.tensor_copy(copies.rearrange("p c (s n) -> p c s n", s=3)[:, :, :, 0:NS],
                                  k.h[:, :, TP:T].unsqueeze(2).to_broadcast([P, DC, 3, NS])).then_inc(s_fill, 1)
            split_tokens(0)
            v.wait_ge(s_sc, 1)
            v.wait_ge(s_w, 32)
            link(nc.vector.tensor_tensor(biased, score, bias.unsqueeze(1).to_broadcast([P, TT, NE]), ALU.add))
            for t in range(TT):
                for g in range(NG):
                    ins = nc.vector.max(out=best[:, t, g, :], in_=biased[:, t, g * 8:(g + 1) * 8])
            link(ins)
            link(nc.vector.tensor_tensor(gscore, best[:, :, :, 0], best[:, :, :, 1], ALU.add))
            mine = gscore.unsqueeze(3).to_broadcast([P, TT, NG, NG])
            other = gscore.unsqueeze(2).to_broadcast([P, TT, NG, NG])
            nc.vector.tensor_tensor(beats, other, mine, ALU.is_gt)
            link(nc.vector.tensor_tensor(ties, other, mine, ALU.is_equal))
            tri = k.const("gtri").rearrange("p (g n) -> p g n", g=NG).unsqueeze(1).to_broadcast([P, TT, NG, NG])
            link(nc.vector.tensor_tensor(ties, ties, tri, ALU.mult))
            link(nc.vector.tensor_tensor(beats, beats, ties, ALU.add))
            link(nc.vector.tensor_reduce(gmask, beats, AX.X, ALU.add))
            link(nc.vector.tensor_scalar(gmask, gmask, TOPG - 0.5, None, ALU.is_lt))
            open_ = gmask.unsqueeze(3).to_broadcast([P, TT, NG, 8])
            b4 = biased.rearrange("p t (g n) -> p t g n", g=NG)
            link(nc.vector.tensor_tensor(b4, b4, open_, ALU.mult))
            link(nc.vector.tensor_scalar(gmask, gmask, 1.0, 1.0e30, ALU.subtract, ALU.mult))
            link(nc.vector.tensor_tensor(b4, b4, open_, ALU.add))
            for t in range(TT):
                ins = nc.vector.max(out=top[:, t, :], in_=biased[:, t, :])
            link(ins)
            for t in range(TT):
                ins = nc.vector.match_replace(out=left[:, t, :], in_to_replace=top[:, t, :], in_values=biased[:, t, :],
                                              imm_value=-3.0e38)
            link(ins)
            link(nc.vector.tensor_tensor(chosen, left, biased, ALU.not_equal))
            valid = k.const("valid").unsqueeze(2).to_broadcast([P, TT, NE])
            nc.vector.tensor_tensor(chosen, chosen, valid, ALU.mult).then_inc(s_ch, 1)
            v.wait_ge(s_ch, 1)
            split_tokens(1)
            for m in range(FC):
                v.wait_ge(s_shs, m + 1)
                wait_used(k, v, n_sh + 1)
                nc.vector.tensor_tensor(sh_hid[:, m], sh_silu[:, m], k.ps[:, 4 + m, 0:T], ALU.mult).then_inc(s_shh, 1)
            v.wait_ge(s_rk, 1)
            ranks = k.ps[:, 1, 0:TT * NE].rearrange("p (t e) -> p t e", t=TT)
            link(nc.vector.tensor_copy(rank, ranks))
            link(nc.vector.tensor_copy(count, k.ps[:, 1, TT * NE:(TT + 1) * NE]))
            link(nc.vector.scalar_tensor_tensor(left, rank, 1.0, chosen, ALU.add, ALU.mult))
            link(nc.vector.tensor_scalar(left, left, -1.0, None, ALU.add))
            link(nc.vector.tensor_tensor(weight, score, chosen, ALU.mult))
            link(nc.vector.tensor_reduce(total[:, 0:TT], weight, AX.X, ALU.add))
            nv = total[:, TT:2 * TT]
            link(nc.vector.tensor_scalar(nv, k.const("valid"), -1.0, 1.0, ALU.mult, ALU.add))
            link(nc.vector.tensor_tensor(total[:, 0:TT], total[:, 0:TT], nv, ALU.add))
            link(nc.vector.reciprocal(total[:, 0:TT], total[:, 0:TT]))
            link(nc.vector.tensor_tensor(weight, weight, total[:, 0:TT].unsqueeze(2).to_broadcast([P, TT, NE]),
                                         ALU.mult))
            link(nc.vector.tensor_scalar(weight, weight, SCALE, None, ALU.mult))
            link(nc.vector.tensor_copy(w_parts[:, :, :, 0], weight))
            link(nc.vector.tensor_tensor(w_rest, weight, w_parts[:, :, :, 0], ALU.subtract))
            link(nc.vector.tensor_copy(w_parts[:, :, :, 1], w_rest))
            link(nc.vector.tensor_tensor(w_parts[:, :, :, 2], w_rest, w_parts[:, :, :, 1], ALU.subtract))
            split_tokens(2)

    (s_hot, s_gat, g_even, g_odd, s_ht, s_htc, s_own, s_sil, s_hid, s_hidt, s_hidtc, s_dn, s_rhi, s_rest, s_mid,
     s_part, s_scat, s_add, s_count) = (k.sem(f"{tag}_{n}") for n in (
         "one_hot", "gathered", "gathered_out_even", "gathered_out_odd", "slots_first", "slots_first_out",
         "slot_weight", "silu", "hidden", "hidden_transposed", "hidden_transposed_out", "down", "row_high",
         "row_rest", "row_middle", "row_parts", "spread", "added", "extra_counted"))
    x_gu_load, x_dn_load = k.sem(f"{tag}_extra_gate_up_loaded"), k.sem(f"{tag}_extra_down_loaded")
    X_LOADS = [(0, 0), (1, 0), (0, 1), (1, 1), (2, 0), (2, 1)]
    x_slots = {load: (n_end + i) % RING for i, load in enumerate(X_LOADS)}
    number = extra[0:1, 0:1]

    def place(kind, e):
        return n_moe + PLACE[(kind, e)]

    (x_hot, x_gat, x_ht, x_got, x_tok, x_gu, x_sil, x_hid, x_hidt, x_hidtc, x_dn, x_hi, x_rest, x_part, x_scat,
     x_add, x_step, x_own) = (k.sem(f"{tag}_extra_{n}") for n in (
         "one_hot", "gathered", "slots_first", "gathered_out", "slots_first_out", "gate_up", "silu", "hidden",
         "hidden_transposed", "hidden_transposed_out", "down", "row_high", "row_rest", "row_parts", "spread",
         "added", "vector_step", "slot_weight"))
    XSTEPS = 12

    def place_tokens(v, i):
        steps = [0]

        def link(ins):
            steps[0] += 1
            ins.then_inc(x_step, 1)
            v.wait_ge(x_step, XSTEPS * i + steps[0])

        keys = key.unsqueeze(1).to_broadcast([P, 2, TT, NE])
        bound = lambda a: a.unsqueeze(2).unsqueeze(3).to_broadcast([P, 2, TT, NE])
        nc.vector.tensor_tensor(picked, keys, bound(low), ALU.is_ge)
        link(nc.vector.tensor_tensor(picked_key, keys, bound(high), ALU.is_lt))
        link(nc.vector.tensor_tensor(picked, picked, picked_key, ALU.mult))
        link(nc.vector.tensor_tensor(picked_key, picked, keys, ALU.mult))
        link(nc.vector.tensor_reduce(found, picked_key, AX.X, ALU.add))
        link(nc.vector.tensor_tensor(found, found, low.unsqueeze(2).to_broadcast([P, 2, TT]), ALU.subtract))
        link(nc.vector.tensor_tensor(hot[:, :, 0:2, :].rearrange("p t b s -> p b t s"),
                                     found.unsqueeze(3).to_broadcast([P, 2, TT, CAP]),
                                     iota[:, 0:CAP].unsqueeze(1).unsqueeze(1).to_broadcast([P, 2, TT, CAP]),
                                     ALU.is_equal))
        for j in range(2):
            link(nc.vector.tensor_tensor(w_picked, w_parts,
                                         picked[:, j].unsqueeze(3).to_broadcast([P, TT, NE, 3]), ALU.mult))
            link(nc.vector.tensor_reduce(w_sum[:, j], w_picked.rearrange("p t e s -> p t s e"), AX.X, ALU.add))
        link(nc.vector.tensor_scalar(limits, limits, 2.0 * CAP, None, ALU.add))
        link(nc.vector.tensor_copy(w_now[:, :, 0:2, :].rearrange("p t b s -> p b t s"), w_sum))
        assert steps[0] == XSTEPS
        v.sem_inc(x_hot, 1)

    def expert_weight(name, e):
        w = inp[name][layer].rearrange("e " + rows_of(name).format("e p"), p=P)
        return w[bass.ds(e, 1)].rearrange("o p k n -> (o p) k n")

    def load_extra(sp, loads, experts_):
        for kind, j in loads:
            src = expert_weight(("moe_w_gate", "moe_w_up", "moe_w_down")[kind], experts_[j])
            sp.dma_start(slot(k, x_slots[kind, j], src.shape[2]), src)\
                .then_inc(x_dn_load if kind == 2 else x_gu_load, 16)

    def pair_experts(sp, i):
        return [sp.value_load(extra[0:1, bass.ds(2 * i + 1 + j, 1)], min_val=0, max_val=NE - 1) for j in range(2)]

    with nc.Block() as block:
        @block.sync
        def _(sp):
            with sp.Fori(1, ROUNDS) as r:
                for name, e in ROUND:
                    n = place(name, e)
                    src = expert_weight(name, r * EPI + e)
                    sp.wait_ge(k.ring_free[n % RING], r + n // RING)
                    sp.dma_start(slot(k, n, src.shape[2]), src).then_inc(k.ring_full[n % RING], 16)
            for i in range(len(X_LOADS)):
                sp.wait_ge(k.ring_free[(n_end + i) % RING], (n_end + i) // RING)
            sp.wait_ge(s_count, 1)
            with sp.If(sp.value_load(number, min_val=0, max_val=XPAIRS) > 0):
                load_extra(sp, X_LOADS, pair_experts(sp, 0))
            k.issued = n_end + len(X_LOADS)
            load_until(k, sp, n_end + RING)

        def gather(pe, r):
            pe.wait_ge(s_hot, r + 1)
            for c in range(DC):
                b = (c // 2) % 2
                if c % 2 == 0 and c >= 4:
                    pe.wait_ge(g_odd if b else g_even, 2 * r + 1)
                for t, s in PRODUCTS:
                    mm = nc.tensor.matmul(k.ps[:, b, (c % 2) * 256:(c % 2 + 1) * 256],
                                          parts_c[0:ROWS[t], t, s, :, c],
                                          hot[0:ROWS[t], t].rearrange("p e s -> p (e s)"),
                                          start=((t, s) == PRODUCTS[0]), stop=((t, s) == PRODUCTS[-1]))
                if c % 2:
                    mm.then_inc(s_gat, 1)

        def slots_first(pe):
            for p in range(PAIRS):
                for t, (t0, n) in enumerate(TOKENS):
                    pair = hot[0:n, t, 2 * p:2 * p + 2, :].rearrange("p e s -> p (e s)")
                    nc.tensor.matmul(k.ps[:, 4 + p, t0:t0 + n], pair, ident16[0:n, 0:n], start=True, stop=True)
                for t, (_, n) in enumerate(TOKENS):
                    pair = hot[0:n, t, 2 * p:2 * p + 2, :].rearrange("p e s -> p (e s)")
                    mm = nc.tensor.matmul(k.ps[:, 4 + p, T:T + 6], pair,
                                          w_now[0:n, t, 2 * p:2 * p + 2, :].rearrange("p e s -> p (e s)"),
                                          start=(t == 0), stop=(t == TT - 1))
            mm.then_inc(s_ht, 1)

        def spread(pe, r):
            pe.wait_ge(s_htc, r + 1)
            pe.wait_ge(s_part, 4 * r + 4)
            for c in range(DC):
                pe.wait_ge(s_add, DC * (r + 1) + c - 1)
                for p in range(PAIRS):
                    for s in range(3):
                        mm = nc.tensor.matmul(k.ps[:, c % 2, 0:T], row_parts[:, p, s, c * P:(c + 1) * P],
                                              slot_token[:, p, :], start=(p == 0 and s == 0),
                                              stop=(p == PAIRS - 1 and s == 2))
                mm.then_inc(s_scat, 1)

        def pe_round(pe, r, first, last):
            pe.wait_ge(g_even, 2 * r + 2)
            pe.wait_ge(g_odd, 2 * r + 2)
            for p in range(PAIRS):
                for e in (2 * p, 2 * p + 1):
                    for name in ("moe_w_gate", "moe_w_up"):
                        n = place(name, e)
                        pe.wait_ge(k.ring_full[n % RING], 16 * (r + n // RING + 1))
                for j, name in enumerate(("moe_w_gate", "moe_w_up")):
                    for c in range(DC):
                        for e in (2 * p, 2 * p + 1):
                            n, lo = place(name, e), CAP * (e % 2)
                            mm = nc.tensor.matmul(k.ps[lo:lo + CAP, 2 + p, j * DE:(j + 1) * DE],
                                                  xg[:, c, e * CAP:(e + 1) * CAP], slot(k, n, DE)[:, c, :],
                                                  start=(c == 0), stop=(c == DC - 1))
                            if c == DC - 1:
                                mm.then_inc(k.ring_free[n % RING], 1)
            if not first:
                spread(pe, r - 1)
                pe.wait_ge(s_part, 4 * r)
            for p in range(PAIRS):
                pe.wait_ge(s_hid, PAIRS * r + p + 1)
                for m in range(FC):
                    mm = nc.tensor.transpose(k.ps[:, 6 + p, m * P:(m + 1) * P],
                                             hid[:, p, m * P:(m + 1) * P], ident)
                mm.then_inc(s_hidt, 1)
            if not last:
                if not first:
                    pe.wait_ge(s_add, DC * r + DC)
                gather(pe, r + 1)
            for p in range(PAIRS):
                pe.wait_ge(s_hidtc, PAIRS * r + 2)
                for e in (2 * p, 2 * p + 1):
                    n = place("moe_w_down", e)
                    pe.wait_ge(k.ring_full[n % RING], 16 * (r + n // RING + 1))
                for half in range(2):
                    if p:
                        pe.wait_ge(s_rest, 4 * r + 2 * (p - 1) + half + 1)
                    for m in range(FC):
                        for e in (2 * p, 2 * p + 1):
                            n, lo = place("moe_w_down", e), CAP * (e % 2)
                            mm = nc.tensor.matmul(k.ps[lo:lo + CAP, 6 + half, :], hid_t[:, p, m, lo:lo + CAP],
                                                  slot(k, n, D)[:, m, half * 512:(half + 1) * 512],
                                                  start=(m == 0), stop=(m == FC - 1))
                            if half == 1 and m == FC - 1:
                                mm.then_inc(k.ring_free[n % RING], 1)
                            elif half == 0 and m == FC - 1 and e % 2:
                                mm.then_inc(s_dn, 1)
            if not last:
                pe.wait_ge(s_htc, r + 1)
                slots_first(pe)

        @block.tensor
        def _(pe):
            gather(pe, 0)
            slots_first(pe)
            pe_round(pe, 0, True, False)
            with pe.Fori(1, ROUNDS - 1) as r:
                pe_round(pe, r, False, False)
            pe_round(pe, ROUNDS - 1, False, True)
            spread(pe, ROUNDS - 1)

        def one_hot(v, r):
            nc.vector.tensor_copy(w_now, w_parts[:, :, bass.ds(r * EPI, EPI), :])
            nc.vector.tensor_tensor(hot, left[:, :, bass.ds(r * EPI, EPI)].unsqueeze(3).to_broadcast([P, TT, EPI, CAP]),
                                    iota[:, 0:CAP].unsqueeze(1).unsqueeze(1).to_broadcast([P, TT, EPI, CAP]),
                                    ALU.is_equal).then_inc(s_hot, 1)

        def take(eng, r, b, copy, sem):
            for q in range(2):
                eng.wait_ge(s_gat, DC // 2 * r + 2 * q + b + 1)
                c = 4 * q + 2 * b
                copy(xg[:, c:c + 2, :], k.ps[:, b, :].rearrange("p (c n) -> p c n", c=2)).then_inc(sem, 1)

        def rows_done(eng, r, p, half):
            if half == 0:
                eng.wait_ge(s_dn, PAIRS * r + p + 1)
            else:
                n = place("moe_w_down", 2 * p + 1)
                eng.wait_ge(k.ring_free[n % RING], r + n // RING + 1)

        def count_extra(v):
            link = lambda ins: k.dve.link(v, ins)
            link(nc.vector.tensor_scalar(blocks, count, CAP + 0.5, None, ALU.is_gt))
            for j in range(2, (T - 1) // CAP + 1):
                link(nc.vector.scalar_tensor_tensor(blocks, count, CAP * j + 0.5, blocks, ALU.is_gt, ALU.add))
            link(nc.vector.tensor_tensor_scan(ends, ones[:, 0:NE], blocks, 0.0, ALU.mult, ALU.add))
            link(nc.vector.tensor_tensor(shift, ends, blocks, ALU.subtract))
            link(nc.vector.tensor_scalar(shift, shift, float(CAP), 1.0 - CAP, ALU.mult, ALU.add))
            link(nc.vector.tensor_tensor(key, rank, shift.unsqueeze(1).to_broadcast([P, TT, NE]), ALU.add))
            link(nc.vector.scalar_tensor_tensor(key, left, CAP - 0.5, key, ALU.is_gt, ALU.mult))
            link(nc.vector.tensor_scalar(lookup[0:1, 0:XPAIRS], iota[0:1, 0:XPAIRS], 2.0, ends[0:1, NE - 1:NE],
                                         ALU.mult, ALU.is_lt))
            link(nc.vector.tensor_reduce(found[0:1, 0, 0:1], lookup[0:1, 0:XPAIRS], AX.X, ALU.add))
            link(nc.vector.tensor_copy(extra[0:1, 0:1], found[0:1, 0, 0:1]))
            link(nc.vector.tensor_tensor(compare, ends[0:1, :].unsqueeze(1).to_broadcast([1, XB, NE]),
                                         iota[0:1, 0:XB].unsqueeze(2).to_broadcast([1, XB, NE]), ALU.is_le))
            link(nc.vector.tensor_reduce(lookup[0:1, 0:XB], compare, AX.X, ALU.add))
            link(nc.vector.tensor_scalar(lookup[0:1, 0:XB], lookup[0:1, 0:XB], NE - 1.0, None, ALU.min))
            link(nc.vector.tensor_copy(extra[0:1, 1:1 + XB], lookup[0:1, 0:XB]))
            nc.vector.memset(limits[:, 0:1], 1.0)
            nc.vector.memset(limits[:, 1:3], 1.0 + CAP)
            nc.vector.memset(limits[:, 3:4], 1.0 + 2 * CAP).then_inc(s_count, 1)

        @block.vector
        def _(v):
            def add_spread(r):
                v.wait_ge(s_add, DC * (r + 1))
                for c in range(DC):
                    v.wait_ge(s_scat, DC * r + c + 1)
                    nc.vector.tensor_tensor(acc[:, c, :], acc[:, c, :], k.ps[:, c % 2, 0:T], ALU.add).then_inc(s_add, 1)

            def round_(r, first, last):
                v.wait_ge(s_ht, r + 1)
                for p in range(PAIRS):
                    nc.vector.scalar_tensor_tensor(own[:, p, :], k.ps[:, 4 + p, T:T + 6], 1.0, k.const("own"), ALU.mult,
                                                   ALU.mult, accum_out=slot_weight[:, p:p + 1]).then_inc(s_own, 1)
                v.wait_ge(s_own, PAIRS * r + PAIRS)
                for p in range(PAIRS):
                    v.wait_ge(s_sil, PAIRS * r + p + 1)
                    nc.vector.scalar_tensor_tensor(hid[:, p, :], silu[:, p, :], slot_weight[:, p:p + 1],
                                                   k.ps[:, 2 + p, DE:2 * DE], ALU.mult, ALU.mult).then_inc(s_hid, 1)
                if not first:
                    add_spread(r - 1)
                if not last:
                    take(v, r + 1, 0, nc.vector.tensor_copy, g_even)
                for q in range(2 * PAIRS):
                    p, half = divmod(q, 2)
                    cols = slice(half * 512, (half + 1) * 512)
                    v.wait_ge(s_rhi, 4 * r + q + 1)
                    if not first or q >= 2:
                        v.wait_ge(s_part, 4 * r + q - 1)
                    nc.vector.tensor_tensor(rest[:, half], k.ps[:, 6 + half, :], row_parts[:, p, 0, cols],
                                            ALU.subtract).then_inc(s_rest, 1)
                    v.wait_ge(s_rest, 4 * r + q + 1)
                    nc.vector.tensor_copy(row_parts[:, p, 1, cols], rest[:, half]).then_inc(s_mid, 1)
                    v.wait_ge(s_mid, 4 * r + q + 1)
                    nc.vector.tensor_tensor(row_parts[:, p, 2, cols], rest[:, half], row_parts[:, p, 1, cols],
                                            ALU.subtract).then_inc(s_part, 1)

            v.sem_inc(s_add, DC)
            one_hot(v, 0)
            take(v, 0, 0, nc.vector.tensor_copy, g_even)
            v.wait_ge(s_ht, 1)
            one_hot(v, 1)
            count_extra(v)
            round_(0, True, False)
            v.wait_ge(s_ht, 2)
            one_hot(v, 2)
            with v.Fori(1, ROUNDS - 2) as r:
                round_(r, False, False)
                v.wait_ge(s_ht, r + 2)
                one_hot(v, r + 2)
            round_(ROUNDS - 2, False, False)
            v.wait_ge(s_ht, ROUNDS)
            v.wait_ge(s_part, 4 * ROUNDS - 4)
            place_tokens(v, 0)
            round_(ROUNDS - 1, False, True)
            add_spread(ROUNDS - 1)

        @block.scalar
        def _(act):
            def slots_out(r):
                act.wait_ge(s_own, PAIRS * r + PAIRS)
                for p in range(PAIRS):
                    ins = nc.scalar.copy(slot_token[:, p, :], k.ps[:, 4 + p, 0:T])
                ins.then_inc(s_htc, 1)

            def round_(r, first, last):
                for p in range(PAIRS):
                    n = place("moe_w_up", 2 * p + 1)
                    act.wait_ge(k.ring_free[n % RING], r + n // RING + 1)
                    nc.scalar.activation(silu[:, p, :], k.ps[:, 2 + p, 0:DE], ACT.Silu).then_inc(s_sil, 1)
                if first:
                    act.wait_ge(s_ht, 1)
                else:
                    act.wait_ge(s_scat, DC * r)
                slots_out(r)
                for p in range(PAIRS):
                    act.wait_ge(s_hidt, PAIRS * r + p + 1)
                    nc.scalar.copy(hid_t[:, p].rearrange("p m s -> p (m s)"), k.ps[:, 6 + p, 0:DE])\
                        .then_inc(s_hidtc, 1)
                if not last:
                    take(act, r + 1, 1, nc.scalar.copy, g_odd)
                for q in range(2 * PAIRS):
                    p, half = divmod(q, 2)
                    rows_done(act, r, p, half)
                    nc.scalar.copy(row_parts[:, p, 0, half * 512:(half + 1) * 512], k.ps[:, 6 + half, :])\
                        .then_inc(s_rhi, 1)

            take(act, 0, 1, nc.scalar.copy, g_odd)
            round_(0, True, False)
            with act.Fori(1, ROUNDS - 1) as r:
                round_(r, False, False)
            round_(ROUNDS - 1, False, True)

    with nc.Block() as block:
        @block.sync
        def _(sp):
            pairs = sp.value_load(number, min_val=0, max_val=XPAIRS)
            with sp.If(pairs > 1):
                with sp.Fori(1, pairs) as i:
                    which_ = pair_experts(sp, i)
                    sp.wait_ge(x_gu, i)
                    load_extra(sp, X_LOADS[0:4], which_)
                    sp.wait_ge(x_dn, 2 * i)
                    load_extra(sp, X_LOADS[4:6], which_)

        @block.tensor
        def _(pe):
            def gather_pair(i):
                pe.wait_ge(x_hot, i + 1)
                for c in range(DC):
                    for t, s in PRODUCTS:
                        mm = nc.tensor.matmul(k.ps[:, c // 4, (c % 4) * P:(c % 4 + 1) * P],
                                              parts_c[0:ROWS[t], t, s, :, c],
                                              hot[0:ROWS[t], t, 0:2, :].rearrange("p e s -> p (e s)"),
                                              start=((t, s) == PRODUCTS[0]), stop=((t, s) == PRODUCTS[-1]))
                    if c % 4 == 3:
                        mm.then_inc(x_gat, 1)
                for t, (t0, n) in enumerate(TOKENS):
                    pair = hot[0:n, t, 0:2, :].rearrange("p e s -> p (e s)")
                    nc.tensor.matmul(k.ps[:, 4, t0:t0 + n], pair, ident16[0:n, 0:n], start=True, stop=True)
                for t, (_, n) in enumerate(TOKENS):
                    pair = hot[0:n, t, 0:2, :].rearrange("p e s -> p (e s)")
                    mm = nc.tensor.matmul(k.ps[:, 4, T:T + 6], pair,
                                          w_now[0:n, t, 0:2, :].rearrange("p e s -> p (e s)"),
                                          start=(t == 0), stop=(t == TT - 1))
                mm.then_inc(x_ht, 1)

            pe.sem_inc(x_scat, DC)
            pairs = pe.value_load(number, min_val=0, max_val=XPAIRS)
            with pe.If(pairs > 0):
                gather_pair(0)
                with pe.Fori(0, pairs) as i:
                    pe.wait_ge(x_got, 2 * i + 2)
                    pe.wait_ge(x_gu_load, 64 * i + 64)
                    pe.wait_ge(x_add, DC * i + DC)
                    for kind in range(2):
                        for c in range(DC):
                            for j in range(2):
                                lo = CAP * j
                                mm = nc.tensor.matmul(k.ps[lo:lo + CAP, 2, kind * DE:(kind + 1) * DE],
                                                      xg_pair[:, c, lo:lo + CAP],
                                                      slot(k, x_slots[kind, j], DE)[:, c, :],
                                                      start=(c == 0), stop=(c == DC - 1))
                    mm.then_inc(x_gu, 1)
                    pe.wait_ge(x_hid, i + 1)
                    for m in range(FC):
                        mm = nc.tensor.transpose(k.ps[:, 3, m * P:(m + 1) * P], hid[:, 0, m * P:(m + 1) * P], ident)
                    mm.then_inc(x_hidt, 1)
                    pe.wait_ge(x_hidtc, i + 1)
                    pe.wait_ge(x_dn_load, 32 * i + 32)
                    for half in range(2):
                        for m in range(FC):
                            for j in range(2):
                                lo = CAP * j
                                mm = nc.tensor.matmul(k.ps[lo:lo + CAP, 6 + half, :], hid_t[:, 0, m, lo:lo + CAP],
                                                      slot(k, x_slots[2, j], D)[:, m, half * 512:(half + 1) * 512],
                                                      start=(m == 0), stop=(m == FC - 1))
                        mm.then_inc(x_dn, 1)
                    pe.wait_ge(x_tok, i + 1)
                    gather_pair(i + 1)
                    pe.wait_ge(x_part, 2 * i + 2)
                    for c in range(DC):
                        if c >= 2:
                            pe.wait_ge(x_add, DC * i + DC + c - 1)
                        for s in range(3):
                            mm = nc.tensor.matmul(k.ps[:, 2 + c % 2, 0:T], row_parts[:, 0, s, c * P:(c + 1) * P],
                                                  slot_token[:, 0, :], start=(s == 0), stop=(s == 2))
                        mm.then_inc(x_scat, 1)

        @block.vector
        def _(v):
            v.sem_inc(x_add, DC)
            pairs = v.value_load(number, min_val=0, max_val=XPAIRS)
            with v.If(pairs > 0):
                with v.Fori(0, pairs) as i:
                    v.wait_ge(x_ht, i + 1)
                    nc.vector.scalar_tensor_tensor(own[:, 0, :], k.ps[:, 4, T:T + 6], 1.0, k.const("own"), ALU.mult,
                                                   ALU.mult, accum_out=slot_weight[:, 0:1]).then_inc(x_own, 1)
                    v.wait_ge(x_own, i + 1)
                    place_tokens(v, i + 1)
                    v.wait_ge(x_sil, i + 1)
                    nc.vector.scalar_tensor_tensor(hid[:, 0, :], silu[:, 0, :], slot_weight[:, 0:1],
                                                   k.ps[:, 2, DE:2 * DE], ALU.mult, ALU.mult).then_inc(x_hid, 1)
                    for half in range(2):
                        cols = slice(half * 512, (half + 1) * 512)
                        v.wait_ge(x_hi, 2 * i + half + 1)
                        nc.vector.tensor_tensor(rest[:, half], k.ps[:, 6 + half, :], row_parts[:, 0, 0, cols],
                                                ALU.subtract).then_inc(x_rest, 1)
                        v.wait_ge(x_rest, 4 * i + 2 * half + 1)
                        nc.vector.tensor_copy(row_parts[:, 0, 1, cols], rest[:, half]).then_inc(x_rest, 1)
                        v.wait_ge(x_rest, 4 * i + 2 * half + 2)
                        nc.vector.tensor_tensor(row_parts[:, 0, 2, cols], rest[:, half], row_parts[:, 0, 1, cols],
                                                ALU.subtract).then_inc(x_part, 1)
                    v.wait_ge(x_part, 2 * i + 2)
                    v.wait_ge(x_add, DC * i + DC)
                    for c in range(DC):
                        v.wait_ge(x_scat, DC * (i + 1) + c + 1)
                        nc.vector.tensor_tensor(acc[:, c, :], acc[:, c, :], k.ps[:, 2 + c % 2, 0:T],
                                                ALU.add).then_inc(x_add, 1)

        @block.scalar
        def _(act):
            pairs = act.value_load(number, min_val=0, max_val=XPAIRS)
            with act.If(pairs > 0):
                with act.Fori(0, pairs) as i:
                    for b in range(2):
                        act.wait_ge(x_gat, 2 * i + b + 1)
                        nc.scalar.copy(xg_pair[:, 4 * b:4 * b + 4, :],
                                       k.ps[:, b, :].rearrange("p (c n) -> p c n", c=4)).then_inc(x_got, 1)
                    act.wait_ge(x_own, i + 1)
                    act.wait_ge(x_scat, DC * i + DC)
                    nc.scalar.copy(slot_token[:, 0, :], k.ps[:, 4, 0:T]).then_inc(x_tok, 1)
                    act.wait_ge(x_gu, i + 1)
                    nc.scalar.activation(silu[:, 0, :], k.ps[:, 2, 0:DE], ACT.Silu).then_inc(x_sil, 1)
                    act.wait_ge(x_hidt, i + 1)
                    nc.scalar.copy(hid_t[:, 0].rearrange("p m s -> p (m s)"), k.ps[:, 3, 0:DE]).then_inc(x_hidtc, 1)
                    for half in range(2):
                        act.wait_ge(x_dn, 2 * i + half + 1)
                        nc.scalar.copy(row_parts[:, 0, 0, half * 512:(half + 1) * 512], k.ps[:, 6 + half, :])\
                            .then_inc(x_hi, 1)

    k.pending = (acc, k.mod[:, layer, 5], keep_small)
    k.skipped = (n_end, n_end + len(X_LOADS))



_INS = ["x_prompt", "x_sample", "state_ret", "state_gla", "c_prompt", "c_sample", "ret_w_in", "ret_norm_g",
        "ret_w_out", "gla_w_in", "gla_w_a1", "gla_w_a2", "gla_b_a", "gla_norm_g", "gla_w_out", "ada_w", "ada_b",
        "norm_mix_g", "norm_ffn_g", "moe_w_router", "moe_router_bias", "moe_w_gate", "moe_w_up", "moe_w_down",
        "sh_w_gate", "sh_w_up", "sh_w_down", "final_norm_g"]
_OUTS = [("y_prompt", (1, TP, D)), ("y_sample", (NS, 1, D)), ("ret_prompt", (1, 1, RH, RDK, RDV)),
         ("gla_prompt", (1, 1, GH, GDK, GDV)), ("ret_sample", (1, NS, RH, RDK, RDV)),
         ("gla_sample", (1, NS, GH, GDK, GDV))]


def kernel(**inputs):
    import concourse.bacc as bacc
    from concourse.bass_utils import run_bass_kernel_spmd

    nc = bacc.Bacc("TRN2", target_bir_lowering=False, num_devices=1)
    arrays, inp, out = {}, {}, {}
    for name in _INS + ["tables"]:
        a = np.ascontiguousarray(tables() if name == "tables" else inputs[name])
        arrays[f"in_{name}"] = a
        inp[name] = nc.dram_tensor(f"in_{name}", a.shape, mybir.dt.from_np(a.dtype), kind="ExternalInput").ap()
    for name, shape in _OUTS:
        out[name] = nc.dram_tensor(f"out_{name}", shape, F32, kind="ExternalOutput").ap()
    build(nc, inp, out)
    r = run_bass_kernel_spmd(nc, [arrays], core_ids=[0])
    return tuple(r.results[0][f"out_{name}"] for name, _ in _OUTS)
```
